# Optimizing a Trainium2 kernel written in Bass

```python
import functools
import jax
import jax.numpy as jnp
from jax import lax
import numpy as np

D_MODEL = 1024
BATCH = 1
SEQ = 128
DEPTH = 2
DEC_BATCH = 1
DEC_SEQ = 256
PAST_LEN = 128

GRID_W = 64
C_CONV = 256
CONV_W = 31
C_FNO = 256
FNO_GROUPS = 4
FNO_GW = C_FNO // FNO_GROUPS
N_HEADS = 8
HEAD_DIM = 64
C_RWKV = N_HEADS * HEAD_DIM
G_RANK = 128
W_RANK = 64
A_RANK = 64
N_DIR = 2
N_BRANCH = 3
D_FF = 2816
N_EXPERTS = 8
TOP_K = 2
D_FF_E = 1408
N_DENSE = (DEPTH + 1) // 2
N_MOE = DEPTH // 2
RMS_EPS = 1e-6
LN_EPS = 1e-5
GN_EPS = 64e-5

OFF_CONV = 0
OFF_FNO = OFF_CONV + 2 * C_CONV
OFF_RWKV = OFF_FNO + C_FNO
N_SHIFT = 3 * C_RWKV + G_RANK + N_DIR * (W_RANK + A_RANK)
OFF_GATE = OFF_RWKV + N_SHIFT
D_IN = OFF_GATE + N_BRANCH * D_MODEL

kernel_name = "hybrid_conv_fnet_rwkv7_diffusion_step"

def rmsnorm(x, g):
    xf = x.astype(jnp.float32)
    y = xf * lax.rsqrt(jnp.mean(xf * xf, axis=-1, keepdims=True) + RMS_EPS)
    return (y * g.astype(jnp.float32)).astype(x.dtype)

def layernorm(x, g, b, eps):
    xf = x.astype(jnp.float32)
    mu = jnp.mean(xf, axis=-1, keepdims=True)
    var = jnp.mean(jnp.square(xf - mu), axis=-1, keepdims=True)
    y = (xf - mu) * lax.rsqrt(var + eps) * g.astype(jnp.float32) + b.astype(jnp.float32)
    return y.astype(x.dtype)

def conv_branch(u, n_rows, dw_w, dw_b, ln_g, ln_b, w_out):
    bsz, t_len, _ = u.shape
    h = u[..., :C_CONV] * jax.nn.sigmoid(u[..., C_CONV:])
    if n_rows is not None:
        h = h.reshape(bsz * n_rows, GRID_W, C_CONV)
    h = lax.conv_general_dilated(
        h, dw_w[:, None, :].astype(h.dtype), window_strides=(1,),
        padding=[(CONV_W // 2, CONV_W // 2)],
        dimension_numbers=("NWC", "WIO", "NWC"), feature_group_count=C_CONV)
    h = h.reshape(bsz, t_len, C_CONV) + dw_b
    h = jax.nn.silu(layernorm(h, ln_g, ln_b, LN_EPS))
    return h @ w_out

def fourier_branch(u, w_out):
    bsz, t_len, _ = u.shape
    h = u.astype(jnp.float32).reshape(bsz, t_len, FNO_GROUPS, FNO_GW)
    h = jnp.fft.fft2(h, axes=(1, 3), norm="ortho").real
    return h.reshape(bsz, t_len, C_FNO).astype(u.dtype) @ w_out

def wkv_scan(r, w, k, v, a_, b_, s0, reverse):
    def step(s, inp):
        r_t, w_t, k_t, v_t, a_t, b_t = inp
        sa = jnp.einsum("bhvk,bhk->bhv", s, a_t)
        s = (s * w_t[:, :, None, :] + sa[..., None] * b_t[:, :, None, :]
             + v_t[..., None] * k_t[:, :, None, :])
        return s, jnp.einsum("bhvk,bhk->bhv", s, r_t)
    xs = tuple(jnp.moveaxis(t, 1, 0) for t in (r, w, k, v, a_, b_))
    s_fin, ys = lax.scan(step, s0, xs, reverse=reverse)
    return jnp.moveaxis(ys, 0, 1), s_fin

def rwkv_branch(z, s0, mu, g_up, dec_w0, dec_up, iclr_a0, iclr_up, k_k, k_a, r_k,
                gn_g, gn_b, w_out):
    f32 = jnp.float32
    bsz, t_len, _ = z.shape
    zp = jnp.pad(z, ((0, 0), (1, 1), (0, 0)))
    z = z + mu * (0.5 * (zp[:, :-2] + zp[:, 2:]) - z)
    zf = z.astype(f32)
    heads = lambda t: t.reshape(t.shape[:-1] + (N_HEADS, HEAD_DIM))
    r = zf[..., 0:C_RWKV]
    k = zf[..., C_RWKV:2 * C_RWKV]
    v = zf[..., 2 * C_RWKV:3 * C_RWKV]
    o = 3 * C_RWKV
    g = jax.nn.sigmoid(zf[..., o:o + G_RANK]) @ g_up.astype(f32)
    o += G_RANK
    wd = zf[..., o:o + N_DIR * W_RANK].reshape(bsz, t_len, N_DIR, W_RANK)
    o += N_DIR * W_RANK
    ad = zf[..., o:o + N_DIR * A_RANK].reshape(bsz, t_len, N_DIR, A_RANK)
    w_log = -jax.nn.softplus(-(dec_w0 + jnp.einsum("btdr,drc->btdc", jnp.tanh(wd), dec_up))) - 0.5
    decay = jnp.exp(-jnp.exp(w_log))
    a = jax.nn.sigmoid(iclr_a0 + jnp.einsum("btdr,drc->btdc", ad, iclr_up))
    kk = heads(k * k_k)
    kk = kk / jnp.maximum(jnp.linalg.norm(kk, axis=-1, keepdims=True), 1e-12)
    rh, vh = heads(r), heads(v)
    ys, finals = [], []
    for d in range(N_DIR):
        a_d = a[:, :, d]
        k_d = heads(k * (1 + (a_d - 1) * k_a))
        y_d, s_d = wkv_scan(rh, heads(decay[:, :, d]), k_d, vh, -kk, kk * heads(a_d),
                            s0[:, d].astype(f32), reverse=(d == 1))
        ys.append(y_d)
        finals.append(s_d)
    y = layernorm(ys[0] + ys[1], gn_g.reshape(N_HEADS, HEAD_DIM),
                  gn_b.reshape(N_HEADS, HEAD_DIM), GN_EPS)
    y = y + jnp.sum(rh * heads(k) * r_k, axis=-1, keepdims=True) * vh
    y = y.reshape(bsz, t_len, C_RWKV) * g
    return y.astype(z.dtype) @ w_out, jnp.stack(finals, axis=1)

def swiglu(h, w_gate, w_up, w_down):
    return (jax.nn.silu(h @ w_gate) * (h @ w_up)) @ w_down

def moe_swiglu(h, w_router, b_router, w_gate, w_up, w_down):
    bsz, t_len, dm = h.shape
    t = h.reshape(bsz * t_len, dm)
    logits = (t @ w_router).astype(jnp.float32) + b_router.astype(jnp.float32)
    top_v, top_i = lax.top_k(logits, TOP_K)
    top_p = jax.nn.softmax(top_v, axis=-1)
    comb = jnp.sum(jax.nn.one_hot(top_i, N_EXPERTS, dtype=jnp.float32) * top_p[..., None], axis=1)
    y = jnp.zeros_like(t)
    for e in range(N_EXPERTS):
        y = y + comb[:, e:e + 1].astype(t.dtype) * swiglu(t, w_gate[e], w_up[e], w_down[e])
    return y.reshape(bsz, t_len, dm)

def trunk_layer(x, mod, s0, n_rows, lp, ffn):
    bsz, t_len, _ = x.shape
    sh1, sc1, g1, sh2, sc2, g2 = jnp.split(mod, 6, axis=-1)
    h = rmsnorm(x, lp["norm1"]) * (1 + sc1) + sh1
    u = h @ lp["w_in"]
    y_conv = conv_branch(u[..., OFF_CONV:OFF_FNO], n_rows, lp["dw_w"], lp["dw_b"],
                         lp["conv_ln_g"], lp["conv_ln_b"], lp["w_conv_out"])
    y_fno = fourier_branch(u[..., OFF_FNO:OFF_RWKV], lp["w_fno_out"])
    y_rwkv, s_fin = rwkv_branch(u[..., OFF_RWKV:OFF_GATE], s0, lp["shift_mu"], lp["g_up"],
                                lp["dec_w0"], lp["dec_up"], lp["iclr_a0"], lp["iclr_up"],
                                lp["k_k"], lp["k_a"], lp["r_k"], lp["gn_g"], lp["gn_b"],
                                lp["w_rwkv_out"])
    gates = jax.nn.sigmoid(u[..., OFF_GATE:].reshape(bsz, t_len, N_BRANCH, D_MODEL))
    merged = gates[:, :, 0] * y_conv + gates[:, :, 1] * y_fno + gates[:, :, 2] * y_rwkv
    x = x + g1 * (merged @ lp["w_o"])
    h = rmsnorm(x, lp["norm2"]) * (1 + sc2) + sh2
    x = x + g2 * ffn(h)
    return x, s_fin

def setup_inputs(seed: int = 0) -> dict:
    key = jax.random.key(seed)
    ks = jax.random.split(key, 40)
    L = DEPTH
    nrm = lambda i, shape, s: jax.random.normal(ks[i], shape, jnp.float32) * s
    gain = lambda i, shape: 1.0 + nrm(i, shape, 0.05)
    return {
        "x_prompt": nrm(0, (BATCH, SEQ, D_MODEL), 1.0),
        "x_sample": nrm(1, (DEC_BATCH, DEC_SEQ, D_MODEL), 1.0),
        "state_rwkv": nrm(2, (DEC_BATCH, L, N_DIR, N_HEADS, HEAD_DIM, HEAD_DIM), 0.5),
        "c": nrm(3, (DEC_BATCH, D_MODEL), 1.0),
        "c_ctx": nrm(4, (D_MODEL,), 1.0),
        "norm1": gain(5, (L, D_MODEL)),
        "norm2": gain(6, (L, D_MODEL)),
        "w_ada": nrm(7, (L, D_MODEL, 6 * D_MODEL), 0.5 * D_MODEL ** -0.5),
        "b_ada": nrm(8, (L, 6 * D_MODEL), 0.02),
        "w_in": nrm(9, (L, D_MODEL, D_IN), D_MODEL ** -0.5),
        "dw_w": nrm(10, (L, CONV_W, C_CONV), CONV_W ** -0.5),
        "dw_b": nrm(11, (L, C_CONV), 0.02),
        "conv_ln_g": gain(12, (L, C_CONV)),
        "conv_ln_b": nrm(13, (L, C_CONV), 0.02),
        "w_conv_out": nrm(14, (L, C_CONV, D_MODEL), C_CONV ** -0.5),
        "w_fno_out": nrm(15, (L, C_FNO, D_MODEL), C_FNO ** -0.5),
        "shift_mu": jax.random.uniform(ks[16], (L, N_SHIFT), jnp.float32),
        "g_up": nrm(17, (L, G_RANK, C_RWKV), G_RANK ** -0.5),
        "dec_w0": jax.random.uniform(ks[18], (L, N_DIR, C_RWKV), jnp.float32, -1.5, 1.5),
        "dec_up": nrm(19, (L, N_DIR, W_RANK, C_RWKV), 0.1),
        "iclr_a0": nrm(20, (L, N_DIR, C_RWKV), 0.5),
        "iclr_up": nrm(21, (L, N_DIR, A_RANK, C_RWKV), A_RANK ** -0.5),
        "k_k": 1.0 + nrm(22, (L, C_RWKV), 0.1),
        "k_a": 1.0 + nrm(23, (L, C_RWKV), 0.1),
        "r_k": nrm(24, (L, N_HEADS, HEAD_DIM), 0.1),
        "gn_g": gain(25, (L, C_RWKV)),
        "gn_b": nrm(26, (L, C_RWKV), 0.02),
        "w_rwkv_out": nrm(27, (L, C_RWKV, D_MODEL), C_RWKV ** -0.5),
        "w_o": nrm(28, (L, D_MODEL, D_MODEL), D_MODEL ** -0.5),
        "ffn_w_gate": nrm(29, (N_DENSE, D_MODEL, D_FF), D_MODEL ** -0.5),
        "ffn_w_up": nrm(30, (N_DENSE, D_MODEL, D_FF), D_MODEL ** -0.5),
        "ffn_w_down": nrm(31, (N_DENSE, D_FF, D_MODEL), D_FF ** -0.5),
        "w_router": nrm(32, (N_MOE, D_MODEL, N_EXPERTS), D_MODEL ** -0.5),
        "b_router": nrm(33, (N_MOE, N_EXPERTS), 0.01),
        "moe_w_gate": nrm(34, (N_MOE, N_EXPERTS, D_MODEL, D_FF_E), D_MODEL ** -0.5),
        "moe_w_up": nrm(35, (N_MOE, N_EXPERTS, D_MODEL, D_FF_E), D_MODEL ** -0.5),
        "moe_w_down": nrm(36, (N_MOE, N_EXPERTS, D_FF_E, D_MODEL), D_FF_E ** -0.5),
        "final_norm": gain(37, (D_MODEL,)),
    }

def reference(x_prompt, x_sample, state_rwkv, c, c_ctx, norm1, norm2, w_ada, b_ada, w_in,
              dw_w, dw_b, conv_ln_g, conv_ln_b, w_conv_out, w_fno_out, shift_mu, g_up,
              dec_w0, dec_up, iclr_a0, iclr_up, k_k, k_a, r_k, gn_g, gn_b, w_rwkv_out, w_o,
              ffn_w_gate, ffn_w_up, ffn_w_down, w_router, b_router,
              moe_w_gate, moe_w_up, moe_w_down, final_norm):
    n_rows = x_sample.shape[1] // GRID_W
    s_zero = jnp.zeros((x_prompt.shape[0], N_DIR, N_HEADS, HEAD_DIM, HEAD_DIM), jnp.float32)
    xp, xs = x_prompt, x_sample
    ctx_states = []
    for l in range(DEPTH):
        lp = {
            "norm1": norm1[l], "norm2": norm2[l], "w_in": w_in[l],
            "dw_w": dw_w[l], "dw_b": dw_b[l], "conv_ln_g": conv_ln_g[l],
            "conv_ln_b": conv_ln_b[l], "w_conv_out": w_conv_out[l], "w_fno_out": w_fno_out[l],
            "shift_mu": shift_mu[l], "g_up": g_up[l], "dec_w0": dec_w0[l], "dec_up": dec_up[l],
            "iclr_a0": iclr_a0[l], "iclr_up": iclr_up[l], "k_k": k_k[l], "k_a": k_a[l],
            "r_k": r_k[l], "gn_g": gn_g[l], "gn_b": gn_b[l], "w_rwkv_out": w_rwkv_out[l],
            "w_o": w_o[l],
        }
        i = l // 2
        if l % 2 == 0:
            ffn = functools.partial(swiglu, w_gate=ffn_w_gate[i], w_up=ffn_w_up[i],
                                    w_down=ffn_w_down[i])
        else:
            ffn = functools.partial(moe_swiglu, w_router=w_router[i], b_router=b_router[i],
                                    w_gate=moe_w_gate[i], w_up=moe_w_up[i],
                                    w_down=moe_w_down[i])
        mod_p = (jax.nn.silu(c_ctx) @ w_ada[l] + b_ada[l])[None, None, :]
        mod_s = (jax.nn.silu(c) @ w_ada[l] + b_ada[l])[:, None, :]
        xp, s_ctx = trunk_layer(xp, mod_p, s_zero, None, lp, ffn)
        xs, _ = trunk_layer(xs, mod_s, state_rwkv[:, l], n_rows, lp, ffn)
        ctx_states.append(s_ctx)
    y_prompt = rmsnorm(xp, final_norm)
    y_sample = rmsnorm(xs, final_norm)
    new_state_rwkv = jnp.stack(ctx_states, axis=1).astype(x_prompt.dtype)
    return (y_prompt, y_sample, new_state_rwkv)


_drawn_inputs = setup_inputs


def setup_inputs(seed=0):
    import zlib

    import numpy as np

    out = dict(_drawn_inputs(seed))
    spreads = {}
    factors = {'state_rwkv': 5.007,
     'dw_b': 7.039,
     'conv_ln_g': 4.739,
     'conv_ln_b': 8.0,
     'gn_g': 5.832,
     'gn_b': 24.887,
     'b_router': 17.399,
     'norm2': 2.916}
    for name, (base, spread) in spreads.items():
        noise = np.random.default_rng([zlib.crc32(name.encode()), seed]).standard_normal(out[name].shape)
        drawn = base * np.exp(spread * noise) if base else spread * noise
        out[name] = jnp.asarray(drawn.astype(out[name].dtype))
    for name, factor in factors.items():
        out[name] = (out[name] * factor).astype(out[name].dtype)
    return out
```

```python
from contextlib import ExitStack

import numpy as np
import concourse.bass as bass
from concourse import mybir

P = 128
DM, DEPTH = 1024, 2
TP, TS = 128, 256
T = TP + TS
SEG = ((0, TP), (TP, T))
KD = DM // P
GRID, CONV_W = 64, 31
CC, CF, CR = 256, 256, 512
HD, NH = 64, 8
NM = CR // P
C = 64
NC_ = T // C
NCP = T // P
LEVELS = 6
NZ = 15
OFF_Z, OFF_G = 768, 2688
DFF, KF = 2816, 22
NE, DE, KE = 8, 1408, 11
CHUNKS = ((0, 512), (512, 512), (1024, 384))
DOWN = ((0, 4), (4, 4), (8, 3))
NCODE = 3 * NE
NJOB = 16
DECAY = float(np.exp(-0.5))

F32 = mybir.dt.float32
I32 = mybir.dt.int32
U32 = mybir.dt.uint32
ALU = mybir.AluOpType
ACT = mybir.ActivationFunctionType
AX = mybir.AxisListType


def tables():
    i = np.arange(P)
    out = {}
    out["ident"] = np.eye(P)
    out["ones"] = np.ones((P, P))
    out["before"] = (i[:, None] < i[None, :]) * 1.0
    out["iota"] = np.tile(np.arange(P), (P, 1))
    out["code"] = np.tile(np.arange(24), (P, 1))
    out["eps"] = np.tile(np.array([1e-6, 1e-5, 64e-5, 0.0]), (P, 1))
    out["heads"] = (i[:, None] // HD == i[None, :] // HD) * 1.0
    c = np.arange(HD)
    ang = 2 * np.pi * (np.outer(c, c) % HD) / HD
    for name, m in (("dft_c", np.cos(ang)), ("dft_s", np.sin(ang))):
        out[name] = np.kron(np.eye(2), m)
    for name, n in (("p", TP), ("s", TS)):
        t = np.arange(n)
        ang = 2 * np.pi * (np.outer(t, t) % n) / n
        scale = 1.0 / np.sqrt(n * HD)
        both = np.stack([np.cos(ang), -np.sin(ang)]) * scale
        out["time_" + name] = both.reshape(2, n // P, P, n).transpose(2, 1, 0, 3).reshape(P, -1)
    s, t = np.arange(C)[:, None], np.arange(C)[None, :]
    both = []
    for strict in (s < t, s > t):
        incl = strict | (s == t)
        both.append(np.concatenate([strict, incl, strict, incl], 1))
    out["pair_mask"] = np.tile(np.concatenate(both, 1), (2, 1))
    lev = []
    for m in range(LEVELS):
        b = 1 << m
        low = (s // (2 * b) == t // (2 * b)) & (s // b > t // b)
        lev += [low, low.T, low]
    out["level_mask"] = np.tile(np.concatenate(lev, 1), (2, 1))
    out["eye2"] = np.tile(np.eye(C), (2, 2))
    out["reset"] = np.tile(np.arange(T) % C != 0, (P, 1))
    return {k: np.asarray(v, np.float32) for k, v in out.items()}


FIRST = ("ident", "ones", "before", "iota", "code", "eps")


def table_columns():
    at, n = {}, 0
    for k, v in tables().items():
        at[k] = (n, v.shape[1])
        n += v.shape[1]
    return at, n


VEC = {
    "A": (("dw_w", 62), ("dw_b", 2), ("conv_ln_g", 2), ("conv_ln_b", 2), ("norm1", 8), ("norm2", 8)),
    "B": (("b_ada", 48), ("shift_mu", 15), ("dec_w0", 8), ("iclr_a0", 8), ("k_k", 4), ("k_a", 4),
          ("r_k", 4), ("gn_g", 4), ("gn_b", 4)),
}
SHARED = (("final_norm", 8), ("c", 8), ("c_ctx", 8))


R_LG, R_MX, R_IX, R_IF, R_D, R_P, R_OH = 24, 48, 72, 96, 120, 124, 132
R_CW, R_RK, R_CNT, R_SL, R_FL, R_PS, R_JL, R_TM = 180, 252, 276, 284, 356, 372, 388, 408


def order(d):
    return (0, 2, 1, 3, 4, 5) if d == 0 else (1, 5, 0, 4, 3, 2)


def starts(d):
    return (0, 2) if d == 0 else (1, 5)


def nxt(d, c):
    n = c + 1 if d == 0 else c - 1
    if d == 0:
        return "end" if c == 1 else None if c == 5 else n
    return "end" if c == 0 else None if c == 2 else n


def L3(d):
    return 2 if d == 0 else 3


def other(d):
    return 5 - L3(d)


def flat(ap):
    return ap if len(ap.shape) == 1 else ap.rearrange("a b -> (a b)")


def e_transposes(pe, s, transpose, psum, eprod, i, c):
    pe.wait_ge(s("e_prod"), i * 3 + 3 + c + 1)
    if c == 2:
        pe.wait_ge(s("e_pT"), i * 3 + 1)
    k0, kn = DOWN[c]
    for k in range(kn):
        last = transpose(psum[6 + c % 2][:, k * P:(k + 1) * P], eprod[:, (k0 + k) * P:(k0 + k + 1) * P])
    last.then_inc(s("e_pT_full"), 1)


def e_copy(act, a, s, psum, eprodT, i, c):
    act.wait_ge(s("e_pT_full"), i * 3 + c + 1)
    k0, kn = DOWN[c]
    a(eprodT[:, k0:k0 + kn, :], psum[6 + c % 2][:, 0:kn * P].rearrange("p (k s) -> p k s", k=kn), ACT.Copy)\
        .then_inc(s("e_pT"), 1)


def build(nc, dram, outs, marks):
    yp, ys, new_state = outs
    tcol, ncols = table_columns()

    with ExitStack() as ctx:
        TOTAL = 52992 - 80
        mem = ctx.enter_context(nc.sbuf_tensor("mem", [P, TOTAL], F32))
        psum = [ctx.enter_context(nc.psum_tensor(f"bank{i}", [P, 512], F32)) for i in range(8)]
        used = {}

        def cut(name, start, n):
            used[name] = (start, start + n)
            assert start + n <= TOTAL, (name, start + n)
            return mem[:, start:start + n]

        n_first = sum(tcol[k][1] for k in FIRST)
        o = 0
        xT = cut("xT", o, KD * T).rearrange("p (k t) -> p k t", k=KD); o += KD * T
        first = cut("first", o, n_first); o += n_first
        vec = cut("vec", o, 4 * P).rearrange("p (g c) -> p g c", g=4); o += 4 * P
        mod = cut("mod", o, 96).rearrange("p (m s) -> p m s", s=2); o += 96
        modA = cut("modA", o, 32).rearrange("p (w k s) -> p w k s", w=2, s=2); o += 32
        cond = cut("cond", o, 16).rearrange("p (k s) -> p k s", s=2); o += 16
        condx = cut("condx", o, 16).rearrange("p (k s) -> p k s", s=2); o += 16
        mix = cut("mix", o, 32).rearrange("p (w z) -> p w z", w=2); o += 32
        oneka = cut("oneka", o, 4); o += 4
        pc = cut("pc", o, 24).rearrange("p (m c) -> p m c", m=NM); o += 24
        stat = cut("stat", o, 96); o += 96
        hT = cut("hT", o, KD * T).rearrange("p (k t) -> p k t", k=KD); o += KD * T
        low_end = o
        second = cut("second", o, ncols - n_first); o += ncols - n_first
        RING, SLOT = 4, 8 * 256
        ring = [cut(f"ring{i}", o + i * SLOT, SLOT) for i in range(RING)]; o += RING * SLOT
        arena = o
        z = cut("z", o, NZ * T).rearrange("p (m t) -> p m t", m=NZ)
        merged = cut("merged", o, KD * T).rearrange("p (k t) -> p k t", k=KD)
        rows = cut("rows", o, 4 * P).rearrange("p (g c) -> p g c", g=4)
        o += NZ * T
        cvT = cut("cvT", o, 2 * T).rearrange("p (m t) -> p m t", m=2); o += 2 * T
        fnT = cut("fnT", o, 2 * T).rearrange("p (m t) -> p m t", m=2); o += 2 * T
        kk = cut("kk", o, NM * T).rearrange("p (m t) -> p m t", m=NM); o += NM * T
        ffn_at = o
        AR = cut("AR", o, 2 * NM * T).rearrange("p (m c k t) -> p m c k t", m=NM, c=NC_, k=2)
        ksq = cut("ksq", o, NM * T).rearrange("p (m t) -> p m t", m=NM)
        o += 2 * NM * T
        BK = cut("BK", o, 2 * NM * T).rearrange("p (k m t) -> p k m t", k=2, m=NM)
        TQ = cut("TQ", o, 24 * P).rearrange("p (c h w) -> p c h w", c=NCP, h=NH)
        U = TQ[:, :, :, 0:C]
        yT = cut("yT", o, NM * T).rearrange("p (m t) -> p m t", m=NM)
        o += 2 * NM * T
        S1 = cut("S1", o, 24 * 256).rearrange("p (c h w) -> p c h w", c=NCP, h=NH)
        tmp4 = [cut(f"tmp{i}", o + i * NM * T, NM * T) for i in range(4)]
        shifted = cut("shifted", o, NZ * T).rearrange("p (m t) -> p m t", m=NZ)
        o += 24 * 256
        tok = cut("tok", o, 2 * NCP * CR).rearrange("p (k c w) -> p k c w", k=2, c=NCP)
        fno_u = cut("fno_u", o, 2 * T).rearrange("p (m t) -> p m t", m=2)
        fno_z = cut("fno_z", o + 2 * T, NCP * 512).rearrange("p (j m w) -> p j m w", j=NCP, m=2)
        sq = cut("sq", o, KD * T).rearrange("p (k t) -> p k t", k=KD)
        xin = cut("xin", o, 3 * DM).rearrange("p (j d) -> p j d", j=3)
        o += 2 * NCP * CR
        PADC = TP + 30 + 4 * (GRID + 30)
        glu = cut("glu", o, 2 * PADC).rearrange("p (m t) -> p m t", m=2)
        diag = [cut(f"diag{i}", o + 2 * PADC + i * P, P) for i in range(3)]
        assert 2 * PADC + 3 * P <= NCP * CR
        vtok = cut("vtok", o, NCP * CR).rearrange("p (c w) -> p c w", c=NCP); o += NCP * CR
        conv_b = cut("conv_b", o, 2 * T).rearrange("p (m t) -> p m t", m=2)
        diag += [cut(f"diag{3 + i}", o + 2 * T + i * P, P) for i in range(5)]
        Y = cut("Y", o, NCP * CR).rearrange("p (c w) -> p c w", c=NCP); o += NCP * CR
        St = cut("St", o, NC_ * 512).rearrange("p (c m v) -> p c m v", c=NC_, m=NM); o += NC_ * 512
        Sfin = cut("Sfin", o, 256).rearrange("p (m v) -> p m v", m=NM); o += 256
        XW = o
        Wb = [cut(f"Wb{i}", o + 512 * i, 512) for i in range(2)]
        Xs = [cut(f"Xs{i}", o + 256 * i, 256) for i in range(3)]
        rs = cut("rs", o, T); o += 1024
        st_in = cut("st_in", o, 1024); o += 1024
        sout = cut("sout", o, 512); o += 512
        prod = cut("prod", ffn_at, KF * T).rearrange("p (k t) -> p k t", k=KF)
        fsig = [cut(f"fsig{i}", ffn_at + KF * T + i * T, T) for i in range(3)]
        assert o <= TOTAL, o
        o = low_end
        htok = cut("htok", o, 3 * DM).rearrange("p (j d) -> p j d", j=3); o += 3 * DM
        hG = cut("hG", o, DM).rearrange("p (k s) -> p k s", k=KD); o += DM
        eprod = cut("eprod", o, DE)
        ey = cut("ey", o, DM); o += DE
        eprodT = cut("eprodT", o, KE * P).rearrange("p (k s) -> p k s", k=KE); o += KE * P
        sel = cut("sel", o, 3 * P).rearrange("p (j s) -> p j s", j=3); o += 3 * P
        selc = cut("selc", o, 3 * P).rearrange("p (j s) -> p j s", j=3); o += 3 * P
        selT = cut("selT", o, 3 * P).rearrange("p (j s) -> p j s", j=3); o += 3 * P
        esig = cut("esig", o, 512); o += 512
        rt = cut("rt", o, 900); o += 900
        rt_i = rt[:, 560:600].bitcast(I32)
        wrt = cut("wrt", o, 64).rearrange("p (k e) -> p k e", k=KD); o += 64
        brt = cut("brt", o, 8); o += 8
        yacc = cut("yacc", used["hT"][0], 3 * DM).rearrange("p (j d) -> p j d", j=3)
        o = TOTAL - (2 * KD * DE + KE * DM)
        assert o >= used["brt"][1], (o, used["brt"])
        wgu = []
        for c, (c0, n) in enumerate(CHUNKS):
            pair = []
            for which in range(2):
                pair.append(cut(f"wgu{c}{which}", o, KD * n).rearrange("p (k n) -> p k n", k=KD)); o += KD * n
            wgu.append(pair)
        wdn = cut("wdn", o, KE * DM).rearrange("p (k n) -> p k n", k=KE)

        def tab(name):
            a, n = tcol[name]
            return first[:, a:a + n] if name in FIRST else second[:, a - n_first:a - n_first + n]

        ident, ones, heads, before, iota = (tab(k) for k in ("ident", "ones", "heads", "before", "iota"))
        pair_mask = tab("pair_mask").rearrange("p (d w) -> p d w", d=2)
        level_mask = tab("level_mask").rearrange("p (l w) -> p l w", l=LEVELS)
        time_p = tab("time_p").rearrange("p (j k n) -> p j k n", j=1, k=2)
        time_s = tab("time_s").rearrange("p (j k n) -> p j k n", j=2, k=2)
        eps = {v: tab("eps")[:, i:i + 1] for i, v in enumerate((1e-6, 1e-5, 64e-5))}

        vat = {}
        for l in range(DEPTH):
            for gi, g in enumerate("AB"):
                r = 0
                for name, n in VEC[g]:
                    vat[name, l] = (2 * l + gi, r)
                    r += n
                if g == "A" and l == 0:
                    for name, n in SHARED:
                        vat[name, 0] = (0, r)
                        r += n

        def v(name, l, i=0, n=1):
            g, r = vat[name, l]
            return vec[:, g, r + i:r + i + n]

        def gsig(i):
            return tmp4[3 if i % 8 >= 4 else 0][:, (i % 4) * T:(i % 4 + 1) * T]

        sems = {}

        class Sem:
            def __init__(self, name):
                self.h, self.n = ctx.enter_context(nc.semaphore(name)), 0

        def sem(name):
            if name not in sems:
                sems[name] = Sem(name)
            return sems[name]

        def at(name, *key):
            return sem(name).h, marks.get((name,) + key, 1)

        class Counts:

            def __init__(self, steps):
                self.steps = steps

            def up(self, name, *key, by=1):
                s = sem(name)
                s.n += by
                marks[(name,) + key] = s.n
                if by == 1:
                    self.last = (s.h, s.n)
                return s.h, by

            def step(self):
                return self.up(self.steps)

            def read(self, *job):
                name = f"bank_free{marks.get(('bank',) + job, 0)}"
                self.last = at(name, *job)
                return sem(name).h, 1

            def fill(self, *job):
                return self.up(f"bank_full{marks[('bank',) + job]}", *job)

            def latest(self):
                return self.last

        def bank(*job):
            return psum[marks.get(("bank",) + job, 0)]

        def filled(*job):
            return at(f"bank_full{marks.get(('bank',) + job, 0)}", *job)

        def drained(*job):
            return at(f"bank_free{marks.get(('bank',) + job, 0)}", *job)

        blocks = []

        def wview(i, k, n):
            return ring[i][:, 0:k * n].rearrange("p (k n) -> p k n", k=k)

        def cols(w, c0, n, k=KD):
            return w.rearrange("(k p) n -> p k n", p=P)[:, :, c0:c0 + n], k, n

        def add(key, srcs, last):
            blocks.append((key, srcs, last))

        for l in range(DEPTH):
            for i in range(24):
                add(("ada", l, i), [cols(dram["w_ada"][l], 256 * i, 256)], ("ada", l, i))
            for i in range(8):
                n = 256 if i < 7 else 128
                add(("z", l, i), [cols(dram["w_in"][l], OFF_Z + 256 * i, n)], ("z", l, min(2 * i + 1, 14)))
            for i in range(3):
                add(("cf", l, i), [cols(dram["w_in"][l], 256 * i, 256)], ("cf", l, 2 * i + 1))
            add(("low", l), [(dram["dec_up"][l].rearrange("d r c -> (d r) c"), 1, 512),
                             (dram["iclr_up"][l].rearrange("d r c -> (d r) c"), 1, 512),
                             (dram["g_up"][l], 1, 512)], ("gup", l, 3))
            for b, (w, k) in enumerate((("w_conv_out", 2), ("w_fno_out", 2), ("w_rwkv_out", 4))):
                for i in range(4):
                    add(("bw", l, b, i), [cols(dram[w][l], 256 * i, 256, k)], ("br", l, b, 2 * i + 1))
                    add(("gate", l, b, i), [cols(dram["w_in"][l], OFF_G + DM * b + 256 * i, 256)], ("gate", l, b, 2 * i + 1))
            for i in range(4):
                add(("wo", l, i), [cols(dram["w_o"][l], 256 * i, 256)], ("o", l, 2 * i + 1))
            if l % 2 == 0:
                for i in range(KF // 2):
                    add(("fg", l, i), [cols(dram["ffn_w_gate"][l // 2], 256 * i, 256)], ("fg", l, 2 * i + 1))
                    add(("fu", l, i), [cols(dram["ffn_w_up"][l // 2], 256 * i, 256)], ("fu", l, 2 * i + 1))
                for i in range(KF // 2):
                    add(("fd", l, i), [(dram["ffn_w_down"][l // 2].rearrange("(k p) n -> p k n", p=P)[:, 2 * i:2 * i + 2, :], 2, DM)],
                        ("fd", l, i))
        slot_of = {key: n % RING for n, (key, _, _) in enumerate(blocks)}

        block = ctx.enter_context(nc.Block())

        @block.sync
        def _(sp):
            S = Counts("sync_step")
            for n, (key, srcs, last) in enumerate(blocks):
                if n >= RING:
                    prev = blocks[n - RING]
                    if prev[2][0] in ("ada", "fd"):
                        sp.wait_ge(*at("block_used", *prev[2]))
                    else:
                        sp.wait_ge(*filled(*prev[2]))
                at_ = 0
                for src, k, w in srcs:
                    dst = ring[n % RING][:, at_:at_ + k * w]
                    if len(src.shape) == 3:
                        dst = dst.rearrange("p (k n) -> p k n", k=k)
                    sp.dma_start(dst, src).then_inc(*S.up(f"block_in{n % RING}", *key, by=16))
                    at_ += k * w
            sp.wait_ge(*at("h2_ready", 1))
            sp.wait_ge(*filled("o", 1, 7))
            sp.wait_ge(*at("out_stored", "state", 1, 1))

            def expert_weights(e, wait):
                for c, (c0, n) in enumerate(CHUNKS):
                    if wait is not None:
                        sp.wait_ge(sem("e_gu").h, wait * 3 + (c + 1))
                    for which, w in enumerate(("moe_w_gate", "moe_w_up")):
                        src = dram[w][0, e].rearrange("(k p) n -> p k n", p=P)[:, :, c0:c0 + n]
                        sp.dma_start(wgu[c][which][:, :, :], src).then_inc(sem(f"e_gu_in{c}").h, 16)
                    k0, kn = DOWN[c]
                    if wait is not None and c == 0:
                        sp.wait_ge(sem("e_y").h, wait + 1)
                    src = dram["moe_w_down"][0, e].rearrange("(k p) n -> p k n", p=P)[:, k0:k0 + kn, :]
                    sp.dma_start(wdn[:, k0:k0 + kn, :], src).then_inc(sem(f"e_dn_in{c}").h, 16)

            expert_weights(0, None)
            sp.wait_ge(*at("jobs_ready"))
            jobs = sp.value_load(rt_i[0:1, 0:1], min_val=NE, max_val=NJOB)
            with sp.Fori(1, jobs) as j:
                e = sp.value_load(rt_i[0:1, bass.ds(j + 1, 1)], min_val=0, max_val=NE - 1)
                expert_weights(e, j - 1)
            sp.wait_ge(sem("out_stored").h, 16 * 7)

        @block.tensor
        def _(pe):
            E = Counts("pe_step")
            jobs = [0]
            uses = [0] * 4
            prev_job = {}

            def used_for(b, *job):
                uses[b] += 1
                marks[(f"bank_free{b}",) + job] = uses[b]
                prev_job[b] = job

            def begin(*job):
                b = jobs[0] % 4
                jobs[0] += 1
                marks[("bank",) + job] = b
                if b in prev_job:
                    pe.wait_ge(*at(f"bank_free{b}", *prev_job[b]))
                used_for(b, *job)
                return psum[b]

            def transpose(out, src, n=P):
                return pe.transpose(out, src, ident[0:n, 0:n])

            def mm(out, lhsT, rhs, start, stop):
                return pe.matmul(out, lhsT, rhs, start=start, stop=stop)

            def tile(out, w, rhs, kn=KD):
                for k in range(kn):
                    last = mm(out, w(k), rhs(k), k == 0, k == kn - 1)
                return last

            pe.wait_ge(*at("first_in"))
            pe.wait_ge(*at("rows_in"))
            b = begin("vec")
            for g in range(4):
                n = sum(r for _, r in VEC["AB"[g % 2]]) + (24 if g == 0 else 0)
                last = transpose(b[:, g * P:g * P + n], rows[0:n, g, :], n)
            last.then_inc(*E.fill("vec"))
            pe.wait_ge(*at("x_in"))
            for k in range(KD):
                b = begin("xt", k)
                for j in range(3):
                    last = transpose(b[:, j * P:(j + 1) * P], xin[:, j, k * P:(k + 1) * P])
                last.then_inc(*E.fill("xt", k))

            def norm_sum(l, which):
                b = begin("norm", l, which)
                for k in range(KD):
                    if k == 0 or k == 4:
                        pe.wait_ge(*at("sq_ready", l, which, k // 4))
                    last = mm(b[:, 0:T], ones, sq[:, k, :], k == 0, k == KD - 1)
                last.then_inc(*E.fill("norm", l, which))

            def pair_tiles(kind, l, nblk, ntile, rhs, need=None):
                for i in range(nblk):
                    key = (kind,) + l + (i,)
                    jobk = {"wo": "o"}.get(kind, kind)
                    pe.wait_ge(*at(f"block_in{slot_of[key]}", *key))
                    n = min(2, ntile - 2 * i)
                    w = wview(slot_of[key], KD, n * P)
                    for h in range(n):
                        m = 2 * i + h
                        b = begin(jobk, *l, m)
                        tile(b[:, 0:T], lambda k: w[:, k, h * P:(h + 1) * P], rhs).then_inc(*E.fill(jobk, *l, m))
                        yield m

            for l in range(DEPTH):
                if l == 0:
                    pe.wait_ge(*at("cond_ready"))
                b = begin("ada", l)
                for i in range(24):
                    key = ("ada", l, i)
                    pe.wait_ge(*at(f"block_in{slot_of[key]}", *key))
                    w = wview(slot_of[key], KD, 256)
                    for h in range(2):
                        m = 2 * i + h
                        last = tile(b[:, 2 * m:2 * m + 2], lambda k: w[:, k, h * P:(h + 1) * P], lambda k: cond[:, k, :])
                    last.then_inc(*E.up("block_used", "ada", l, i))
                norm_sum(l, 0)
                pe.wait_ge(*at("h_ready", l))
                for _ in pair_tiles("z", (l,), 8, NZ, lambda k: hT[:, k, :]):
                    pass
                for _ in pair_tiles("cf", (l,), 3, 6, lambda k: hT[:, k, :]):
                    pass
                if l == 0:
                    pe.wait_ge(*at("second_in"))
                for m in range(NM):
                    b = begin("kks", l, m)
                    if m == 0:
                        pe.wait_ge(*at("ksq_ready", l))
                    mm(b[:, 0:T], heads, ksq[:, m, :], True, True).then_inc(*E.fill("kks", l, m))
                lowk = ("low", l)
                low = ring[slot_of[lowk]][:, 0:1536].rearrange("p (w c) -> p w c", w=3)

                def lowrank(d):
                    if d == 0:
                        pe.wait_ge(*at(f"block_in{slot_of[lowk]}", *lowk))
                        pe.wait_ge(*at("low_in_ready", l))
                    r = slice(64 * d, 64 * d + 64)
                    for which in range(2):
                        for m in range(NM):
                            b = begin("low", l, d, which, m)
                            mm(b[:, 0:T], low[r, which, m * P:(m + 1) * P], z[r, 13 + which, :], True, True).then_inc(*E.fill("low", l, d, which, m))

                lowrank(0)
                for m in range(4, 6):
                    pe.wait_ge(*drained("cf", l, m))
                for j in range(NCP):
                    b = begin("fno1", l, j)
                    for m in range(2):
                        last = mm(b[:, m * 256:(m + 1) * 256], fno_u[:, m, j * P:(j + 1) * P],
                                  second[:, tcol["dft_c"][0] - n_first:tcol["dft_c"][0] - n_first + 256], True, True)
                    last.then_inc(*E.fill("fno1", l, j))
                for j in range(NCP):
                    pe.wait_ge(*drained("fno1", l, j))
                for m in range(2):
                    b = begin("fno2", l, m)
                    for i in range(2):
                        mm(b[:, 0:TP], fno_z[:, 0, m, i * P:(i + 1) * P], time_p[:, 0, i, :], i == 0, i == 1)
                    for j in range(2):
                        for i in range(2):
                            last = mm(b[:, TP:T], fno_z[:, 1 + j, m, i * P:(i + 1) * P], time_s[:, j, i, :],
                                      j == 0 and i == 0, j == 1 and i == 1)
                    last.then_inc(*E.fill("fno2", l, m))
                pe.wait_ge(*at("glu_ready", l))
                for m in range(2):
                    b = begin("conv", l, m)
                    b2 = begin("conv_s", l, m)
                    sp_ = glu[:, m, TP + 30:].rearrange("p (r t) -> p r t", r=4)
                    for j in range(CONV_W):
                        i = m * CONV_W + j
                        pe.wait_ge(*at("diag_ready", l, i))
                        mm(b[:, 0:TP], diag[i % 8], glu[:, m, j:j + TP], j == 0, j == CONV_W - 1)
                        last = mm(b2[:, 0:TS].rearrange("p (r t) -> p r t", r=4), diag[i % 8], sp_[:, :, j:j + GRID], j == 0, j == CONV_W - 1)
                        if j < CONV_W - 1:
                            last.then_inc(*E.up("diag_used", l, i))
                    last.then_inc(*E.fill("conv_s", l, m))
                for w in range(2):
                    b = begin("cln", l, w)
                    if w == 0:
                        for m in range(2):
                            pe.wait_ge(*drained("conv", l, m))
                            pe.wait_ge(*drained("conv_s", l, m))
                    else:
                        pe.wait_ge(*at("conv_sq", l))
                    src = cvT if w == 0 else conv_b
                    for m in range(2):
                        last = mm(b[:, 0:T], ones, src[:, m, :], m == 0, m == 1)
                    last.then_inc(*E.fill("cln", l, w))

                for d in range(2):
                    if d == 1:
                        lowrank(1)
                    pe.wait_ge(*at("ark_ready", l, d))
                    for cp in range(NCP):
                        for i in range(3 if d == 0 else 2):
                            b = begin("tok", l, d, cp, i)
                            for m in range(NM):
                                src = (BK[:, i, m, :] if i < 2 else z[:, 8 + m, :])[:, cp * P:(cp + 1) * P]
                                last = transpose(b[:, m * P:(m + 1) * P], src)
                            last.then_inc(*E.fill("tok", l, d, cp, i))
                    for cp in range(NCP):
                        for hp in range(NH // 2):
                            b = begin("pair", l, d, cp, hp)
                            r = slice(64 * (hp % 2), 64 * (hp % 2) + 64)
                            for i in range(2):
                                for hh in range(2):
                                    m = 2 * (hp // 2) + hh
                                    for par in range(2):
                                        q = slice(64 * par, 64 * par + 64)
                                        c = 2 * cp + par
                                        o_ = hh * 256 + i * P
                                        last = mm(b[q, o_:o_ + P], BK[r, i, m, c * C:(c + 1) * C],
                                                  AR[r, m, c, :, :], True, True)
                            last.then_inc(*E.fill("pair", l, d, cp, hp))
                    for lev in range(LEVELS):
                        for u in range(7):
                            if u < 6:
                                cp, g = divmod(u, 2)
                                b = begin("X", l, d, lev, u)
                                if lev == 0:
                                    pe.wait_ge(*at("TQ_ready", l, d, u))
                                else:
                                    pe.wait_ge(*drained("TAT", l, d, lev - 1, u))
                                for par in range(2):
                                    q = slice(64 * par, 64 * par + 64)
                                    for h in range(4):
                                        last = mm(b[q, h * C:(h + 1) * C], S1[q, cp, 4 * g + h, 0:C],
                                                  TQ[q, cp, 4 * g + h, 0:C], True, True)
                                last.then_inc(*E.fill("X", l, d, lev, u))
                            if u > 0:
                                w = u - 1
                                cp, g = divmod(w, 2)
                                b = begin("TAT", l, d, lev, w)
                                pe.wait_ge(*drained("X", l, d, lev, w))
                                for par in range(2):
                                    q = slice(64 * par, 64 * par + 64)
                                    for h in range(4):
                                        Q = TQ[q, cp, 4 * g + h, C:2 * C]
                                        X = Xs[w % 3][q, h * C:(h + 1) * C]
                                        mm(b[q, h * P:h * P + C], Q, X, True, True)
                                        last = mm(b[q, h * P + C:(h + 1) * P], X, Q, True, True)
                                last.then_inc(*E.fill("TAT", l, d, lev, w))
                    if d == 0:
                        pe.wait_ge(*at("st_in", l))
                    b = begin("s0", l, d)
                    sti = st_in.rearrange("p (d h k) -> p d h k", d=2, h=NH)
                    for m in range(NM):
                        last = transpose(b[:, m * C:(m + 1) * C], sti[0:64, d, 2 * m:2 * m + 2, :], 64)
                    last.then_inc(*E.fill("s0", l, d))
                    for n, c in enumerate(order(d)):
                        cp, par = divmod(c, 2)
                        q = slice(64 * par, 64 * par + 64)
                        if c == starts(d)[1]:
                            pe.wait_ge(*drained("s0", l, d))
                        else:
                            pe.wait_ge(*at("S_ready", l, d, c))
                        b = begin("W", l, d, c)
                        for m in range(NM):
                            mm(b[q, m * P:(m + 1) * P], AR[:, m, c, 0, :], St[:, c, m, :], m == 0, False)
                        for h in range(NH):
                            last = mm(b[q, h * C:(h + 1) * C], S1[q, cp, h, 2 * C:3 * C], vtok[q, cp, h * C:(h + 1) * C],
                                      False, h == NH - 1)
                        last.then_inc(*E.fill("W", l, d, c))
                        b = begin("U", l, d, c)
                        pe.wait_ge(*drained("W", l, d, c))
                        for h in range(NH):
                            last = mm(b[q, h * C:(h + 1) * C], TQ[q, cp, h, C:2 * C], Wb[n % 2][q, h * C:(h + 1) * C], True, True)
                        last.then_inc(*E.fill("U", l, d, c))
                        if nxt(d, c) is None:
                            continue
                        b = begin("S", l, d, c)
                        pe.wait_ge(*drained("U", l, d, c))
                        for h in range(NH):
                            m, r = h // 2, slice(64 * (h % 2), 64 * (h % 2) + 64)
                            oc = b[r, m * C:(m + 1) * C]
                            hs = slice(h * C, (h + 1) * C)
                            mm(oc, tok[q, 1, cp, hs], vtok[q, cp, hs], True, False)
                            last = mm(oc, tok[q, 0, cp, hs], U[q, cp, h, :], False, True)
                        last.then_inc(*E.fill("S", l, d, c))
                    pe.wait_ge(*drained("U", l, d, order(d)[-1]))
                    for cp in range(NCP):
                        b = begin("Y", l, d, cp)
                        for par in range(2):
                            q = slice(64 * par, 64 * par + 64)
                            c = 2 * cp + par
                            for m in range(NM):
                                mm(b[q, m * P:(m + 1) * P], AR[:, m, c, 1, :], St[:, c, m, :], m == 0, False)
                            for h in range(NH):
                                hs = slice(h * C, (h + 1) * C)
                                mm(b[q, hs], S1[q, cp, h, C:2 * C], U[q, cp, h, :], False, False)
                                last = mm(b[q, hs], S1[q, cp, h, 3 * C:4 * C], vtok[q, cp, hs], False, h == NH - 1)
                        last.then_inc(*E.fill("Y", l, d, cp))
                    b = begin("sf", l, d)
                    pe.wait_ge(*at("Sfin_ready", l, d))
                    for m in range(NM):
                        last = transpose(b[0:64, m * P:(m + 1) * P], Sfin[:, m, :])
                    last.then_inc(*E.fill("sf", l, d))
                for cp in range(NCP):
                    b = begin("yt", l, cp)
                    if cp == 0:
                        pe.wait_ge(*at("yn_ready", l))
                    for m in range(NM):
                        last = transpose(b[:, m * P:(m + 1) * P], Y[:, cp, m * P:(m + 1) * P])
                    last.then_inc(*E.fill("yt", l, cp))
                for m in range(NM):
                    b = begin("bon", l, m)
                    if m == 0:
                        pe.wait_ge(*at("rk_ready", l))
                    mm(b[:, 0:T], heads, tmp4[1][:, m * T:(m + 1) * T], True, True).then_inc(*E.fill("bon", l, m))
                for m in range(NM):
                    b = begin("gup", l, m)
                    mm(b[:, 0:T], low[:, 2, m * P:(m + 1) * P], z[:, 12, :], True, True).then_inc(*E.fill("gup", l, m))
                for b_, (src, kn) in enumerate(((cvT, 2), (fnT, 2), (yT, 4))):
                    if b_ == 0:
                        pe.wait_ge(*at("cv_ready", l))
                    for m in range(2 if b_ == 1 else NM if b_ == 2 else 0):
                        pe.wait_ge(*drained(*(("fno2", l, m) if b_ == 1 else ("gup", l, m))))
                    for i in range(4):
                        key = ("gate", l, b_, i)
                        pe.wait_ge(*at(f"block_in{slot_of[key]}", *key))
                        w = wview(slot_of[key], KD, 256)
                        key = ("bw", l, b_, i)
                        pe.wait_ge(*at(f"block_in{slot_of[key]}", *key))
                        wb = wview(slot_of[key], kn, 256)
                        for h in range(2):
                            m = 2 * i + h
                            b = begin("gate", l, b_, m)
                            tile(b[:, 0:T], lambda k: w[:, k, h * P:(h + 1) * P], lambda k: hT[:, k, :]).then_inc(*E.fill("gate", l, b_, m))
                            b = begin("br", l, b_, m)
                            tile(b[:, 0:T], lambda k: wb[:, k, h * P:(h + 1) * P], lambda k: src[:, k, :], kn).then_inc(*E.fill("br", l, b_, m))
                pe.wait_ge(*at("gated", l, 2, KD - 1))
                for _ in pair_tiles("wo", (l,), 4, 8, lambda k: merged[:, k, :]):
                    pass
                norm_sum(l, 1)
                pe.wait_ge(*at("h2_ready", l))
                if l % 2 == 0:
                    for i in range(KF // 2):
                        for kind in ("fg", "fu"):
                            key = (kind, l, i)
                            pe.wait_ge(*at(f"block_in{slot_of[key]}", *key))
                        wg, wu = (wview(slot_of[(kind, l, i)], KD, 256) for kind in ("fg", "fu"))
                        for h in range(2):
                            m = 2 * i + h
                            for kind, w in (("fg", wg), ("fu", wu)):
                                b = begin(kind, l, m)
                                tile(b[:, 0:T], lambda k: w[:, k, h * P:(h + 1) * P], lambda k: hT[:, k, :]).then_inc(*E.fill(kind, l, m))
                    for m in range(4):
                        pe.wait_ge(*at(f"bank_free{m}", *prev_job[m]))
                    for i in range(KF // 2):
                        key = ("fd", l, i)
                        pe.wait_ge(*at(f"block_in{slot_of[key]}", *key))
                        w = wview(slot_of[key], 2, DM)
                        pe.wait_ge(*drained("fu", l, 2 * i + 1))
                        for h in range(2):
                            k = 2 * i + h
                            for m in range(KD):
                                last = mm(psum[m][:, 0:T], w[:, h, m * P:(m + 1) * P], prod[:, k, :], k == 0, k == KF - 1)
                        last.then_inc(*E.up("block_used", "fd", l, i))
                    for m in range(4):
                        used_for(m, "fdown", l, m)
            b = begin("logit")
            pe.wait_ge(*at("router_in"))
            for j in range(3):
                for k in range(KD):
                    mm(b[:, j * NE:(j + 1) * NE], hT[:, k, j * P:(j + 1) * P], wrt[:, k, :], k == 0, False)
                last = mm(b[:, j * NE:(j + 1) * NE], ones[0:1, :], brt[0:1, :], False, True)
            last.then_inc(*E.fill("logit"))
            for k in range(6):
                b = begin("htok", k)
                for i in range(4):
                    j, kk_ = divmod(4 * k + i, KD)
                    last = transpose(b[:, i * P:(i + 1) * P], hT[:, kk_, j * P:(j + 1) * P])
                last.then_inc(*E.fill("htok", k))
            b = begin("rank")
            pe.wait_ge(*at("chosen_ready"))
            ch = rt[:, 0:24]
            for j in range(3):
                for i in range(j + 1):
                    mm(b[:, j * NE:(j + 1) * NE], before if i == j else ones, ch[:, i * NE:(i + 1) * NE], i == 0, i == j)
            for i in range(3):
                last = mm(b[:, 24:32], ones, ch[:, i * NE:(i + 1) * NE], i == 0, i == 2)
            last.then_inc(*E.fill("rank"))
            pe.wait_ge(*at("jobs_ready"))
            for m in range(4):
                pe.wait_ge(*at(f"bank_free{m}", *prev_job[m]))
            pe.wait_ge(*at("fdown_done", 0))
            s = lambda name: sem(name).h
            pe.sem_inc(s("e_sc"), 6)
            njobs = pe.value_load(rt_i[0:1, 0:1], min_val=NE, max_val=NJOB)
            with pe.Fori(0, njobs) as i:
                pe.wait_ge(s("e_sel"), i + 1)
                pe.wait_ge(s("e_ydrained"), i * 2 + 2)
                for j in range(3):
                    last = transpose(psum[4][:, j * P:(j + 1) * P], selc[:, j, :])
                last.then_inc(s("e_selT_full"), 1)
                pe.wait_ge(s("e_sc_done"), i * 6 + 6)
                for k in range(KD):
                    for j in range(3):
                        last = mm(psum[6 + k // 4][:, (k % 4) * P:(k % 4 + 1) * P], htok[:, j, k * P:(k + 1) * P],
                                  sel[:, j, :], j == 0, j == 2)
                    if k % 4 == 3:
                        last.then_inc(s("e_gather"), 1)
                pe.wait_ge(s("e_hG"), i * 2 + 2 + 2)
                for c, (c0, n) in enumerate(CHUNKS):
                    bg, bu = psum[2 * (c % 2)], psum[2 * (c % 2) + 1]
                    pe.wait_ge(s("e_prod"), i * 3 + 3 + (1 if c == 2 else 0))
                    pe.wait_ge(s(f"e_gu_in{c}"), i * 32 + 32)
                    for which, bb in ((0, bg), (1, bu)):
                        for k in range(KD):
                            last = mm(bb[:, 0:n], hG[:, k, :], wgu[c][which][:, k, :], k == 0, k == KD - 1)
                    last.then_inc(s("e_gu"), 1)
                    if c > 0:
                        e_transposes(pe, s, transpose, psum, eprod, i, c - 1)
                for c, (k0, kn) in enumerate(DOWN):
                    if c == 2:
                        e_transposes(pe, s, transpose, psum, eprod, i, 2)
                    pe.wait_ge(s(f"e_dn_in{c}"), i * 16 + 16)
                    pe.wait_ge(s("e_pT"), i * 3 + c + 1)
                    if c == 0:
                        pe.wait_ge(s("e_selT"), i + 1)
                    for k in range(k0, k0 + kn):
                        for half in range(2):
                            last = mm(psum[4 + half][:, :], eprodT[:, k, :], wdn[:, k, half * 512:(half + 1) * 512],
                                      k == 0, k == KE - 1)
                last.then_inc(s("e_y"), 1)
                pe.wait_ge(s("e_ydrained"), i * 2 + 2 + 2)
                for j in range(3):
                    for half in range(2):
                        n_ = 2 * j + half
                        if n_ >= 2:
                            pe.wait_ge(s("e_sc_done"), i * 6 + 6 + n_ - 1)
                        mm(psum[6 + half][:, :], selT[:, j, :], ey[:, half * 512:(half + 1) * 512], True, True)\
                            .then_inc(s("e_sc"), 1)
            for m in range(4):
                prev_job.pop(m, None)
            pe.wait_ge(*at("yacc_ready"))
            for k in range(KD):
                b = begin("ey", k)
                for j in range(3):
                    last = transpose(b[:, j * P:(j + 1) * P], yacc[:, j, k * P:(k + 1) * P])
                last.then_inc(*E.fill("ey", k))
            norm_sum(DEPTH, 0)
            pe.wait_ge(*at("h_ready", DEPTH))
            for j in range(3):
                for half in range(2):
                    b = begin("yo", j, half)
                    for k in range(4):
                        last = transpose(b[:, k * P:(k + 1) * P], sq[:, 4 * half + k, j * P:(j + 1) * P])
                    last.then_inc(*E.fill("yo", j, half))

        @block.scalar
        def _(act):
            E = Counts("act_step")
            a = act.activation

            act.dma_start(first, dram["tables"][:, 0:n_first]).then_inc(*E.up("first_in", by=16))
            for g in range(4):
                l, r = g // 2, 0
                for name, n in VEC["AB"[g % 2]]:
                    src = dram[name][l]
                    act.dma_start(rows[r:r + n, g, :], flat(src).rearrange("(r c) -> r c", c=P)).then_inc(*E.up("rows_in", by=16))
                    r += n
                if g == 0:
                    for name, n in SHARED:
                        act.dma_start(rows[r:r + n, g, :], flat(dram[name]).rearrange("(r c) -> r c", c=P)).then_inc(*E.up("rows_in", by=16))
                        r += n
            for j in range(3):
                src = dram["x_prompt"][0] if j == 0 else dram["x_sample"][0][(j - 1) * P:j * P, :]
                act.dma_start(xin[:, j, :], src).then_inc(*E.up("x_in", by=16))
            act.dma_start(second, dram["tables"][:, n_first:ncols]).then_inc(*E.up("second_in", by=16))

            def load_state(l):
                sti = st_in.rearrange("p (d h k) -> p d h k", d=2, h=NH)
                for d in range(2):
                    act.dma_start(sti[0:64, d, :, :], dram["state_rwkv"][0, l, d].rearrange("h v k -> v h k")).then_inc(*E.up("st_in", l, by=16))

            load_state(0)
            act.wait_ge(*filled("vec"))
            for g in range(4):
                n = sum(r for _, r in VEC["AB"[g % 2]]) + (24 if g == 0 else 0)
                ins = a(vec[:, g, 0:n], bank("vec")[:, g * P:g * P + n], ACT.Copy)
                if g == 3:
                    ins.then_inc(*E.read("vec"))
            act.wait_ge(*E.latest())
            for i, name in ((0, "c_ctx"), (1, "c")):
                a(condx[:, :, i], v(name, 0, 0, 8), ACT.Copy).then_inc(*E.step())
                a(cond[:, :, i], v(name, 0, 0, 8), ACT.Sigmoid).then_inc(*E.up("cond_sig", i))
            for k in range(KD):
                act.wait_ge(*filled("xt", k))
                a(xT[:, k, :], bank("xt", k)[:, 0:T], ACT.Copy).then_inc(*E.read("xt", k))

            def squares(l, which):
                for i in range(2):
                    if which == 1:
                        act.wait_ge(*drained("o", l, 4 * i + 3))
                    elif l == DEPTH:
                        act.wait_ge(*drained("ey", 4 * i + 3))
                    elif l > 0 and i == 0:
                        act.wait_ge(*at("bank_free3", "fdown", l - 1, 3))
                    elif l > 0:
                        act.wait_ge(*at("fdown_done", l - 1))
                    elif i == 0:
                        act.wait_ge(*E.latest())
                    a(sq[:, 4 * i:4 * i + 4, :], xT[:, 4 * i:4 * i + 4, :], ACT.Square).then_inc(*E.up("sq_ready", l, which, i))

            def root(l, which):
                act.wait_ge(*filled("norm", l, which))
                a(rs, bank("norm", l, which)[:, 0:T], ACT.Sqrt, bias=eps[1e-6], scale=1.0 / DM).then_inc(*E.read("norm", l, which))

            def modulate(l, which):
                for k in range(KD):
                    act.wait_ge(*at("xn_ready", l, which, k // 4))
                    for s_, (t0, t1) in enumerate(SEG):
                        ins = a(hT[:, k, t0:t1], hT[:, k, t0:t1], ACT.Identity,
                                bias=mod[:, 24 * which + k, s_:s_ + 1], scale=modA[:, which, k, s_:s_ + 1])
                        if k == KD - 1 and s_ == 1:
                            ins.then_inc(*E.up("h2_ready" if which else "h_ready", l))

            for l in range(DEPTH):
                squares(l, 0)
                root(l, 0)
                act.wait_ge(*at("modA_ready", l))
                modulate(l, 0)
                for m in range(NZ):
                    act.wait_ge(*filled("z", l, m))
                    a(z[:, m, :], bank("z", l, m)[:, 0:T], ACT.Copy).then_inc(*E.read("z", l, m))
                for m in range(6):
                    act.wait_ge(*filled("cf", l, m))
                    src = bank("cf", l, m)[:, 0:T]
                    if m < 2:
                        ins = a(cvT[:, m, :], src, ACT.Copy)
                    elif m < 4:
                        ins = a(conv_b[:, m - 2, :], src, ACT.Sigmoid)
                    else:
                        ins = a(fno_u[:, m - 4, :], src, ACT.Copy)
                    ins.then_inc(*E.read("cf", l, m))
                act.wait_ge(*at("mix_done", l))
                a(z[:, 12, :], z[:, 12, :], ACT.Sigmoid).then_inc(*E.up("act_step"))
                a(z[:, 13, :], z[:, 13, :], ACT.Tanh).then_inc(*E.up("low_in_ready", l))
                act.wait_ge(*at("kkp_ready", l))
                a(ksq, kk, ACT.Square).then_inc(*E.up("ksq_ready", l))
                for m in range(NM):
                    act.wait_ge(*filled("kks", l, m))
                    a(tmp4[0][:, m * T:(m + 1) * T], bank("kks", l, m)[:, 0:T], ACT.Sqrt).then_inc(*E.read("kks", l, m))

                def lowrank(d):
                    if d == 0:
                        act.wait_ge(*at("kk_ready", l))
                    else:
                        act.wait_ge(*filled("Y", l, 0, NCP - 1))
                    for which, name in enumerate(("dec_w0", "iclr_a0")):
                        for m in range(NM):
                            act.wait_ge(*filled("low", l, d, which, m))
                            ins = a(tmp4[which][:, m * T:(m + 1) * T], bank("low", l, d, which, m)[:, 0:T], ACT.Sigmoid,
                                    bias=v(name, l, NM * d + m))
                            ins.then_inc(*E.read("low", l, d, which, m))

                def exps(d):
                    act.wait_ge(*at("L_ready", l, d))
                    L = L3(d)
                    tot = tmp4[2].rearrange("p (m c t) -> p m c t", m=NM, c=NC_)[:, :, :, C - 1]
                    a(pc, tot, ACT.Exp, scale=-DECAY).then_inc(*E.step())
                    a(tmp4[0], tmp4[0], ACT.Exp, scale=-DECAY).then_inc(*E.up("E1_ready", l, d))
                    act.wait_ge(*E.latest())
                    a(tmp4[other(d)], tmp4[L], ACT.Exp, scale=-DECAY).then_inc(*E.up("E2_ready", l, d))
                    act.wait_ge(*E.latest())
                    a(tmp4[L], tmp4[L], ACT.Exp, scale=DECAY).then_inc(*E.up("E3_ready", l, d))

                lowrank(0)
                exps(0)
                for m in range(2):
                    act.wait_ge(*filled("fno2", l, m))
                    a(fnT[:, m, :], bank("fno2", l, m)[:, 0:T], ACT.Copy).then_inc(*E.read("fno2", l, m))
                for m in range(2):
                    act.wait_ge(*filled("conv_s", l, m))
                    if m == 0:
                        act.wait_ge(*at("glu_ready", l))
                    a(cvT[:, m, 0:TP], bank("conv", l, m)[:, 0:TP], ACT.Identity, bias=v("dw_b", l, m)).then_inc(*E.read("conv", l, m))
                    a(cvT[:, m, TP:T], bank("conv_s", l, m)[:, 0:TS], ACT.Identity, bias=v("dw_b", l, m)).then_inc(*E.read("conv_s", l, m))
                act.wait_ge(*drained("cln", l, 0))
                a(conv_b, cvT, ACT.Square).then_inc(*E.up("conv_sq", l))
                act.wait_ge(*filled("cln", l, 1))
                a(conv_b[:, 0, :], bank("cln", l, 1)[:, 0:T], ACT.Sqrt, bias=eps[1e-5], scale=1.0 / CC).then_inc(*E.read("cln", l, 1))
                act.wait_ge(*at("conv_affine", l))
                a(conv_b, cvT, ACT.Sigmoid).then_inc(*E.up("conv_sig", l))

                for d in range(2):
                    if d == 1:
                        lowrank(1)
                        exps(1)
                    for cp in range(NCP):
                        for i in range(3 if d == 0 else 2):
                            act.wait_ge(*filled("tok", l, d, cp, i))
                            dst = tok[:, i, cp, :] if i < 2 else vtok[:, cp, :]
                            a(dst, bank("tok", l, d, cp, i)[:, :], ACT.Copy).then_inc(*E.read("tok", l, d, cp, i))
                    for lev in range(LEVELS):
                        for u in range(6):
                            act.wait_ge(*filled("X", l, d, lev, u))
                            g = lev * 6 + u
                            if g >= 3:
                                pl, pu = divmod(g - 3, 6)
                                act.wait_ge(*filled("TAT", l, d, pl, pu))
                            a(Xs[u % 3], bank("X", l, d, lev, u)[:, 0:256], ACT.Copy).then_inc(*E.read("X", l, d, lev, u))
                    act.wait_ge(*filled("s0", l, d))
                    act.wait_ge(*filled("TAT", l, d, LEVELS - 1, 5))
                    c0 = starts(d)[1]
                    for hh in range(2):
                        r = slice(64 * hh, 64 * hh + 64)
                        ins = a(St[r, c0, :, r], bank("s0", l, d)[r, 0:256].rearrange("p (m v) -> p m v", m=NM), ACT.Copy)
                    ins.then_inc(*E.read("s0", l, d))
                    if d == 1 and l + 1 < DEPTH:
                        load_state(l + 1)
                    for n, c in enumerate(order(d)):
                        q = slice(64 * (c % 2), 64 * (c % 2) + 64)
                        act.wait_ge(*filled("W", l, d, c))
                        if n >= 2:
                            act.wait_ge(*filled("U", l, d, order(d)[n - 2]))
                        a(Wb[n % 2][q, :], bank("W", l, d, c)[q, :], ACT.Copy).then_inc(*E.read("W", l, d, c))
                    if d == 0:
                        for cp in range(NCP):
                            act.wait_ge(*filled("Y", l, d, cp))
                            a(Y[:, cp, :], bank("Y", l, d, cp)[:, :], ACT.Copy).then_inc(*E.read("Y", l, d, cp))
                    act.wait_ge(*filled("sf", l, d))
                    if (l, d) != (0, 0):
                        act.wait_ge(*at("out_stored", "state", *((l, 0) if d else (l - 1, 1))))
                    so = sout[0:64, :]
                    a(so, bank("sf", l, d)[0:64, :], ACT.Copy).then_inc(*E.read("sf", l, d))
                    act.wait_ge(*E.latest())
                    act.dma_start(new_state[0, l, d].rearrange("h v k -> v h k"), so.rearrange("p (h k) -> p h k", h=NH)).then_inc(*E.up("out_stored", "state", l, d, by=16))
                act.wait_ge(*at("Y_centred", l))
                a(tmp4[0].rearrange("p (c w) -> p c w", c=NCP), Y, ACT.Square).then_inc(*E.up("Ysq_ready", l))
                act.wait_ge(*at("Yvar_ready", l))
                a(stat[:, 24:48], stat[:, 0:24], ACT.Sqrt, bias=eps[64e-5], scale=1.0 / HD).then_inc(*E.up("Ystd_ready", l))
                for b_ in range(3):
                    for m in range(KD):
                        act.wait_ge(*filled("gate", l, b_, m))
                        i = b_ * KD + m
                        if i >= 16:
                            act.wait_ge(*at("gated", l, *divmod(i - 8, KD)))
                        elif i >= 8:
                            act.wait_ge(*drained("br", l, 0, m))
                        a(gsig(i), bank("gate", l, b_, m)[:, 0:T], ACT.Sigmoid).then_inc(*E.read("gate", l, b_, m))
                squares(l, 1)
                root(l, 1)
                modulate(l, 1)
                if l % 2 == 0:
                    for m in range(KF):
                        act.wait_ge(*filled("fg", l, m))
                        if m >= 3:
                            act.wait_ge(*drained("fu", l, m - 3))
                        a(fsig[m % 3], bank("fg", l, m)[:, 0:T], ACT.Sigmoid).then_inc(*E.up("fsig_ready", l, m))
            act.dma_start(wrt, dram["w_router"][0].rearrange("(k p) e -> p k e", p=P)).then_inc(*E.up("router_in", by=16))
            act.dma_start(brt[0:1, :], dram["b_router"]).then_inc(*E.up("router_in", by=16))
            act.wait_ge(*at("chosen_ready"))
            for i in range(2):
                a(rt[:, R_P + 3 * i:R_P + 3 * i + 3], rt[:, R_D:R_D + 3], ACT.Sigmoid, scale=1.0 if i == 0 else -1.0).then_inc(*E.up("weights_ready", i))
            for k in range(6):
                act.wait_ge(*filled("htok", k))
                flatk = htok.rearrange("p j d -> p (j d)")[:, k * 512:(k + 1) * 512]
                a(flatk, bank("htok", k)[:, :], ACT.Copy).then_inc(*E.read("htok", k))
            s = lambda name: sem(name).h
            act.wait_ge(*at("jobs_ready"))
            act.sem_inc(s("e_hG"), 2)
            act.sem_inc(s("e_ydrained"), 2)
            njobs = act.value_load(rt_i[0:1, 0:1], min_val=NE, max_val=NJOB)
            with act.Fori(0, njobs) as i:
                act.wait_ge(s("e_selT_full"), i + 1)
                act.wait_ge(s("e_sc"), i * 6 + 6)
                a(selT, psum[4][:, 0:3 * P].rearrange("p (j s) -> p j s", j=3), ACT.Copy).then_inc(s("e_selT"), 1)
                for h in range(2):
                    act.wait_ge(s("e_gather"), i * 2 + h + 1)
                    a(hG[:, 4 * h:4 * h + 4, :], psum[6 + h][:, :].rearrange("p (k s) -> p k s", k=4), ACT.Copy)\
                        .then_inc(s("e_hG"), 1)
                for c, (c0, n) in enumerate(CHUNKS):
                    act.wait_ge(s("e_gu"), i * 3 + c + 1)
                    act.wait_ge(s("e_prod"), i * 3 + 3 + c)
                    a(esig[:, 0:n], psum[2 * (c % 2)][:, 0:n], ACT.Sigmoid).then_inc(s("e_sig"), 1)
                    if c > 0:
                        e_copy(act, a, s, psum, eprodT, i, c - 1)
                e_copy(act, a, s, psum, eprodT, i, 2)
                act.wait_ge(s("e_y"), i + 1)
                for half in range(2):
                    a(ey[:, half * 512:(half + 1) * 512], psum[4 + half][:, :], ACT.Copy).then_inc(s("e_ydrained"), 1)
            squares(DEPTH, 0)
            root(DEPTH, 0)
            for j in range(3):
                for half in range(2):
                    act.wait_ge(*filled("yo", j, half))
                    a(htok[:, j, half * 512:(half + 1) * 512], bank("yo", j, half)[:, :], ACT.Copy).then_inc(*E.read("yo", j, half))
                act.wait_ge(*E.latest())
                dst = yp[0] if j == 0 else ys[0][(j - 1) * P:j * P, :]
                act.dma_start(dst, htok[:, j, :]).then_inc(*E.up("out_stored", "y", j, by=16))

        @block.vector
        def _(dve):
            E = Counts("dve_step")
            tt, ts, stt = dve.tensor_tensor, dve.tensor_scalar, dve.scalar_tensor_tensor
            M, A, SUB = ALU.mult, ALU.add, ALU.subtract

            for i in range(2):
                dve.wait_ge(*at("cond_sig", i))
            tt(cond, cond, condx, M).then_inc(*E.up("cond_ready"))

            def normed(l, which, scale=None):
                dve.wait_ge(*drained("norm", l, which))
                dve.reciprocal(rs, rs).then_inc(*E.step())
                dve.wait_ge(*E.latest())
                dst = hT if scale is None else sq
                if scale is None:
                    for i in range(2):
                        tt(hT[:, 4 * i:4 * i + 4, :], xT[:, 4 * i:4 * i + 4, :],
                                 rs.rearrange("p (a t) -> p a t", a=1).broadcast_to([P, 4, T]), M).then_inc(*E.up("xn_ready", l, which, i))
                else:
                    for k in range(KD):
                        ins = stt(sq[:, k, :], xT[:, k, :], scale(k), rs, M, M)
                        if k < KD - 1:
                            ins.then_inc(*E.step())
                        else:
                            ins.then_inc(*E.up("h_ready", l))

            def residual(job, l, gate, which):
                for m in range(KD):
                    src = bank(*job(m)) if job(m)[0] != "fdown" else psum[m]
                    if job(m)[0] == "fdown":
                        dve.wait_ge(*at("block_used", "fd", l, KF // 2 - 1))
                    else:
                        dve.wait_ge(*filled(*job(m)))
                    for s_, (t0, t1) in enumerate(SEG):
                        ins = stt(xT[:, m, t0:t1], src[:, t0:t1], mod[:, gate + m, s_:s_ + 1], xT[:, m, t0:t1], M, A)
                        if s_ == 0:
                            ins.then_inc(*E.step())
                    if job(m)[0] == "fdown":
                        if m < 4:
                            ins.then_inc(sem(f"bank_free{m}").h, 1)
                        else:
                            ins.then_inc(*E.up("fdown_done", l))
                    else:
                        ins.then_inc(*E.read(*job(m)))

            dve.memset(St, 0.0).then_inc(*E.step())
            for l in range(DEPTH):
                dve.wait_ge(*at("block_used", "ada", l, 23))
                adab = bank("ada", l)[:, 0:96].rearrange("p (m s) -> p m s", s=2)
                ba = v("b_ada", l, 0, 48)
                dve.wait_ge(*E.latest())
                for s_ in range(2):
                    ins = tt(mod[:, :, s_], adab[:, :, s_], ba, A)
                    if s_ == 0:
                        ins.then_inc(*E.step())
                    else:
                        ins.then_inc(*E.read("ada", l))
                dve.wait_ge(*E.latest())
                for which, name in ((0, "norm1"), (1, "norm2")):
                    for s_ in range(2):
                        stt(modA[:, which, :, s_], mod[:, 24 * which + 8:24 * which + 16, s_], 1.0,
                                  v(name, l, 0, 8), A, M).then_inc(*E.up("modA_ready", l))
                mu = v("shift_mu", l, 0, NZ)
                ts(mix[:, 0, 0:NZ], mu, -1.0, 1.0, M, A).then_inc(*E.step())
                ts(mix[:, 1, 0:NZ], mu, 0.5, None, M).then_inc(*E.step())
                ts(oneka, v("k_a", l, 0, 4), -1.0, 1.0, M, A).then_inc(*E.step())
                normed(l, 0)
                for g in range(3):
                    full_z = 5 * g + 4
                    dve.wait_ge(*drained('z', l, full_z))
                    for m in range(5 * g, 5 * g + 4):
                        dve.wait_ge(*drained('z', l, m))
                    gs = slice(5 * g, 5 * g + 5)
                    zz, sh = z[:, gs, :], shifted[:, gs, :]
                    tt(sh[:, :, 1:T - 1], zz[:, :, 0:T - 2], zz[:, :, 2:T], A).then_inc(*E.step())
                    dve.wait_ge(*E.latest())
                    dve.tensor_copy(sh[:, :, TP - 1:TP + 1], zz[:, :, TP - 2:TP + 2:3]).then_inc(*E.step())
                    dve.tensor_copy(sh[:, :, 0:T:T - 1], zz[:, :, 1:T - 1:T - 3]).then_inc(*E.step())
                    dve.wait_ge(*E.latest())
                    for m in range(5 * g, 5 * g + 5):
                        ts(z[:, m, :], z[:, m, :], mix[:, 0, m:m + 1], None, M).then_inc(*E.step())
                    dve.wait_ge(*E.latest())
                    for m in range(5 * g, 5 * g + 5):
                        ins = stt(z[:, m, :], shifted[:, m, :], mix[:, 1, m:m + 1], z[:, m, :], M, A)
                        ins.then_inc(*E.up("mix_done", l)) if m == NZ - 1 else ins.then_inc(*E.step())
                dve.wait_ge(*E.latest())
                r_, k_, v_ = z[:, 0:4, :], z[:, 4:8, :], z[:, 8:12, :]
                for m in range(NM):
                    ins = ts(kk[:, m, :], z[:, 4 + m, :], v("k_k", l, m), None, M)
                    ins.then_inc(*E.up("kkp_ready", l)) if m == 3 else ins.then_inc(*E.step())
                dve.wait_ge(*E.latest())
                dve.wait_ge(*at("second_in"))
                for m in range(4):
                    dve.wait_ge(*drained("cf", l, m))
                dve.memset(glu, 0.0).then_inc(*E.step())
                dve.wait_ge(*E.latest())
                for m in range(2):
                    tt(glu[:, m, 15:15 + TP], cvT[:, m, 0:TP], conv_b[:, m, 0:TP], M).then_inc(*E.step())
                    tt(glu[:, m, TP + 30:].rearrange("p (r t) -> p r t", r=4)[:, :, 15:15 + GRID],
                             cvT[:, m, TP:T].rearrange("p (r t) -> p r t", r=4),
                             conv_b[:, m, TP:T].rearrange("p (r t) -> p r t", r=4), M).then_inc(*E.up("glu_ready", l))
                for m in range(NM):
                    dve.wait_ge(*drained('kks', l, m))
                nrm = tmp4[0]
                ts(nrm, nrm, 1e-12, None, ALU.max).then_inc(*E.step()); dve.wait_ge(*E.latest())
                dve.reciprocal(nrm, nrm).then_inc(*E.step()); dve.wait_ge(*E.latest())
                tt(kk, kk, nrm.rearrange("p (m t) -> p m t", m=NM), M).then_inc(*E.up("kk_ready", l))
                for j in range(NCP):
                    dve.wait_ge(*filled("fno1", l, j))
                    dve.tensor_copy(fno_z[:, j, :, :], bank("fno1", l, j)[:, :].rearrange("p (m w) -> p m w", m=2)).then_inc(*E.read("fno1", l, j))

                def prep(d):
                    sg, ag, F3 = tmp4[0], tmp4[1], tmp4[3]
                    for m in range(NM):
                        dve.wait_ge(*drained('low', l, d, 0, m))
                    for m in range(NM):
                        o_ = slice(m * T, (m + 1) * T)
                        dve.tensor_tensor_scan(tmp4[2][:, o_], tab("reset"), sg[:, o_], 0.0, M, A).then_inc(*E.step())
                    dve.wait_ge(*E.latest())
                    cs = tmp4[2]
                    if d == 1:
                        tt(F3, sg, cs, SUB).then_inc(*E.step()); dve.wait_ge(*E.latest())
                        tot = cs.rearrange("p (m c t) -> p m c t", m=NM, c=NC_)
                        for m in range(NM):
                            tt(F3.rearrange("p (m c t) -> p m c t", m=NM, c=NC_)[:, m],
                                      F3.rearrange("p (m c t) -> p m c t", m=NM, c=NC_)[:, m],
                                      tot[:, m, :, C - 1:C].broadcast_to([P, NC_, C]), A).then_inc(*E.step())
                        dve.wait_ge(*E.latest())
                    L = tmp4[L3(d)]
                    tt(sg, L, sg, SUB).then_inc(*E.up("L_ready", l, d))
                    ar = AR.rearrange("p m c k t -> p k m c t")
                    v4 = lambda x: x.rearrange("p (m c t) -> p m c t", m=NM, c=NC_)
                    v3 = lambda x: x.rearrange("p (m t) -> p m t", m=NM)
                    kk4 = kk.rearrange("p m (c t) -> p m c t", c=NC_)
                    for m in range(NM):
                        dve.wait_ge(*drained('low', l, d, 1, m))
                    tt(BK[:, 0], kk, v3(ag), M).then_inc(*E.step())
                    for m in range(NM):
                        ts(BK[:, 1, m, :], v3(ag)[:, m, :], v("k_a", l, m), oneka[:, m:m + 1], M, A).then_inc(*E.step())
                    dve.wait_ge(*E.latest())
                    tt(BK[:, 1], BK[:, 1], k_, M).then_inc(*E.step())
                    dve.wait_ge(*at("E1_ready", l, d))
                    for m in range(NM):
                        stt(ar[:, 0, m], kk4[:, m], -1.0, v4(sg)[:, m], M, M).then_inc(*E.step())
                    dve.wait_ge(*at("E2_ready", l, d))
                    for m in range(NM):
                        tt(ar[:, 1, m], r_[:, m, :].rearrange("p (c t) -> p c t", c=NC_), v4(tmp4[other(d)])[:, m], M).then_inc(*E.step())
                    dve.wait_ge(*at("E3_ready", l, d))
                    dve.wait_ge(*E.latest())
                    tt(BK[:, 0], BK[:, 0], v3(L), M).then_inc(*E.step())
                    tt(BK[:, 1], BK[:, 1], v3(L), M).then_inc(*E.up("ark_ready", l, d))

                prep(0)
                dve.wait_ge(*filled("cln", l, 0))
                for m in range(2):
                    ins = stt(cvT[:, m, :], bank("cln", l, 0)[:, 0:T], -1.0 / CC, cvT[:, m, :], M, A)
                    if m == 0:
                        ins.then_inc(*E.step())
                    else:
                        ins.then_inc(*E.read("cln", l, 0))
                dve.wait_ge(*drained('cln', l, 1))
                dve.reciprocal(conv_b[:, 0, :], conv_b[:, 0, :]).then_inc(*E.step()); dve.wait_ge(*E.latest())
                for m in range(2):
                    tt(cvT[:, m, :], cvT[:, m, :], conv_b[:, 0, :], M).then_inc(*E.step())
                dve.wait_ge(*E.latest())
                for m in range(2):
                    ts(cvT[:, m, :], cvT[:, m, :], v("conv_ln_g", l, m), v("conv_ln_b", l, m), M, A).then_inc(*E.up("conv_affine", l))
                dve.wait_ge(*at("conv_sig", l))
                tt(cvT, cvT, conv_b, M).then_inc(*E.up("cv_ready", l))

                for d in range(2):
                    if d == 1:
                        dve.wait_ge(*filled("Y", l, 0, NCP - 1))
                        prep(1)
                    for cp in range(NCP):
                        for hp in range(NH // 2):
                            dve.wait_ge(*filled("pair", l, d, cp, hp))
                            src = bank("pair", l, d, cp, hp)[:, :].rearrange("p (h w) -> p h w", h=2)
                            msk = pair_mask[:, d:d + 1, :].broadcast_to([P, 2, 256])
                            h0 = 4 * (hp // 2) + hp % 2
                            tt(S1[:, cp, h0:h0 + 3:2, :], src, msk, M).then_inc(*E.read("pair", l, d, cp, hp))
                    for u in range(6):
                        cp, g = divmod(u, 2)
                        dve.tensor_copy(TQ[:, cp, 4 * g:4 * g + 4, :],
                                              tab("eye2").rearrange("p (a w) -> p a w", a=1).broadcast_to([P, 4, P])).then_inc(*E.up("TQ_ready", l, d, u))
                    for lev in range(LEVELS):
                        for u in range(6):
                            cp, g = divmod(u, 2)
                            dve.wait_ge(*filled("TAT", l, d, lev, u))
                            msk = level_mask[:, lev:lev + 1, 64 * d:64 * d + P].bitcast(I32)
                            for h in range(4):
                                ins = dve.copy_predicated(TQ[:, cp, 4 * g + h, :], msk[:, 0, :],
                                                          bank("TAT", l, d, lev, u)[:, h * P:(h + 1) * P])
                                if h < 3:
                                    ins.then_inc(*E.step())
                            ins.then_inc(*E.read("TAT", l, d, lev, u))
                    c0 = starts(d)[0]
                    dve.memset(St[:, c0, :, :], 0.0).then_inc(*E.up("S_ready", l, d, c0))
                    for c in order(d):
                        cp, par = divmod(c, 2)
                        q = slice(64 * par, 64 * par + 64)
                        dve.wait_ge(*filled("U", l, d, c))
                        dve.tensor_copy(U[q, cp, :, :], bank("U", l, d, c)[q, :].rearrange("p (h v) -> p h v", h=NH)).then_inc(*E.read("U", l, d, c))
                        n = nxt(d, c)
                        if n is None:
                            continue
                        dve.wait_ge(*filled("S", l, d, c))
                        dst = lambda r: Sfin[r, :, :] if n == "end" else St[r, n, :, r]
                        if n == "end" and (l, d) != (0, 0):
                            dve.wait_ge(*filled("sf", *((l, 0) if d else (l - 1, 1))))
                        for r in (slice(0, 64), slice(64, P)):
                            ins = tt(dst(r), bank("S", l, d, c)[r, 0:256].rearrange("p (m v) -> p m v", m=NM), St[r, c, :, r], A)
                        ins.then_inc(*E.read("S", l, d, c))
                        dve.wait_ge(*E.latest())
                        for r in (slice(0, 64), slice(64, P)):
                            ins = tt(dst(r), dst(r), pc[r, :, c:c + 1].broadcast_to([64, NM, HD]), M)
                        if n == "end":
                            ins.then_inc(*E.up("Sfin_ready", l, d))
                        else:
                            ins.then_inc(*E.up("S_ready", l, d, n))
                    if d == 1:
                        for cp in range(NCP):
                            dve.wait_ge(*filled("Y", l, d, cp))
                            if cp == 0:
                                for i in range(NCP):
                                    dve.wait_ge(*drained('Y', l, 0, i))
                            tt(Y[:, cp, :], Y[:, cp, :], bank("Y", l, d, cp)[:, :], A).then_inc(*E.read("Y", l, d, cp))
                        dve.wait_ge(*E.latest())
                Yh = Y.rearrange("p c (h v) -> p (c h) v", v=HD)
                dve.tensor_reduce(stat[:, 0:24], Yh, AX.X, A).then_inc(*E.step()); dve.wait_ge(*E.latest())
                ts(stat[:, 0:24], stat[:, 0:24], 1.0 / HD, None, M).then_inc(*E.step()); dve.wait_ge(*E.latest())
                tt(Yh, Yh, stat[:, 0:24].rearrange("p (a b) -> p a b", b=1).broadcast_to([P, 24, HD]), SUB).then_inc(*E.up("Y_centred", l))
                dve.wait_ge(*at("Ysq_ready", l))
                dve.wait_ge(*E.latest())
                dve.tensor_reduce(stat[:, 0:24], tmp4[0].rearrange("p (n v) -> p n v", v=HD), AX.X, A).then_inc(*E.up("Yvar_ready", l))
                dve.wait_ge(*at("Ystd_ready", l))
                dve.reciprocal(stat[:, 24:48], stat[:, 24:48]).then_inc(*E.step()); dve.wait_ge(*E.latest())
                tt(Yh, Yh, stat[:, 24:48].rearrange("p (a b) -> p a b", b=1).broadcast_to([P, 24, HD]), M).then_inc(*E.up("yn_ready", l))
                for m in range(NM):
                    o_ = tmp4[1][:, m * T:(m + 1) * T]
                    ins = stt(o_, z[:, m, :], v("r_k", l, m), z[:, 4 + m, :], M, M)
                    ins.then_inc(*E.up("rk_ready", l)) if m == 3 else ins.then_inc(*E.step())
                for cp in range(NCP):
                    dve.wait_ge(*filled("yt", l, cp))
                    for m in range(NM):
                        ins = ts(yT[:, m, cp * P:(cp + 1) * P], bank("yt", l, cp)[:, m * P:(m + 1) * P],
                                 v("gn_g", l, m), v("gn_b", l, m), M, A)
                        if m < 3:
                            ins.then_inc(*E.step())
                    ins.then_inc(*E.read("yt", l, cp))
                for m in range(NM):
                    dve.wait_ge(*filled("bon", l, m))
                    tt(tmp4[2][:, m * T:(m + 1) * T], bank("bon", l, m)[:, 0:T], z[:, 8 + m, :], M).then_inc(*E.read("bon", l, m))
                dve.wait_ge(*E.latest())
                tt(yT, yT, tmp4[2].rearrange("p (m t) -> p m t", m=NM), A).then_inc(*E.step()); dve.wait_ge(*E.latest())
                for m in range(NM):
                    dve.wait_ge(*filled("gup", l, m))
                    tt(yT[:, m, :], yT[:, m, :], bank("gup", l, m)[:, 0:T], M).then_inc(*E.read("gup", l, m))
                for b_ in range(3):
                    for m in range(KD):
                        dve.wait_ge(*filled("br", l, b_, m))
                        dve.wait_ge(*drained('gate', l, b_, m))
                        g = gsig(b_ * KD + m)
                        dst = merged[:, m, :] if b_ == 0 else g
                        tt(dst, g, bank("br", l, b_, m)[:, 0:T], M).then_inc(*E.read("br", l, b_, m))
                        if b_ > 0:
                            dve.wait_ge(*E.latest())
                            tt(merged[:, m, :], merged[:, m, :], g, A).then_inc(*E.up("gated", l, b_, m))
                residual(lambda m: ("o", l, m), l, 16, 1)
                normed(l, 1)
                if l % 2 == 0:
                    for m in range(KF):
                        dve.wait_ge(*at("fsig_ready", l, m))
                        dve.wait_ge(*filled("fg", l, m))
                        tt(fsig[m % 3], fsig[m % 3], bank("fg", l, m)[:, 0:T], M).then_inc(*E.read("fg", l, m))
                        dve.wait_ge(*E.latest())
                        dve.wait_ge(*filled("fu", l, m))
                        tt(prod[:, m, :], fsig[m % 3], bank("fu", l, m)[:, 0:T], M).then_inc(*E.read("fu", l, m))
                    residual(lambda m: ("fdown", l, m), l, 40, 2)
            dve.wait_ge(*filled("logit"))
            lg = rt[:, R_LG:R_LG + 24]
            dve.tensor_copy(lg, bank("logit")[:, 0:24]).then_inc(*E.read("logit")); dve.wait_ge(*E.latest())
            for j in range(3):
                dve.max(rt[:, R_MX + 8 * j:R_MX + 8 * j + 8], lg[:, 8 * j:8 * j + 8]).then_inc(*E.step())
            dve.wait_ge(*E.latest())
            for j in range(3):
                dve.max_index(rt[:, R_IX + 8 * j:R_IX + 8 * j + 8].bitcast(U32), rt[:, R_MX + 8 * j:R_MX + 8 * j + 8],
                                     lg[:, 8 * j:8 * j + 8]).then_inc(*E.step())
            mx = rt[:, R_MX:R_MX + 24].rearrange("p (j e) -> p j e", j=3)
            tt(rt[:, R_D:R_D + 3], mx[:, :, 0], mx[:, :, 1], SUB).then_inc(*E.step())
            dve.wait_ge(*E.latest())
            dve.tensor_copy(rt[:, R_IF:R_IF + 24], rt[:, R_IX:R_IX + 24].bitcast(U32)).then_inc(*E.step()); dve.wait_ge(*E.latest())
            code8 = tab("code")[:, 0:NE]
            for j in range(3):
                for i in range(2):
                    ts(rt[:, R_OH + 24 * i + 8 * j:R_OH + 24 * i + 8 * j + 8], code8,
                              rt[:, R_IF + 8 * j + i:R_IF + 8 * j + i + 1], None, ALU.is_equal).then_inc(*E.step())
            dve.wait_ge(*E.latest())
            tt(rt[:, 0:24], rt[:, R_OH:R_OH + 24], rt[:, R_OH + 24:R_OH + 48], A).then_inc(*E.up("chosen_ready"))
            for i in range(2):
                dve.wait_ge(*at("weights_ready", i))
            for j in range(3):
                o_ = rt[:, R_OH + 8 * j:R_OH + 8 * j + 8]
                ts(o_, o_, rt[:, R_P + j:R_P + j + 1], None, M).then_inc(*E.step())
            dve.wait_ge(*E.latest())
            for j in range(3):
                for t in range(3):
                    stt(rt[:, R_CW + 24 * j + 8 * t:R_CW + 24 * j + 8 * t + 8],
                               rt[:, R_OH + 24 + 8 * j:R_OH + 24 + 8 * j + 8], rt[:, R_P + 3 + j:R_P + 4 + j],
                               rt[:, R_OH + 8 * j:R_OH + 8 * j + 8], M, A).then_inc(*E.step())
            dve.wait_ge(*filled("rank"))
            rk = rt[:, R_RK:R_RK + 24]
            stt(rk, bank("rank")[:, 0:24], 1.0, rt[:, 0:24], A, M).then_inc(*E.step())
            cnt = rt[:, R_CNT:R_CNT + 8]
            dve.tensor_copy(cnt, bank("rank")[:, 24:32]).then_inc(*E.read("rank")); dve.wait_ge(*E.latest())
            for j in range(3):
                for t in range(3):
                    ts(rt[:, R_SL + 24 * j + 8 * t:R_SL + 24 * j + 8 * t + 8], rk[:, 8 * j:8 * j + 8],
                              -1.0 - P * t, None, A).then_inc(*E.step())
            fl = rt[:, R_FL:R_FL + 16]
            for t in range(2):
                ts(fl[:, 8 * t:8 * t + 8], cnt, float(P * (t + 1)), None, ALU.is_gt).then_inc(*E.step())
            dve.wait_ge(*E.latest())
            dve.tensor_tensor_scan(rt[:, R_PS:R_PS + 16], ones[:, 0:16], fl, 0.0, M, A).then_inc(*E.step()); dve.wait_ge(*E.latest())
            tt(rt[:, R_PS:R_PS + 16], rt[:, R_PS:R_PS + 16], fl, M).then_inc(*E.step())
            jl = rt[:, R_JL:R_JL + 17]
            dve.wait_ge(*E.latest())
            dve.tensor_reduce(jl[:, 0:1], rt[:, R_PS:R_PS + 16], AX.X, ALU.max).then_inc(*E.step()); dve.wait_ge(*E.latest())
            ts(jl[:, 0:1], jl[:, 0:1], float(NE), None, A).then_inc(*E.step())
            dve.tensor_copy(jl[:, 1:9], code8).then_inc(*E.step())
            for q in range(8):
                o_ = rt[:, R_TM + 16 * q:R_TM + 16 * q + 16]
                stt(o_, rt[:, R_PS:R_PS + 16], float(q + 1), tab("code")[:, 8:24], ALU.is_equal, M).then_inc(*E.step())
            dve.wait_ge(*E.latest())
            dve.tensor_reduce(jl[:, 9:17], rt[:, R_TM:R_TM + 128].rearrange("p (q i) -> p q i", q=8), AX.X, A).then_inc(*E.step()); dve.wait_ge(*E.latest())
            t1 = rt[:, R_TM:R_TM + 17]
            ts(t1, jl, float(NE), -float(NE), ALU.is_ge, M).then_inc(*E.step())
            ts(rt[:, R_TM + 32:R_TM + 49], jl, float(2 * NE), -float(NE), ALU.is_ge, M).then_inc(*E.step()); dve.wait_ge(*E.latest())
            tt(t1, t1, rt[:, R_TM + 32:R_TM + 49], A).then_inc(*E.step()); dve.wait_ge(*E.latest())
            tt(t1, t1, jl, A).then_inc(*E.step()); dve.wait_ge(*E.latest())
            dve.tensor_copy(rt_i[:, 1:17], t1[:, 1:17]).then_inc(*E.step())
            dve.tensor_copy(rt_i[:, 0:1], jl[:, 0:1]).then_inc(*E.step())
            dve.tensor_copy(rt_i[:, 17:34], jl).then_inc(*E.up("jobs_ready"))
            for k in range(6):
                dve.wait_ge(*drained('htok', k))
            s = lambda name: sem(name).h
            dve.memset(yacc, 0.0).then_inc(*E.step())
            dve.wait_ge(*E.latest())
            dve.sem_inc(s("e_prod"), 3)
            dve.sem_inc(s("e_sc_done"), 6)
            njobs = dve.value_load(rt_i[0:1, 0:1], min_val=NE, max_val=NJOB)
            with dve.Fori(0, njobs) as i:
                code = dve.value_load(rt_i[0:1, bass.ds(i + 18, 1)], min_val=0, max_val=NCODE - 1)
                dve.wait_ge(s("e_hG"), i * 2 + 2)
                for j in range(3):
                    slot = rt[:, bass.ds(code + (R_SL + 24 * j), 1)]
                    w = rt[:, bass.ds(code + (R_CW + 24 * j), 1)]
                    ts(sel[:, j, :], iota, slot, None, ALU.is_equal)
                    ins = ts(selc[:, j, :], iota, slot, w, ALU.is_equal, M)
                ins.then_inc(s("e_sel"), 1)
                for c, (c0, n) in enumerate(CHUNKS):
                    dve.wait_ge(s("e_sig"), i * 3 + c + 1)
                    if c == 0:
                        dve.wait_ge(s("e_sc"), i * 6 + 6)
                    tt(esig[:, 0:n], esig[:, 0:n], psum[2 * (c % 2)][:, 0:n], M).then_inc(s("e_silu"), 1)
                    dve.wait_ge(s("e_silu"), i * 3 + c + 1)
                    tt(eprod[:, c0:c0 + n], esig[:, 0:n], psum[2 * (c % 2) + 1][:, 0:n], M).then_inc(s("e_prod"), 1)
                for n_ in range(6):
                    j, half = divmod(n_, 2)
                    dve.wait_ge(s("e_sc"), i * 6 + 6 + n_ + 1)
                    if n_ == 0:
                        dve.wait_ge(s("e_sc_done"), i * 6 + 6)
                    dst = yacc[:, j, half * 512:(half + 1) * 512]
                    tt(dst, dst, psum[6 + half][:, :], A).then_inc(s("e_sc_done"), 1)
            dve.tensor_copy(stat[:, 84:85], ident[:, 0:1]).then_inc(*E.up("yacc_ready"))
            residual(lambda m: ("ey", m), 1, 40, 2)
            normed(DEPTH, 0, lambda k: v("final_norm", 0, k))

        @block.gpsimd
        def _(pool):
            E = Counts("pool_step")
            for l in range(DEPTH):
                if l == 0:
                    pool.wait_ge(*drained('vec'))
                pool.wait_ge(*at("mix_done", l))
                for i in range(2 * CONV_W):
                    m, j = divmod(i, CONV_W)
                    if i >= 8 and (i - 8) % CONV_W == CONV_W - 1:
                        pool.wait_ge(*filled("conv_s", l, (i - 8) // CONV_W))
                    elif i >= 8:
                        pool.wait_ge(*at("diag_used", l, i - 8))
                    pool.tensor_scalar(diag[i % 8], ident, v("dw_w", l, 2 * j + m), None, ALU.mult).then_inc(*E.up("diag_ready", l, i))


_INS = ["x_prompt", "x_sample", "state_rwkv", "c", "c_ctx", "norm1", "norm2", "w_ada", "b_ada", "w_in",
        "dw_w", "dw_b", "conv_ln_g", "conv_ln_b", "w_conv_out", "w_fno_out", "shift_mu", "g_up",
        "dec_w0", "dec_up", "iclr_a0", "iclr_up", "k_k", "k_a", "r_k", "gn_g", "gn_b", "w_rwkv_out", "w_o",
        "ffn_w_gate", "ffn_w_up", "ffn_w_down", "w_router", "b_router",
        "moe_w_gate", "moe_w_up", "moe_w_down", "final_norm"]
_OUTS = [(1, TP, DM), (1, TS, DM), (1, DEPTH, 2, NH, HD, HD)]


def kernel(**inputs):
    import concourse.bacc as bacc
    from concourse.bass_utils import run_bass_kernel_spmd as run

    arrays = {n: np.ascontiguousarray(inputs[n]) for n in _INS}
    arrays["tables"] = np.concatenate(list(tables().values()), 1)
    marks = {}
    for _ in range(2):
        nc = bacc.Bacc("TRN2", target_bir_lowering=False, num_devices=1)
        dram = {n: nc.dram_tensor(f"in_{n}", a.shape, F32, kind="ExternalInput").ap() for n, a in arrays.items()}
        outs = [nc.dram_tensor(f"out_{i}", s, F32, kind="ExternalOutput").ap() for i, s in enumerate(_OUTS)]
        build(nc, dram, outs, marks)
    r = run(nc, [{f"in_{n}": a for n, a in arrays.items()}], core_ids=[0])
    return tuple(r.results[0][f"out_{i}"] for i in range(len(_OUTS)))
```

```python
from contextlib import ExitStack

import numpy as np
import concourse.bass as bass
from concourse import mybir

P = 128
DM, DEPTH = 1024, 2
TP, TS = 128, 256
T = TP + TS
SEG = ((0, TP), (TP, T))
KD = DM // P
GRID, CONV_W = 64, 31
CC, CF, CR = 256, 256, 512
HD, NH = 64, 8
NM = CR // P
C = 64
NC_ = T // C
NCP = T // P
B = C // 2
LEVELS = 5
NZ = 15
OFF_Z, OFF_G = 768, 2688
DFF, KF = 2816, 22
NE, DE, KE = 8, 1408, 11
CHUNKS = ((0, 512), (512, 512), (1024, 384))
DOWN = ((0, 4), (4, 4), (8, 3))
NCODE = 3 * NE
NJOB = 16
DECAY = float(np.exp(-0.5))

F32 = mybir.dt.float32
F32R = mybir.dt.float32r
I32 = mybir.dt.int32
U32 = mybir.dt.uint32
ALU = mybir.AluOpType
ACT = mybir.ActivationFunctionType
AX = mybir.AxisListType


def tables():
    i = np.arange(P)
    out = {}
    out["ident"] = np.eye(P)
    out["ones"] = np.ones((P, P))
    out["before"] = (i[:, None] < i[None, :]) * 1.0
    out["iota"] = np.tile(np.arange(P), (P, 1))
    out["code"] = np.tile(np.arange(24), (P, 1))
    out["eps"] = np.tile(np.array([1e-6, 1e-5, 64e-5, 0.0]), (P, 1))
    out["heads"] = (i[:, None] // HD == i[None, :] // HD) * 1.0
    c = np.arange(HD)
    ang = 2 * np.pi * (np.outer(c, c) % HD) / HD
    for name, m in (("dft_c", np.cos(ang)), ("dft_s", np.sin(ang))):
        out[name] = np.kron(np.eye(2), m)
    for name, n in (("p", TP), ("s", TS)):
        t = np.arange(n)
        ang = 2 * np.pi * (np.outer(t, t) % n) / n
        scale = 1.0 / np.sqrt(n * HD)
        both = np.stack([np.cos(ang), -np.sin(ang)]) * scale
        out["time_" + name] = both.reshape(2, n // P, P, n).transpose(2, 1, 0, 3).reshape(P, -1)
    s, t = np.arange(C)[:, None], np.arange(C)[None, :]
    both = []
    for strict in (s < t, s > t):
        incl = strict | (s == t)
        both.append(np.concatenate([strict, incl, strict, incl], 1))
    out["pair_mask"] = np.tile(np.concatenate(both, 1), (2, 1))
    lev = []
    s, t = s[:B], t[:, :B]
    for m in range(LEVELS):
        b = 1 << m
        low = (s // (2 * b) == t // (2 * b)) & (s // b > t // b)
        lev += [low, low.T, low]
    out["level_mask"] = np.tile(np.concatenate(lev, 1), (4, 1))
    out["eye2"] = np.tile(np.eye(B), (4, 2))
    out["reset"] = np.tile(np.arange(T) % C != 0, (P, 1))
    return {k: np.asarray(v, np.float32) for k, v in out.items()}


FIRST = ("ident", "ones", "before", "iota", "code", "eps")


def table_columns():
    at, n = {}, 0
    for k, v in tables().items():
        at[k] = (n, v.shape[1])
        n += v.shape[1]
    return at, n


VEC = {
    "A": (("dw_w", 62), ("dw_b", 2), ("conv_ln_g", 2), ("conv_ln_b", 2), ("norm1", 8), ("norm2", 8)),
    "B": (("b_ada", 48), ("shift_mu", 15), ("dec_w0", 8), ("iclr_a0", 8), ("k_k", 4), ("k_a", 4),
          ("r_k", 4), ("gn_g", 4), ("gn_b", 4)),
}
SHARED = (("final_norm", 8), ("c", 8), ("c_ctx", 8))


R_LG, R_MX, R_IX, R_IF, R_D, R_P, R_OH = 24, 48, 72, 96, 120, 124, 132
R_CW, R_RK, R_CNT, R_SL, R_FL, R_PS, R_JL, R_TM = 180, 252, 276, 284, 356, 372, 388, 408


def order(d):
    return (0, 2, 1, 3, 4, 5) if d == 0 else (1, 5, 0, 4, 3, 2)


def starts(d):
    return (0, 2) if d == 0 else (1, 5)


def nxt(d, c):
    n = c + 1 if d == 0 else c - 1
    if d == 0:
        return "end" if c == 1 else None if c == 5 else n
    return "end" if c == 0 else None if c == 2 else n


def L3(d):
    return 2 if d == 0 else 3


def other(d):
    return 5 - L3(d)


def flat(ap):
    return ap if len(ap.shape) == 1 else ap.rearrange("a b -> (a b)")


def e_transposes(pe, s, transpose, psum, eprod, i, c):
    pe.wait_ge(s("e_prod"), i * 3 + 3 + c + 1)
    if c == 2:
        pe.wait_ge(s("e_pT"), i * 3 + 1)
    k0, kn = DOWN[c]
    for k in range(kn):
        last = transpose(psum[6 + c % 2][:, k * P:(k + 1) * P], eprod[:, (k0 + k) * P:(k0 + k + 1) * P])
    last.then_inc(s("e_pT_full"), 1)


def e_copy(act, a, s, psum, eprodT, i, c):
    act.wait_ge(s("e_pT_full"), i * 3 + c + 1)
    k0, kn = DOWN[c]
    a(eprodT[:, k0:k0 + kn, :], psum[6 + c % 2][:, 0:kn * P].rearrange("p (k s) -> p k s", k=kn), ACT.Copy)\
        .then_inc(s("e_pT"), 1)


def build(nc, dram, outs, marks):
    yp, ys, new_state = outs
    tcol, ncols = table_columns()

    with ExitStack() as ctx:
        TOTAL = 52992 - 80
        base = (nc.sbuf_base + 31) // 32 * 32
        ctx.enter_context(nc.sbuf_tensor("arena", [P, TOTAL], F32))
        psum = [ctx.enter_context(nc.psum_tensor(f"bank{i}", [P, 512], F32)) for i in range(8)]
        used = {}

        def cut(name, start, n):
            used[name] = (start, start + n)
            assert start + n <= TOTAL, (name, start + n)
            return nc.alloc_sbuf_tensor_at(name, [P, n], F32, offset=base + 4 * start, align_bytes=4)[:, :]

        def parts(name, w, k, *starts):
            return [nc.alloc_sbuf_tensor_at(f"{name}_{part}", [P, k * w], F32R, offset=base + 4 * start, align_bytes=4)[:, :]
                    .rearrange("p (k t) -> p k t", k=k) for part, start in zip(("rounded", "rest"), starts)]

        n_first = sum(tcol[k][1] for k in FIRST)
        o = 0
        xT = cut("xT", o, KD * T).rearrange("p (k t) -> p k t", k=KD); o += KD * T
        first = cut("first", o, n_first); o += n_first
        vec = cut("vec", o, 4 * P).rearrange("p (g c) -> p g c", g=4); o += 4 * P
        mods = cut("mods", o, 96 * DEPTH).rearrange("p (l m s) -> p l m s", l=DEPTH, s=2); o += 96 * DEPTH
        modAs = cut("modAs", o, 32 * DEPTH).rearrange("p (l w k s) -> p l w k s", l=DEPTH, w=2, s=2); o += 32 * DEPTH
        condp = cut("condp", o, 32 * KD).rearrange("p (k s) -> p k s", s=32); o += 32 * KD
        cond = cut("cond", o, 16).rearrange("p (k s) -> p k s", s=2); o += 16
        condx = cut("condx", o, 16).rearrange("p (k s) -> p k s", s=2); o += 16
        mix = cut("mix", o, 32).rearrange("p (w z) -> p w z", w=2); o += 32
        oneka = cut("oneka", o, 4); o += 4
        pc = cut("pc", o, 24).rearrange("p (m c) -> p m c", m=NM); o += 24
        stat = cut("stat", o, 96); o += 96
        hT = cut("hT", o, KD * T).rearrange("p (k t) -> p k t", k=KD); o += KD * T
        low_end = o
        second = cut("second", o, ncols - n_first); o += ncols - n_first
        RING, SLOT = 6, 4 * 256
        ring = [cut(f"ring{i}", o + i * SLOT, SLOT) for i in range(RING)]; o += RING * SLOT
        low = cut("low", o, 3 * CR).rearrange("p (w c) -> p w c", w=3); o += 3 * CR
        z = cut("z", o, NZ * T).rearrange("p (m t) -> p m t", m=NZ)
        rows = cut("rows", o, 4 * P).rearrange("p (g c) -> p g c", g=4)
        o += NZ * T
        cvT = cut("cvT", o, 2 * T).rearrange("p (m t) -> p m t", m=2); o += 2 * T
        fnT = cut("fnT", o, 2 * T).rearrange("p (m t) -> p m t", m=2); o += 2 * T
        kk = cut("kk", o, NM * T).rearrange("p (m t) -> p m t", m=NM); o += NM * T
        ffn_at = o
        AR = cut("AR", o, 2 * NM * T).rearrange("p (m c k t) -> p m c k t", m=NM, c=NC_, k=2)
        ksq = cut("ksq", o, NM * T).rearrange("p (m t) -> p m t", m=NM)
        o += 2 * NM * T
        BK = cut("BK", o, 2 * NM * T).rearrange("p (k m t) -> p k m t", k=2, m=NM)
        TQ = cut("TQ", o, 24 * C).rearrange("p (c h w) -> p c h w", c=NCP, h=NH)
        U = cut("U", o, 24 * C).rearrange("p (c h w) -> p c h w", c=NCP, h=NH)
        Q = cut("Q", o + 24 * C, 24 * C).rearrange("p (c h w) -> p c h w", c=NCP, h=NH)
        yT = cut("yT", o, NM * T).rearrange("p (m t) -> p m t", m=NM)
        o += 2 * NM * T
        S1 = cut("S1", o, 24 * 256).rearrange("p (c h w) -> p c h w", c=NCP, h=NH)
        tmp4 = [cut(f"tmp{i}", o + i * NM * T, NM * T) for i in range(4)]
        shifted = cut("shifted", o, NZ * T).rearrange("p (m t) -> p m t", m=NZ)
        o += 24 * 256
        tok = cut("tok", o, 2 * NCP * CR).rearrange("p (k c w) -> p k c w", k=2, c=NCP)
        fno_u = cut("fno_u", o, 2 * T).rearrange("p (m t) -> p m t", m=2)
        fno_z = cut("fno_z", o + 2 * T, NCP * 512).rearrange("p (j m w) -> p j m w", j=NCP, m=2)
        sq = cut("sq", o, KD * T).rearrange("p (k t) -> p k t", k=KD)
        xin = cut("xin", o, 3 * DM).rearrange("p (j d) -> p j d", j=3)
        o += 2 * NCP * CR
        PADC = TP + 30 + 4 * (GRID + 30)
        glu = cut("glu", o, 2 * PADC).rearrange("p (m t) -> p m t", m=2)
        diag = [cut(f"diag{i}", o + 2 * PADC + i * P, P) for i in range(3)]
        assert 2 * PADC + 3 * P <= NCP * CR
        vtok = cut("vtok", o, NCP * CR).rearrange("p (c w) -> p c w", c=NCP); o += NCP * CR
        conv_b = cut("conv_b", o, 2 * T).rearrange("p (m t) -> p m t", m=2)
        diag += [cut(f"diag{3 + i}", o + 2 * T + i * P, P) for i in range(5)]
        adas = cut("adas", o, 1536)
        Y = cut("Y", o, NCP * CR).rearrange("p (c w) -> p c w", c=NCP); o += NCP * CR
        St = cut("St", o, NC_ * 512).rearrange("p (c m v) -> p c m v", c=NC_, m=NM); o += NC_ * 512
        Sfin = cut("Sfin", o, 256).rearrange("p (m v) -> p m v", m=NM); o += 256
        XW = o
        Wb = [cut(f"Wb{i}", o + 512 * i, 512) for i in range(2)]
        Xs = [cut(f"Xs{i}", o + 256 * i, 256) for i in range(3)]
        rs = cut("rs", o, T); o += 1024
        st_in = cut("st_in", o, 1024); o += 1024
        sout = cut("sout", o, 512); o += 512
        fsig = [cut(f"fsig{i}", ffn_at + KF * T + i * T, T) for i in range(3)]
        fprod = [cut(f"fprod{i}", ffn_at + KF * T + (3 + i) * T, T) for i in range(3)]
        assert ffn_at + (KF + 6) * T <= used["tok"][0] and used["kk"][1] - used["z"][0] >= KF * T
        assert o <= TOTAL, o
        at_ = lambda name: used[name][0]
        merged = [cut(f"merged{k}", at_("Q") + k * T if k < 4 else at_("kk") + (k - 4) * T, T) for k in range(KD)]
        h_parts = {
            "z": parts("h1", T, KD, at_("AR"), at_("BK")),
            "gate": parts("hg", T, KD, at_("AR"), at_("tok")),
            "ffn": parts("h2", T, KD, at_("tok"), at_("vtok")),
            "merged": parts("merged", T, KD, at_("z"), at_("z") + KD * T),
            "prod": parts("prod", T, KF, at_("z"), ffn_at),
        }
        assert at_("z") + 2 * KD * T <= used["cvT"][1]
        NSLOT = 3
        w_parts = [parts(f"weights{i}", P, 4, at_("St") + 1024 * i, at_("St") + 1024 * i + 512) for i in range(NSLOT)]
        o = low_end
        htok = cut("htok", o, 3 * DM).rearrange("p (j d) -> p j d", j=3); o += 3 * DM
        hG = cut("hG", o, DM).rearrange("p (k s) -> p k s", k=KD); o += DM
        eprod = cut("eprod", o, DE)
        ey = cut("ey", o, DM); o += DE
        eprodT = cut("eprodT", o, KE * P).rearrange("p (k s) -> p k s", k=KE); o += KE * P
        sel = cut("sel", o, 3 * P).rearrange("p (j s) -> p j s", j=3); o += 3 * P
        selc = cut("selc", o, 3 * P).rearrange("p (j s) -> p j s", j=3); o += 3 * P
        selT = cut("selT", o, 3 * P).rearrange("p (j s) -> p j s", j=3); o += 3 * P
        esig = cut("esig", o, 512); o += 512
        rt = cut("rt", o, 900); o += 900
        rt_i = rt[:, 560:600].bitcast(I32)
        wrt = cut("wrt", o, 64).rearrange("p (k e) -> p k e", k=KD); o += 64
        brt = cut("brt", o, 8); o += 8
        yacc = cut("yacc", used["hT"][0], 3 * DM).rearrange("p (j d) -> p j d", j=3)
        o = TOTAL - (2 * KD * DE + KE * DM)
        assert o >= used["brt"][1], (o, used["brt"])
        wgu = []
        for c, (c0, n) in enumerate(CHUNKS):
            pair = []
            for which in range(2):
                pair.append(cut(f"wgu{c}{which}", o, KD * n).rearrange("p (k n) -> p k n", k=KD)); o += KD * n
            wgu.append(pair)
        wdn = cut("wdn", o, KE * DM).rearrange("p (k n) -> p k n", k=KE)

        def tab(name):
            a, n = tcol[name]
            return first[:, a:a + n] if name in FIRST else second[:, a - n_first:a - n_first + n]

        ident, ones, heads, before, iota = (tab(k) for k in ("ident", "ones", "heads", "before", "iota"))
        pair_mask = tab("pair_mask").rearrange("p (d w) -> p d w", d=2)
        level_mask = tab("level_mask").rearrange("p (l w) -> p l w", l=LEVELS)
        time_p = tab("time_p").rearrange("p (j k n) -> p j k n", j=1, k=2)
        time_s = tab("time_s").rearrange("p (j k n) -> p j k n", j=2, k=2)
        eps = {v: tab("eps")[:, i:i + 1] for i, v in enumerate((1e-6, 1e-5, 64e-5))}

        vat = {}
        for l in range(DEPTH):
            for gi, g in enumerate("AB"):
                r = 0
                for name, n in VEC[g]:
                    vat[name, l] = (2 * l + gi, r)
                    r += n
                if g == "A" and l == 0:
                    for name, n in SHARED:
                        vat[name, 0] = (0, r)
                        r += n

        def v(name, l, i=0, n=1):
            g, r = vat[name, l]
            return vec[:, g, r + i:r + i + n]

        def gsig(i):
            return tmp4[3 if i % 8 >= 4 else 0][:, (i % 4) * T:(i % 4 + 1) * T]

        sems = {}

        class Sem:
            def __init__(self, name):
                self.h, self.n = ctx.enter_context(nc.semaphore(name)), 0

        def sem(name):
            if name not in sems:
                sems[name] = Sem(name)
            return sems[name]

        def at(name, *key):
            return sem(name).h, marks.get((name,) + key, 1)

        class Counts:

            def __init__(self, steps):
                self.steps = steps

            def up(self, name, *key, by=1):
                s = sem(name)
                s.n += by
                marks[(name,) + key] = s.n
                if by == 1:
                    self.last = (s.h, s.n)
                return s.h, by

            def step(self):
                return self.up(self.steps)

            def read(self, *job):
                name = f"bank_free{marks.get(('bank',) + job, 0)}"
                self.last = at(name, *job)
                return sem(name).h, 1

            def fill(self, *job):
                return self.up(f"bank_full{marks[('bank',) + job]}", *job)

            def latest(self):
                return self.last

        def bank(*job):
            return psum[marks.get(("bank",) + job, 0)]

        def filled(*job):
            return at(f"bank_full{marks.get(('bank',) + job, 0)}", *job)

        def drained(*job):
            return at(f"bank_free{marks.get(('bank',) + job, 0)}", *job)

        blocks = []

        def cols(w, c0, n, k0=0, k=4):
            return w.rearrange("(k p) n -> p k n", p=P)[:, k0:k0 + k, c0:c0 + n], k, n

        def add(key, src, last):
            blocks.append((key, src, last))

        def halves(key, w, c0, n, last):
            for half in range(2):
                add(key + (half,), cols(w, c0, n, 4 * half), last)

        def add_ada(l):
            for i in range(12):
                for half in range(2):
                    for j in range(2):
                        add(("ada", l, i, half, j), cols(dram["w_ada"][l], 512 * i + 256 * j, 256, 4 * half), ("ada", l, i, half))

        add_ada(0)
        for l in range(DEPTH):
            for i in range(8):
                halves(("z", l, i), dram["w_in"][l], OFF_Z + 256 * i, 256 if i < 7 else 128, ("z", l, min(2 * i + 1, 14)))
            for i in range(3):
                halves(("cf", l, i), dram["w_in"][l], 256 * i, 256, ("cf", l, 2 * i + 1))
            if l + 1 < DEPTH:
                add_ada(l + 1)
            for b, (w, k) in enumerate((("w_conv_out", 2), ("w_fno_out", 2), ("w_rwkv_out", 4))):
                for i in range(4):
                    add(("bw", l, b, i, 0), cols(dram[w][l], 256 * i, 256, 0, k), ("br", l, b, 2 * i + 1))
                    halves(("gate", l, b, i), dram["w_in"][l], OFF_G + DM * b + 256 * i, 256, ("gate", l, b, 2 * i + 1))
            for i in range(4):
                halves(("wo", l, i), dram["w_o"][l], 256 * i, 256, ("o", l, 2 * i + 1))
            if l % 2 == 0:
                for i in range(KF // 2):
                    halves(("fg", l, i), dram["ffn_w_gate"][l // 2], 256 * i, 256, ("fg", l, 2 * i + 1))
                    halves(("fu", l, i), dram["ffn_w_up"][l // 2], 256 * i, 256, ("fu", l, 2 * i + 1))
                for i in range(KF):
                    add(("fd", l, i), cols(dram["ffn_w_down"][l // 2], 0, DM, i, 1), ("fd", l, i))
        slot_of = {key: n % RING for n, (key, _, _) in enumerate(blocks)}

        pieces = []

        def tile_pieces(job, block, h):
            for half in range(2):
                n = 128 if block == ("z", block[1], 7) else 256
                raw = ring[slot_of[block + (half,)]][:, 0:4 * n].rearrange("p (k n) -> p k n", k=4)
                pieces.append((job + (half,), block + (half,), raw[:, :, h * P:(h + 1) * P], job if half else None))

        for l in range(DEPTH):
            for kind, n in (("z", NZ), ("cf", 6)):
                for m in range(n):
                    tile_pieces((kind, l, m), (kind, l, m // 2), m % 2)
            for b in range(3):
                for m in range(KD):
                    tile_pieces(("gate", l, b, m), ("gate", l, b, m // 2), m % 2)
            for m in range(KD):
                tile_pieces(("o", l, m), ("wo", l, m // 2), m % 2)
            if l % 2 == 0:
                for m in range(KF):
                    for kind in ("fg", "fu"):
                        tile_pieces((kind, l, m), (kind, l, m // 2), m % 2)
                for i in range(KF):
                    for half in range(2):
                        raw = ring[slot_of[("fd", l, i)]][:, half * 512:(half + 1) * 512].rearrange("p (k n) -> p k n", k=4)
                        pieces.append((("fd", l, i, half), ("fd", l, i), raw, None))
        piece_at = {key: n for n, (key, _, _, _) in enumerate(pieces)}
        last_piece = {block: key for key, block, _, _ in pieces}

        def phase_pieces(*kinds_l):
            return [n for n, (key, _, _, _) in enumerate(pieces) if key[:2] in kinds_l]

        block = ctx.enter_context(nc.Block())

        @block.sync
        def _(sp):
            S = Counts("sync_step")
            for n, (key, (src, k, w), last) in enumerate(blocks):
                if key[0] == "z" and key[2:] == (0, 0):
                    l = key[1]
                    if l > 0:
                        sp.wait_ge(*filled("gup", l - 1, 3))
                    for i, src_ in enumerate((dram["dec_up"][l].rearrange("d r c -> (d r) c"),
                                              dram["iclr_up"][l].rearrange("d r c -> (d r) c"), dram["g_up"][l])):
                        sp.dma_start(low[:, i, :], src_).then_inc(*S.up("low_in", l, by=16))
                if n >= RING:
                    prev = blocks[n - RING][2]
                    if blocks[n - RING][0] in last_piece:
                        sp.wait_ge(*at("rest_ready", *last_piece[blocks[n - RING][0]]))
                    elif prev[0] == "ada":
                        sp.wait_ge(*at("block_used", *prev))
                    else:
                        sp.wait_ge(*filled(*prev))
                dst = ring[n % RING][:, 0:k * w].rearrange("p (k n) -> p k n", k=k)
                sp.dma_start(dst, src).then_inc(*S.up(f"block_in{n % RING}", *key, by=16))
            sp.wait_ge(*at("h2_ready", 1))
            sp.wait_ge(*filled("o", 1, 7))
            sp.wait_ge(*at("out_stored", "state", 1, 1))

            def expert_weights(e, wait):
                for c, (c0, n) in enumerate(CHUNKS):
                    if wait is not None:
                        sp.wait_ge(sem("e_gu").h, wait * 3 + (c + 1))
                    for which, w in enumerate(("moe_w_gate", "moe_w_up")):
                        src = dram[w][0, e].rearrange("(k p) n -> p k n", p=P)[:, :, c0:c0 + n]
                        sp.dma_start(wgu[c][which][:, :, :], src).then_inc(sem(f"e_gu_in{c}").h, 16)
                    k0, kn = DOWN[c]
                    if wait is not None and c == 0:
                        sp.wait_ge(sem("e_y").h, wait + 1)
                    src = dram["moe_w_down"][0, e].rearrange("(k p) n -> p k n", p=P)[:, k0:k0 + kn, :]
                    sp.dma_start(wdn[:, k0:k0 + kn, :], src).then_inc(sem(f"e_dn_in{c}").h, 16)

            expert_weights(0, None)
            sp.wait_ge(*at("jobs_ready"))
            jobs = sp.value_load(rt_i[0:1, 0:1], min_val=NE, max_val=NJOB)
            with sp.Fori(1, jobs) as j:
                e = sp.value_load(rt_i[0:1, bass.ds(j + 1, 1)], min_val=0, max_val=NE - 1)
                expert_weights(e, j - 1)
            sp.wait_ge(sem("out_stored").h, 16 * 7)

        @block.tensor
        def _(pe):
            E = Counts("pe_step")
            jobs = [0]
            uses = [0] * 4
            prev_job = {}

            def used_for(b, *job):
                uses[b] += 1
                marks[(f"bank_free{b}",) + job] = uses[b]
                prev_job[b] = job

            def begin(*job):
                b = jobs[0] % 4
                jobs[0] += 1
                marks[("bank",) + job] = b
                if b in prev_job:
                    pe.wait_ge(*at(f"bank_free{b}", *prev_job[b]))
                used_for(b, *job)
                return psum[b]

            def transpose(out, src, n=P):
                return pe.transpose(out, src, ident[0:n, 0:n])

            def mm(out, lhsT, rhs, start, stop):
                return pe.matmul(out, lhsT, rhs, start=start, stop=stop)

            def tile(out, w, rhs, kn=KD):
                for k in range(kn):
                    last = mm(out, w(k), rhs(k), k == 0, k == kn - 1)
                return last

            pe.wait_ge(*at("first_in"))
            pe.wait_ge(*at("rows_in"))
            b = begin("vec")
            for g in range(4):
                n = sum(r for _, r in VEC["AB"[g % 2]]) + (24 if g == 0 else 0)
                last = transpose(b[:, g * P:g * P + n], rows[0:n, g, :], n)
            last.then_inc(*E.fill("vec"))
            pe.wait_ge(*at("x_in"))
            for k in range(KD):
                b = begin("xt", k)
                for j in range(3):
                    last = transpose(b[:, j * P:(j + 1) * P], xin[:, j, k * P:(k + 1) * P])
                last.then_inc(*E.fill("xt", k))

            def norm_sum(l, which):
                b = begin("norm", l, which)
                for k in range(KD):
                    if k == 0 or k == 4:
                        pe.wait_ge(*at("sq_ready", l, which, k // 4))
                    last = mm(b[:, 0:T], ones, sq[:, k, :], k == 0, k == KD - 1)
                last.then_inc(*E.fill("norm", l, which))

            def weights(key, n, kn=KD):
                slots = []
                for half in range((kn + 3) // 4):
                    key_ = key + (half,)
                    pe.wait_ge(*at(f"block_in{slot_of[key_]}", *key_))
                    slots.append(ring[slot_of[key_]][:, 0:min(kn, 4) * n].rearrange("p (k n) -> p k n", n=n))
                return lambda k, h: slots[k // 4][:, k % 4, h * P:(h + 1) * P]

            def three(out, w, x, i, k, start, stop):
                wr, wl, xr, xl = w[0][:, i], w[1][:, i], x[0][:, k], x[1][:, k]
                mm(out, wr, xr, start, False)
                mm(out, wr, xl, False, False)
                return mm(out, wl, xr, False, stop)

            def dense(job, phase, l, first=False):
                b = begin(*job)
                for half in range(2):
                    key = job + (half,)
                    pe.wait_ge(*at("rest_ready", *key))
                    w = w_parts[piece_at[key] % NSLOT]
                    for i in range(4):
                        k = 4 * half + i
                        if first and k % 2 == 0:
                            pe.wait_ge(*at("x_parts", phase, l, k // 2))
                        last = three(b[:, 0:T], w, h_parts[phase], i, k, k == 0, k == KD - 1)
                    if half == 0:
                        last.then_inc(*E.up("piece_used", *key))
                last.then_inc(*E.fill(*job))


            def ada(l, i):
                for half in range(2):
                    w = []
                    for j in range(2):
                        key = ("ada", l, i, half, j)
                        pe.wait_ge(*at(f"block_in{slot_of[key]}", *key))
                        w.append(ring[slot_of[key]].rearrange("p (k n) -> p k n", n=256))
                    for k in range(4):
                        for j in range(4):
                            last = mm(psum[4 + i // 4][32 * j:32 * j + 32, (i % 4) * P:(i % 4 + 1) * P],
                                      condp[:, 4 * half + k, :], w[j // 2][:, k, (j % 2) * P:(j % 2 + 1) * P],
                                      k + half == 0, k == 3 and half == 1)
                    last.then_inc(*E.up("block_used", "ada", l, i, half))

            def ada_turn(l):
                for g in range(3):
                    b = begin("adaT", l, g)
                    pe.wait_ge(*at("ada_copied", l, g))
                    for i in range(4):
                        last = transpose(b[:, i * P:(i + 1) * P], adas[:, (4 * g + i) * P:(4 * g + i + 1) * P])
                    last.then_inc(*E.fill("adaT", l, g))

            for l in range(DEPTH):
                if l == 0:
                    pe.wait_ge(*at("cond_ready"))
                    for i in range(12):
                        ada(0, i)
                    ada_turn(0)
                norm_sum(l, 0)
                for m in range(NZ):
                    dense(("z", l, m), "z", l, m == 0)
                for m in range(6):
                    dense(("cf", l, m), "z", l)
                if l == 0:
                    pe.wait_ge(*at("second_in"))
                for m in range(NM):
                    b = begin("kks", l, m)
                    if m == 0:
                        pe.wait_ge(*at("ksq_ready", l))
                    mm(b[:, 0:T], heads, ksq[:, m, :], True, True).then_inc(*E.fill("kks", l, m))
                def lowrank(d):
                    if d == 0:
                        pe.wait_ge(*at("low_in", l))
                        pe.wait_ge(*at("low_in_ready", l))
                    r = slice(64 * d, 64 * d + 64)
                    for which in range(2):
                        for m in range(NM):
                            b = begin("low", l, d, which, m)
                            mm(b[:, 0:T], low[r, which, m * P:(m + 1) * P], z[r, 13 + which, :], True, True).then_inc(*E.fill("low", l, d, which, m))

                lowrank(0)
                for m in range(4, 6):
                    pe.wait_ge(*drained("cf", l, m))
                for j in range(NCP):
                    b = begin("fno1", l, j)
                    for m in range(2):
                        last = mm(b[:, m * 256:(m + 1) * 256], fno_u[:, m, j * P:(j + 1) * P],
                                  second[:, tcol["dft_c"][0] - n_first:tcol["dft_c"][0] - n_first + 256], True, True)
                    last.then_inc(*E.fill("fno1", l, j))
                for j in range(NCP):
                    pe.wait_ge(*drained("fno1", l, j))
                for m in range(2):
                    b = begin("fno2", l, m)
                    for i in range(2):
                        mm(b[:, 0:TP], fno_z[:, 0, m, i * P:(i + 1) * P], time_p[:, 0, i, :], i == 0, i == 1)
                    for j in range(2):
                        for i in range(2):
                            last = mm(b[:, TP:T], fno_z[:, 1 + j, m, i * P:(i + 1) * P], time_s[:, j, i, :],
                                      j == 0 and i == 0, j == 1 and i == 1)
                    last.then_inc(*E.fill("fno2", l, m))
                pe.wait_ge(*at("glu_ready", l))
                for m in range(2):
                    b = begin("conv", l, m)
                    b2 = begin("conv_s", l, m)
                    sp_ = glu[:, m, TP + 30:].rearrange("p (r t) -> p r t", r=4)
                    for j in range(CONV_W):
                        i = m * CONV_W + j
                        pe.wait_ge(*at("diag_ready", l, i))
                        mm(b[:, 0:TP], diag[i % 8], glu[:, m, j:j + TP], j == 0, j == CONV_W - 1)
                        last = mm(b2[:, 0:TS].rearrange("p (r t) -> p r t", r=4), diag[i % 8], sp_[:, :, j:j + GRID], j == 0, j == CONV_W - 1)
                        if j < CONV_W - 1:
                            last.then_inc(*E.up("diag_used", l, i))
                    last.then_inc(*E.fill("conv_s", l, m))
                for w in range(2):
                    b = begin("cln", l, w)
                    if w == 0:
                        for m in range(2):
                            pe.wait_ge(*drained("conv", l, m))
                            pe.wait_ge(*drained("conv_s", l, m))
                    else:
                        pe.wait_ge(*at("conv_sq", l))
                    src = cvT if w == 0 else conv_b
                    for m in range(2):
                        last = mm(b[:, 0:T], ones, src[:, m, :], m == 0, m == 1)
                    last.then_inc(*E.fill("cln", l, w))

                for d in range(2):
                    if d == 1:
                        lowrank(1)
                    pe.wait_ge(*at("ark_ready", l, d))
                    for cp in range(NCP):
                        for i in range(3 if d == 0 else 2):
                            b = begin("tok", l, d, cp, i)
                            for m in range(NM):
                                src = (BK[:, i, m, :] if i < 2 else z[:, 8 + m, :])[:, cp * P:(cp + 1) * P]
                                last = transpose(b[:, m * P:(m + 1) * P], src)
                            last.then_inc(*E.fill("tok", l, d, cp, i))
                    for cp in range(NCP):
                        for hp in range(NH // 2):
                            b = begin("pair", l, d, cp, hp)
                            r = slice(64 * (hp % 2), 64 * (hp % 2) + 64)
                            for i in range(2):
                                for hh in range(2):
                                    m = 2 * (hp // 2) + hh
                                    for par in range(2):
                                        q = slice(64 * par, 64 * par + 64)
                                        c = 2 * cp + par
                                        o_ = hh * 256 + i * P
                                        last = mm(b[q, o_:o_ + P], BK[r, i, m, c * C:(c + 1) * C],
                                                  AR[r, m, c, :, :], True, True)
                            last.then_inc(*E.fill("pair", l, d, cp, hp))
                    quarters = [(slice(32 * g, 32 * g + 32), g % 2) for g in range(4)]
                    for lev in range(LEVELS):
                        for u in range(NCP + 1):
                            if u < NCP:
                                b = begin("X", l, d, lev, u)
                                if lev == 0:
                                    pe.wait_ge(*at("TQ_ready", l, d, u))
                                else:
                                    pe.wait_ge(*drained("TAT", l, d, lev - 1, u))
                                for h in range(NH):
                                    for q, blk in quarters:
                                        last = mm(b[q, h * B:(h + 1) * B], S1[q, u, h, blk * B:(blk + 1) * B],
                                                  TQ[q, u, h, 0:B], True, True)
                                last.then_inc(*E.fill("X", l, d, lev, u))
                            if u > 0:
                                w = u - 1
                                b = begin("TAT", l, d, lev, w)
                                pe.wait_ge(*drained("X", l, d, lev, w))
                                for h in range(NH):
                                    for q, blk in quarters:
                                        mm(b[q, h * C:h * C + B], TQ[q, w, h, B:C], Xs[w][q, h * B:(h + 1) * B], True, True)
                                    for q, blk in quarters:
                                        last = mm(b[q, h * C + B:(h + 1) * C], Xs[w][q, h * B:(h + 1) * B], TQ[q, w, h, B:C],
                                                  True, True)
                                last.then_inc(*E.fill("TAT", l, d, lev, w))
                                if d == 0 and l + 1 < DEPTH and 3 * lev + w < 12:
                                    ada(l + 1, 3 * lev + w)
                    for u in range(NCP + 1):
                        if u < NCP:
                            b = begin("XO", l, d, u)
                            pe.wait_ge(*drained("TAT", l, d, LEVELS - 1, u))
                            for h in range(NH):
                                for par in range(2):
                                    fr, to = quarters[2 * par + d][0], quarters[2 * par + 1 - d][0]
                                    last = mm(b[to, h * B:(h + 1) * B], S1[fr, u, h, (1 - d) * B:(2 - d) * B],
                                              TQ[fr, u, h, 0:B], True, True)
                            last.then_inc(*E.fill("XO", l, d, u))
                        if u > 0:
                            w = u - 1
                            b = begin("QO", l, d, w)
                            pe.wait_ge(*drained("XO", l, d, w))
                            for h in range(NH):
                                for par in range(2):
                                    fr, to = quarters[2 * par + d][0], quarters[2 * par + 1 - d][0]
                                    last = mm(b[fr, h * B:(h + 1) * B], Xs[w][to, h * B:(h + 1) * B], TQ[to, w, h, B:C],
                                              True, True)
                            last.then_inc(*E.fill("QO", l, d, w))
                    if d == 0:
                        pe.wait_ge(*at("st_in", l))
                    b = begin("s0", l, d)
                    sti = st_in.rearrange("p (d h k) -> p d h k", d=2, h=NH)
                    for m in range(NM):
                        last = transpose(b[:, m * C:(m + 1) * C], sti[0:64, d, 2 * m:2 * m + 2, :], 64)
                    last.then_inc(*E.fill("s0", l, d))
                    for n, c in enumerate(order(d)):
                        cp, par = divmod(c, 2)
                        q = slice(64 * par, 64 * par + 64)
                        if c == starts(d)[1]:
                            pe.wait_ge(*drained("s0", l, d))
                        else:
                            pe.wait_ge(*at("S_ready", l, d, c))
                        b = begin("W", l, d, c)
                        for m in range(NM):
                            mm(b[q, m * P:(m + 1) * P], AR[:, m, c, 0, :], St[:, c, m, :], m == 0, False)
                        for h in range(NH):
                            last = mm(b[q, h * C:(h + 1) * C], S1[q, cp, h, 2 * C:3 * C], vtok[q, cp, h * C:(h + 1) * C],
                                      False, h == NH - 1)
                        last.then_inc(*E.fill("W", l, d, c))
                        b = begin("U", l, d, c)
                        pe.wait_ge(*drained("W", l, d, c))
                        if n == 0:
                            pe.wait_ge(*at("Qdiag_ready", l, d))
                            for u in range(NCP):
                                pe.wait_ge(*drained("QO", l, d, u))
                        for h in range(NH):
                            last = mm(b[q, h * C:(h + 1) * C], Q[q, cp, h, :], Wb[n % 2][q, h * C:(h + 1) * C], True, True)
                        last.then_inc(*E.fill("U", l, d, c))
                        if nxt(d, c) is None:
                            continue
                        b = begin("S", l, d, c)
                        pe.wait_ge(*drained("U", l, d, c))
                        for h in range(NH):
                            m, r = h // 2, slice(64 * (h % 2), 64 * (h % 2) + 64)
                            oc = b[r, m * C:(m + 1) * C]
                            hs = slice(h * C, (h + 1) * C)
                            mm(oc, tok[q, 1, cp, hs], vtok[q, cp, hs], True, False)
                            last = mm(oc, tok[q, 0, cp, hs], U[q, cp, h, :], False, True)
                        last.then_inc(*E.fill("S", l, d, c))
                    if d == 0 and l + 1 < DEPTH:
                        ada_turn(l + 1)
                    pe.wait_ge(*drained("U", l, d, order(d)[-1]))
                    for cp in range(NCP):
                        b = begin("Y", l, d, cp)
                        halves_ = [(slice(64 * par, 64 * par + 64), 2 * cp + par) for par in range(2)]
                        for m in range(NM):
                            for q, c in halves_:
                                mm(b[q, m * P:(m + 1) * P], AR[:, m, c, 1, :], St[:, c, m, :], m == 0, False)
                        for h in range(NH):
                            hs = slice(h * C, (h + 1) * C)
                            for q, c in halves_:
                                mm(b[q, hs], S1[q, cp, h, C:2 * C], U[q, cp, h, :], False, False)
                            for q, c in halves_:
                                last = mm(b[q, hs], S1[q, cp, h, 3 * C:4 * C], vtok[q, cp, hs], False, h == NH - 1)
                        last.then_inc(*E.fill("Y", l, d, cp))
                    b = begin("sf", l, d)
                    pe.wait_ge(*at("Sfin_ready", l, d))
                    for m in range(NM):
                        last = transpose(b[0:64, m * P:(m + 1) * P], Sfin[:, m, :])
                    last.then_inc(*E.fill("sf", l, d))
                def gates(b_, src, kn):
                    for m in range(KD):
                        if m % 2 == 0:
                            wb = weights(("bw", l, b_, m // 2), 256, kn)
                        dense(("gate", l, b_, m), "gate", l, b_ == 0 and m == 0)
                        b = begin("br", l, b_, m)
                        tile(b[:, 0:T], lambda k: wb(k, m % 2), lambda k: src[:, k, :], kn).then_inc(*E.fill("br", l, b_, m))

                pe.wait_ge(*at("cv_ready", l))
                gates(0, cvT, 2)
                for m in range(2):
                    pe.wait_ge(*drained("fno2", l, m))
                gates(1, fnT, 2)
                for cp in range(NCP):
                    b = begin("yt", l, cp)
                    if cp == 0:
                        pe.wait_ge(*at("yn_ready", l))
                    for m in range(NM):
                        last = transpose(b[:, m * P:(m + 1) * P], Y[:, cp, m * P:(m + 1) * P])
                    last.then_inc(*E.fill("yt", l, cp))
                for m in range(NM):
                    b = begin("bon", l, m)
                    if m == 0:
                        pe.wait_ge(*at("rk_ready", l))
                    mm(b[:, 0:T], heads, tmp4[1][:, m * T:(m + 1) * T], True, True).then_inc(*E.fill("bon", l, m))
                for m in range(NM):
                    b = begin("gup", l, m)
                    mm(b[:, 0:T], low[:, 2, m * P:(m + 1) * P], z[:, 12, :], True, True).then_inc(*E.fill("gup", l, m))
                for m in range(NM):
                    pe.wait_ge(*drained("gup", l, m))
                gates(2, yT, 4)
                for m in range(KD):
                    dense(("o", l, m), "merged", l, m == 0)
                norm_sum(l, 1)
                if l % 2 == 0:
                    for m in range(KF):
                        dense(("fg", l, m), "ffn", l, m == 0)
                        dense(("fu", l, m), "ffn", l)
                    for m in range(4):
                        pe.wait_ge(*at(f"bank_free{m}", *prev_job[m]))
                    for i in range(KF):
                        pe.wait_ge(*at("prod_rest", l, i))
                        for half in range(2):
                            key = ("fd", l, i, half)
                            pe.wait_ge(*at("rest_ready", *key))
                            for m in range(4):
                                last = three(psum[4 * half + m][:, 0:T], w_parts[piece_at[key] % NSLOT], h_parts["prod"], m, i, i == 0, i == KF - 1)
                            last.then_inc(*E.up("piece_used", *key))
                    for m in range(4):
                        used_for(m, "fdown", l, m)
            b = begin("logit")
            pe.wait_ge(*at("h2_ready", DEPTH - 1))
            pe.wait_ge(*at("router_in"))
            for j in range(3):
                for k in range(KD):
                    mm(b[:, j * NE:(j + 1) * NE], hT[:, k, j * P:(j + 1) * P], wrt[:, k, :], k == 0, False)
                last = mm(b[:, j * NE:(j + 1) * NE], ones[0:1, :], brt[0:1, :], False, True)
            last.then_inc(*E.fill("logit"))
            for k in range(6):
                b = begin("htok", k)
                for i in range(4):
                    j, kk_ = divmod(4 * k + i, KD)
                    last = transpose(b[:, i * P:(i + 1) * P], hT[:, kk_, j * P:(j + 1) * P])
                last.then_inc(*E.fill("htok", k))
            b = begin("rank")
            pe.wait_ge(*at("chosen_ready"))
            ch = rt[:, 0:24]
            for j in range(3):
                for i in range(j + 1):
                    mm(b[:, j * NE:(j + 1) * NE], before if i == j else ones, ch[:, i * NE:(i + 1) * NE], i == 0, i == j)
            for i in range(3):
                last = mm(b[:, 24:32], ones, ch[:, i * NE:(i + 1) * NE], i == 0, i == 2)
            last.then_inc(*E.fill("rank"))
            pe.wait_ge(*at("jobs_ready"))
            for m in range(4):
                pe.wait_ge(*at(f"bank_free{m}", *prev_job[m]))
            pe.wait_ge(*at("fdown_done", 0))
            s = lambda name: sem(name).h
            pe.sem_inc(s("e_sc"), 6)
            njobs = pe.value_load(rt_i[0:1, 0:1], min_val=NE, max_val=NJOB)
            with pe.Fori(0, njobs) as i:
                pe.wait_ge(s("e_sel"), i + 1)
                pe.wait_ge(s("e_ydrained"), i * 2 + 2)
                for j in range(3):
                    last = transpose(psum[4][:, j * P:(j + 1) * P], selc[:, j, :])
                last.then_inc(s("e_selT_full"), 1)
                pe.wait_ge(s("e_sc_done"), i * 6 + 6)
                for k in range(KD):
                    for j in range(3):
                        last = mm(psum[6 + k // 4][:, (k % 4) * P:(k % 4 + 1) * P], htok[:, j, k * P:(k + 1) * P],
                                  sel[:, j, :], j == 0, j == 2)
                    if k % 4 == 3:
                        last.then_inc(s("e_gather"), 1)
                pe.wait_ge(s("e_hG"), i * 2 + 2 + 2)
                for c, (c0, n) in enumerate(CHUNKS):
                    bg, bu = psum[2 * (c % 2)], psum[2 * (c % 2) + 1]
                    pe.wait_ge(s("e_prod"), i * 3 + 3 + (1 if c == 2 else 0))
                    pe.wait_ge(s(f"e_gu_in{c}"), i * 32 + 32)
                    for which, bb in ((0, bg), (1, bu)):
                        for k in range(KD):
                            last = mm(bb[:, 0:n], hG[:, k, :], wgu[c][which][:, k, :], k == 0, k == KD - 1)
                    last.then_inc(s("e_gu"), 1)
                    if c > 0:
                        e_transposes(pe, s, transpose, psum, eprod, i, c - 1)
                for c, (k0, kn) in enumerate(DOWN):
                    if c == 2:
                        e_transposes(pe, s, transpose, psum, eprod, i, 2)
                    pe.wait_ge(s(f"e_dn_in{c}"), i * 16 + 16)
                    pe.wait_ge(s("e_pT"), i * 3 + c + 1)
                    if c == 0:
                        pe.wait_ge(s("e_selT"), i + 1)
                    for k in range(k0, k0 + kn):
                        for half in range(2):
                            last = mm(psum[4 + half][:, :], eprodT[:, k, :], wdn[:, k, half * 512:(half + 1) * 512],
                                      k == 0, k == KE - 1)
                last.then_inc(s("e_y"), 1)
                pe.wait_ge(s("e_ydrained"), i * 2 + 2 + 2)
                for j in range(3):
                    for half in range(2):
                        n_ = 2 * j + half
                        if n_ >= 2:
                            pe.wait_ge(s("e_sc_done"), i * 6 + 6 + n_ - 1)
                        mm(psum[6 + half][:, :], selT[:, j, :], ey[:, half * 512:(half + 1) * 512], True, True)\
                            .then_inc(s("e_sc"), 1)
            for m in range(4):
                prev_job.pop(m, None)
            pe.wait_ge(*at("yacc_ready"))
            for k in range(KD):
                b = begin("ey", k)
                for j in range(3):
                    last = transpose(b[:, j * P:(j + 1) * P], yacc[:, j, k * P:(k + 1) * P])
                last.then_inc(*E.fill("ey", k))
            norm_sum(DEPTH, 0)
            pe.wait_ge(*at("h_ready", DEPTH))
            for j in range(3):
                for half in range(2):
                    b = begin("yo", j, half)
                    for k in range(4):
                        last = transpose(b[:, k * P:(k + 1) * P], sq[:, 4 * half + k, j * P:(j + 1) * P])
                    last.then_inc(*E.fill("yo", j, half))

        @block.scalar
        def _(act):
            E = Counts("act_step")
            a = act.activation

            act.dma_start(first, dram["tables"][:, 0:n_first]).then_inc(*E.up("first_in", by=16))
            for g in range(4):
                l, r = g // 2, 0
                for name, n in VEC["AB"[g % 2]]:
                    src = dram[name][l]
                    act.dma_start(rows[r:r + n, g, :], flat(src).rearrange("(r c) -> r c", c=P)).then_inc(*E.up("rows_in", by=16))
                    r += n
                if g == 0:
                    for name, n in SHARED:
                        act.dma_start(rows[r:r + n, g, :], flat(dram[name]).rearrange("(r c) -> r c", c=P)).then_inc(*E.up("rows_in", by=16))
                        r += n
            for j in range(3):
                src = dram["x_prompt"][0] if j == 0 else dram["x_sample"][0][(j - 1) * P:j * P, :]
                act.dma_start(xin[:, j, :], src).then_inc(*E.up("x_in", by=16))
            act.dma_start(second, dram["tables"][:, n_first:ncols]).then_inc(*E.up("second_in", by=16))

            def load_state(l):
                sti = st_in.rearrange("p (d h k) -> p d h k", d=2, h=NH)
                for d in range(2):
                    act.dma_start(sti[0:64, d, :, :], dram["state_rwkv"][0, l, d].rearrange("h v k -> v h k")).then_inc(*E.up("st_in", l, by=16))

            load_state(0)
            act.wait_ge(*filled("vec"))
            for g in range(4):
                n = sum(r for _, r in VEC["AB"[g % 2]]) + (24 if g == 0 else 0)
                ins = a(vec[:, g, 0:n], bank("vec")[:, g * P:g * P + n], ACT.Copy)
                if g == 3:
                    ins.then_inc(*E.read("vec"))
            act.wait_ge(*E.latest())
            for i, name in ((0, "c_ctx"), (1, "c")):
                a(condx[:, :, i], v(name, 0, 0, 8), ACT.Copy).then_inc(*E.step())
                a(cond[:, :, i], v(name, 0, 0, 8), ACT.Sigmoid).then_inc(*E.up("cond_sig", i))
            for k in range(KD):
                act.wait_ge(*filled("xt", k))
                a(xT[:, k, :], bank("xt", k)[:, 0:T], ACT.Copy).then_inc(*E.read("xt", k))

            def ada_copies(l):
                for g in range(3):
                    act.wait_ge(*at("block_used", "ada", l, 4 * g + 3, 1))
                    a(adas[:, g * 512:(g + 1) * 512], psum[4 + g][:, :], ACT.Copy).then_inc(*E.up("ada_copied", l, g))

            def squares(l, which):
                for i in range(2):
                    if which == 1:
                        act.wait_ge(*drained("o", l, 4 * i + 3))
                    elif l == DEPTH:
                        act.wait_ge(*drained("ey", 4 * i + 3))
                    elif l > 0 and i == 0:
                        act.wait_ge(*at("bank_free3", "fdown", l - 1, 3))
                    elif l > 0:
                        act.wait_ge(*at("fdown_done", l - 1))
                    elif i == 0:
                        act.wait_ge(*E.latest())
                    a(sq[:, 4 * i:4 * i + 4, :], xT[:, 4 * i:4 * i + 4, :], ACT.Square).then_inc(*E.up("sq_ready", l, which, i))

            def root(l, which):
                act.wait_ge(*filled("norm", l, which))
                a(rs, bank("norm", l, which)[:, 0:T], ACT.Sqrt, bias=eps[1e-6], scale=1.0 / DM).then_inc(*E.read("norm", l, which))

            def convert(n):
                key, block, raw, _ = pieces[n]
                if n in posted:
                    return
                posted.add(n)
                act.wait_ge(*at(f"block_in{slot_of[block]}", *block))
                if n >= NSLOT:
                    prev, _, _, job = pieces[n - NSLOT]
                    act.wait_ge(*(filled(*job) if job else at("piece_used", *prev)))
                a(w_parts[n % NSLOT][0], raw, ACT.Copy).then_inc(*E.up("rounded_ready", *key))

            posted = set()

            def ahead(*job):
                n = piece_at[job + (1,)]
                for i in range(n + 1, n + NSLOT):
                    if i < len(pieces) and pieces[i][0][:2] in allowed:
                        convert(i)

            allowed = []

            def start_phase(*kinds):
                allowed[:] = kinds
                n = min(i for i, p in enumerate(pieces) if p[0][:2] == kinds[0])
                for i in range(n, n + NSLOT):
                    convert(i)

            def rounded(phase, l, g, src):
                a(h_parts[phase][0][:, 2 * g:2 * g + 2, :], src, ACT.Copy).then_inc(*E.up("x_rounded", phase, l, g))

            def modulate(l, which):
                for k in range(KD):
                    act.wait_ge(*at("xn_ready", l, which, k // 4))
                    for s_, (t0, t1) in enumerate(SEG):
                        ins = a(hT[:, k, t0:t1], hT[:, k, t0:t1], ACT.Identity,
                                bias=mods[:, l, 24 * which + k, s_:s_ + 1], scale=modAs[:, l, which, k, s_:s_ + 1])
                    if k % 2 == 1:
                        ins.then_inc(*E.up("h2_ready" if which else "h_ready", l))
                        if which == 0 or l % 2 == 0:
                            act.wait_ge(*E.latest())
                            rounded("ffn" if which else "z", l, k // 2, hT[:, k - 1:k + 1, :])

            for l in range(DEPTH):
                squares(l, 0)
                if l == 0:
                    ada_copies(0)
                start_phase(("z", l), ("cf", l))
                root(l, 0)
                act.wait_ge(*at("modA_ready", l))
                modulate(l, 0)
                for m in range(NZ):
                    ahead("z", l, m)
                    act.wait_ge(*filled("z", l, m))
                    a(z[:, m, :], bank("z", l, m)[:, 0:T], ACT.Copy).then_inc(*E.read("z", l, m))
                for m in range(6):
                    ahead("cf", l, m)
                    act.wait_ge(*filled("cf", l, m))
                    src = bank("cf", l, m)[:, 0:T]
                    if m < 2:
                        ins = a(cvT[:, m, :], src, ACT.Copy)
                    elif m < 4:
                        ins = a(conv_b[:, m - 2, :], src, ACT.Sigmoid)
                    else:
                        ins = a(fno_u[:, m - 4, :], src, ACT.Copy)
                    ins.then_inc(*E.read("cf", l, m))
                act.wait_ge(*at("mix_done", l))
                a(z[:, 12, :], z[:, 12, :], ACT.Sigmoid).then_inc(*E.up("act_step"))
                a(z[:, 13, :], z[:, 13, :], ACT.Tanh).then_inc(*E.up("low_in_ready", l))
                act.wait_ge(*at("kkp_ready", l))
                a(ksq, kk, ACT.Square).then_inc(*E.up("ksq_ready", l))
                for m in range(NM):
                    act.wait_ge(*filled("kks", l, m))
                    a(tmp4[0][:, m * T:(m + 1) * T], bank("kks", l, m)[:, 0:T], ACT.Sqrt).then_inc(*E.read("kks", l, m))

                def lowrank(d):
                    if d == 0:
                        act.wait_ge(*at("kk_ready", l))
                    else:
                        act.wait_ge(*filled("Y", l, 0, NCP - 1))
                    for which, name in enumerate(("dec_w0", "iclr_a0")):
                        for m in range(NM):
                            act.wait_ge(*filled("low", l, d, which, m))
                            ins = a(tmp4[which][:, m * T:(m + 1) * T], bank("low", l, d, which, m)[:, 0:T], ACT.Sigmoid,
                                    bias=v(name, l, NM * d + m))
                            ins.then_inc(*E.read("low", l, d, which, m))

                def exps(d):
                    act.wait_ge(*at("L_ready", l, d))
                    L = L3(d)
                    tot = tmp4[2].rearrange("p (m c t) -> p m c t", m=NM, c=NC_)[:, :, :, C - 1]
                    a(pc, tot, ACT.Exp, scale=-DECAY).then_inc(*E.step())
                    a(tmp4[0], tmp4[0], ACT.Exp, scale=-DECAY).then_inc(*E.up("E1_ready", l, d))
                    act.wait_ge(*E.latest())
                    a(tmp4[other(d)], tmp4[L], ACT.Exp, scale=-DECAY).then_inc(*E.up("E2_ready", l, d))
                    act.wait_ge(*E.latest())
                    a(tmp4[L], tmp4[L], ACT.Exp, scale=DECAY).then_inc(*E.up("E3_ready", l, d))

                lowrank(0)
                exps(0)
                for m in range(2):
                    act.wait_ge(*filled("fno2", l, m))
                    a(fnT[:, m, :], bank("fno2", l, m)[:, 0:T], ACT.Copy).then_inc(*E.read("fno2", l, m))
                for m in range(2):
                    act.wait_ge(*filled("conv_s", l, m))
                    if m == 0:
                        act.wait_ge(*at("glu_ready", l))
                    a(cvT[:, m, 0:TP], bank("conv", l, m)[:, 0:TP], ACT.Identity, bias=v("dw_b", l, m)).then_inc(*E.read("conv", l, m))
                    a(cvT[:, m, TP:T], bank("conv_s", l, m)[:, 0:TS], ACT.Identity, bias=v("dw_b", l, m)).then_inc(*E.read("conv_s", l, m))
                act.wait_ge(*drained("cln", l, 0))
                a(conv_b, cvT, ACT.Square).then_inc(*E.up("conv_sq", l))
                act.wait_ge(*filled("cln", l, 1))
                a(conv_b[:, 0, :], bank("cln", l, 1)[:, 0:T], ACT.Sqrt, bias=eps[1e-5], scale=1.0 / CC).then_inc(*E.read("cln", l, 1))
                act.wait_ge(*at("conv_affine", l))
                a(conv_b, cvT, ACT.Sigmoid).then_inc(*E.up("conv_sig", l))

                for d in range(2):
                    if d == 1:
                        lowrank(1)
                        exps(1)
                    for cp in range(NCP):
                        for i in range(3 if d == 0 else 2):
                            act.wait_ge(*filled("tok", l, d, cp, i))
                            dst = tok[:, i, cp, :] if i < 2 else vtok[:, cp, :]
                            a(dst, bank("tok", l, d, cp, i)[:, :], ACT.Copy).then_inc(*E.read("tok", l, d, cp, i))
                    for lev in range(LEVELS):
                        for u in range(NCP):
                            act.wait_ge(*filled("X", l, d, lev, u))
                            if lev > 0:
                                act.wait_ge(*filled("TAT", l, d, lev - 1, u))
                            a(Xs[u], bank("X", l, d, lev, u)[:, 0:256], ACT.Copy).then_inc(*E.read("X", l, d, lev, u))
                    for u in range(NCP):
                        act.wait_ge(*filled("XO", l, d, u))
                        act.wait_ge(*filled("TAT", l, d, LEVELS - 1, u))
                        for par in range(2):
                            q = slice(64 * par + 32 * (1 - d), 64 * par + 32 * (2 - d))
                            ins = a(Xs[u][q, :], bank("XO", l, d, u)[q, 0:256], ACT.Copy)
                        ins.then_inc(*E.read("XO", l, d, u))
                    if d == 0 and l + 1 < DEPTH:
                        ada_copies(l + 1)
                    act.wait_ge(*filled("s0", l, d))
                    act.wait_ge(*filled("QO", l, d, NCP - 1))
                    act.wait_ge(*at("St_zero", l))
                    c0 = starts(d)[1]
                    for hh in range(2):
                        r = slice(64 * hh, 64 * hh + 64)
                        ins = a(St[r, c0, :, r], bank("s0", l, d)[r, 0:256].rearrange("p (m v) -> p m v", m=NM), ACT.Copy)
                    ins.then_inc(*E.read("s0", l, d))
                    if d == 1 and l + 1 < DEPTH:
                        load_state(l + 1)
                    for n, c in enumerate(order(d)):
                        q = slice(64 * (c % 2), 64 * (c % 2) + 64)
                        act.wait_ge(*filled("W", l, d, c))
                        if n >= 2:
                            act.wait_ge(*filled("U", l, d, order(d)[n - 2]))
                        a(Wb[n % 2][q, :], bank("W", l, d, c)[q, :], ACT.Copy).then_inc(*E.read("W", l, d, c))
                    if d == 0:
                        if l + 1 < DEPTH:
                            act.wait_ge(*filled("adaT", l + 1, 2))
                        for cp in range(NCP):
                            act.wait_ge(*filled("Y", l, d, cp))
                            a(Y[:, cp, :], bank("Y", l, d, cp)[:, :], ACT.Copy).then_inc(*E.read("Y", l, d, cp))
                    act.wait_ge(*filled("sf", l, d))
                    if (l, d) != (0, 0):
                        act.wait_ge(*at("out_stored", "state", *((l, 0) if d else (l - 1, 1))))
                    so = sout[0:64, :]
                    a(so, bank("sf", l, d)[0:64, :], ACT.Copy).then_inc(*E.read("sf", l, d))
                    act.wait_ge(*E.latest())
                    act.dma_start(new_state[0, l, d].rearrange("h v k -> v h k"), so.rearrange("p (h k) -> p h k", h=NH)).then_inc(*E.up("out_stored", "state", l, d, by=16))
                act.wait_ge(*filled("sf", l, 1))
                act.wait_ge(*filled("Y", l, 1, NCP - 1))
                start_phase(("gate", l), ("o", l))
                for g in range(4):
                    rounded("gate", l, g, hT[:, 2 * g:2 * g + 2, :])
                for b_ in range(3):
                    for m in range(KD):
                        ahead("gate", l, b_, m)
                        act.wait_ge(*filled("gate", l, b_, m))
                        i = b_ * KD + m
                        if i >= 16:
                            act.wait_ge(*at("gated", l, *divmod(i - 8, KD)))
                        elif i >= 8:
                            act.wait_ge(*drained("br", l, 0, m))
                        a(gsig(i), bank("gate", l, b_, m)[:, 0:T], ACT.Sigmoid).then_inc(*E.read("gate", l, b_, m))
                        if i == 1:
                            act.wait_ge(*at("Y_centred", l))
                            a(tmp4[2].rearrange("p (c w) -> p c w", c=NCP), Y, ACT.Square).then_inc(*E.up("Ysq_ready", l))
                        if i == 3:
                            act.wait_ge(*at("Yvar_ready", l))
                            a(stat[:, 24:48], stat[:, 0:24], ACT.Sqrt, bias=eps[64e-5], scale=1.0 / HD).then_inc(*E.up("Ystd_ready", l))
                        if b_ == 2 and m > 0:
                            act.wait_ge(*at("gated", l, 2, m - 1))
                            a(h_parts["merged"][0][:, m - 1, :], merged[m - 1], ACT.Copy).then_inc(*E.up("m_rounded", l, m - 1))
                act.wait_ge(*at("gated", l, 2, KD - 1))
                a(h_parts["merged"][0][:, KD - 1, :], merged[KD - 1], ACT.Copy).then_inc(*E.up("m_rounded", l, KD - 1))
                for m in range(KD):
                    ahead("o", l, m)
                squares(l, 1)
                if l % 2 == 0:
                    start_phase(("fg", l), ("fu", l), ("fd", l))
                root(l, 1)
                modulate(l, 1)
                if l % 2 == 0:
                    for m in range(KF + 1):
                        if m < KF:
                            ahead("fg", l, m)
                            act.wait_ge(*filled("fg", l, m))
                            if m >= 3:
                                act.wait_ge(*drained("fu", l, m - 3))
                            a(fsig[m % 3], bank("fg", l, m)[:, 0:T], ACT.Sigmoid).then_inc(*E.up("fsig_ready", l, m))
                            ahead("fu", l, m)
                        if m > 0:
                            act.wait_ge(*drained("fu", l, m - 1))
                            a(h_parts["prod"][0][:, m - 1, :], fprod[(m - 1) % 3], ACT.Copy)\
                                .then_inc(*E.up("prod_rounded", l, m - 1))
                    for n in phase_pieces(("fd", l)):
                        convert(n)
            act.dma_start(wrt, dram["w_router"][0].rearrange("(k p) e -> p k e", p=P)).then_inc(*E.up("router_in", by=16))
            act.dma_start(brt[0:1, :], dram["b_router"]).then_inc(*E.up("router_in", by=16))
            act.wait_ge(*at("chosen_ready"))
            for i in range(2):
                a(rt[:, R_P + 3 * i:R_P + 3 * i + 3], rt[:, R_D:R_D + 3], ACT.Sigmoid, scale=1.0 if i == 0 else -1.0).then_inc(*E.up("weights_ready", i))
            for k in range(6):
                act.wait_ge(*filled("htok", k))
                flatk = htok.rearrange("p j d -> p (j d)")[:, k * 512:(k + 1) * 512]
                a(flatk, bank("htok", k)[:, :], ACT.Copy).then_inc(*E.read("htok", k))
            s = lambda name: sem(name).h
            act.wait_ge(*at("jobs_ready"))
            act.sem_inc(s("e_hG"), 2)
            act.sem_inc(s("e_ydrained"), 2)
            njobs = act.value_load(rt_i[0:1, 0:1], min_val=NE, max_val=NJOB)
            with act.Fori(0, njobs) as i:
                act.wait_ge(s("e_selT_full"), i + 1)
                act.wait_ge(s("e_sc"), i * 6 + 6)
                a(selT, psum[4][:, 0:3 * P].rearrange("p (j s) -> p j s", j=3), ACT.Copy).then_inc(s("e_selT"), 1)
                for h in range(2):
                    act.wait_ge(s("e_gather"), i * 2 + h + 1)
                    a(hG[:, 4 * h:4 * h + 4, :], psum[6 + h][:, :].rearrange("p (k s) -> p k s", k=4), ACT.Copy)\
                        .then_inc(s("e_hG"), 1)
                for c, (c0, n) in enumerate(CHUNKS):
                    act.wait_ge(s("e_gu"), i * 3 + c + 1)
                    act.wait_ge(s("e_prod"), i * 3 + 3 + c)
                    a(esig[:, 0:n], psum[2 * (c % 2)][:, 0:n], ACT.Sigmoid).then_inc(s("e_sig"), 1)
                    if c > 0:
                        e_copy(act, a, s, psum, eprodT, i, c - 1)
                e_copy(act, a, s, psum, eprodT, i, 2)
                act.wait_ge(s("e_y"), i + 1)
                for half in range(2):
                    a(ey[:, half * 512:(half + 1) * 512], psum[4 + half][:, :], ACT.Copy).then_inc(s("e_ydrained"), 1)
            squares(DEPTH, 0)
            root(DEPTH, 0)
            for j in range(3):
                for half in range(2):
                    act.wait_ge(*filled("yo", j, half))
                    a(htok[:, j, half * 512:(half + 1) * 512], bank("yo", j, half)[:, :], ACT.Copy).then_inc(*E.read("yo", j, half))
                act.wait_ge(*E.latest())
                dst = yp[0] if j == 0 else ys[0][(j - 1) * P:j * P, :]
                act.dma_start(dst, htok[:, j, :]).then_inc(*E.up("out_stored", "y", j, by=16))

        @block.vector
        def _(dve):
            E = Counts("dve_step")
            tt, ts, stt = dve.tensor_tensor, dve.tensor_scalar, dve.scalar_tensor_tensor
            M, A, SUB = ALU.mult, ALU.add, ALU.subtract

            dve.memset(condp, 0.0).then_inc(*E.step())
            dve.wait_ge(*E.latest())
            for i in range(2):
                dve.wait_ge(*at("cond_sig", i))
            tt(condp[:, :, 0:2], cond, condx, M).then_inc(*E.up("cond_ready"))

            def normed(l, which, scale=None):
                dve.wait_ge(*drained("norm", l, which))
                dve.reciprocal(rs, rs).then_inc(*E.step())
                dve.wait_ge(*E.latest())
                dst = hT if scale is None else sq
                if scale is None:
                    for i in range(2):
                        tt(hT[:, 4 * i:4 * i + 4, :], xT[:, 4 * i:4 * i + 4, :],
                                 rs.rearrange("p (a t) -> p a t", a=1).broadcast_to([P, 4, T]), M).then_inc(*E.up("xn_ready", l, which, i))
                else:
                    for k in range(KD):
                        ins = stt(sq[:, k, :], xT[:, k, :], scale(k), rs, M, M)
                        if k < KD - 1:
                            ins.then_inc(*E.step())
                        else:
                            ins.then_inc(*E.up("h_ready", l))

            def residual(job, l, gate, which):
                for m in range(KD):
                    src = bank(*job(m)) if job(m)[0] != "fdown" else psum[m]
                    if job(m)[0] == "fdown":
                        dve.wait_ge(*at("piece_used", "fd", l, KF - 1, m // 4))
                    else:
                        dve.wait_ge(*filled(*job(m)))
                    for s_, (t0, t1) in enumerate(SEG):
                        ins = stt(xT[:, m, t0:t1], src[:, t0:t1], mods[:, l, gate + m, s_:s_ + 1], xT[:, m, t0:t1], M, A)
                        if s_ == 0:
                            ins.then_inc(*E.step())
                    if job(m)[0] == "fdown":
                        if m < 4:
                            ins.then_inc(sem(f"bank_free{m}").h, 1)
                        else:
                            ins.then_inc(*E.up("fdown_done", l))
                    else:
                        ins.then_inc(*E.read(*job(m)))

            def rest(phase, l, g, src):
                dve.wait_ge(*at("x_rounded", phase, l, g))
                xr, xl = (p[:, 2 * g:2 * g + 2, :] for p in h_parts[phase])
                tt(xl, src, xr.bitcast(F32), SUB).then_inc(*E.up("x_parts", phase, l, g))

            def rest_merged(l, m):
                dve.wait_ge(*at("m_rounded", l, m))
                xr, xl = (p[:, m, :] for p in h_parts["merged"])
                ins = tt(xl, merged[m], xr.bitcast(F32), SUB)
                ins.then_inc(*(E.up("x_parts", "merged", l, m // 2) if m % 2 else E.step()))

            def rest_prod(l, m):
                dve.wait_ge(*at("prod_rounded", l, m))
                xr, xl = (p[:, m, :] for p in h_parts["prod"])
                tt(xl, fprod[m % 3], xr.bitcast(F32), SUB).then_inc(*E.up("prod_rest", l, m))

            def modulation(l):
                ba = v("b_ada", l, 0, 48)
                for g in range(3):
                    dve.wait_ge(*filled("adaT", l, g))
                    tb = bank("adaT", l, g)[:, :].rearrange("p (m r) -> p m r", r=32)
                    for s_ in range(2):
                        ins = tt(mods[:, l, 16 * g:16 * g + 16, s_], tb[:, :, s_], ba[:, 16 * g:16 * g + 16], A)
                        if s_ == 0:
                            ins.then_inc(*E.step())
                    ins.then_inc(*E.read("adaT", l, g))
                dve.wait_ge(*E.latest())
                for which, name in ((0, "norm1"), (1, "norm2")):
                    for s_ in range(2):
                        stt(modAs[:, l, which, :, s_], mods[:, l, 24 * which + 8:24 * which + 16, s_], 1.0,
                            v(name, l, 0, 8), A, M).then_inc(*E.up("modA_ready", l))

            for l in range(DEPTH):
                if l == 0:
                    modulation(0)
                dve.wait_ge(*E.latest())
                mu = v("shift_mu", l, 0, NZ)
                ts(mix[:, 0, 0:NZ], mu, -1.0, 1.0, M, A).then_inc(*E.step())
                ts(mix[:, 1, 0:NZ], mu, 0.5, None, M).then_inc(*E.step())
                ts(oneka, v("k_a", l, 0, 4), -1.0, 1.0, M, A).then_inc(*E.step())
                normed(l, 0)
                for g in range(4):
                    rest("z", l, g, hT[:, 2 * g:2 * g + 2, :])
                for g in range(3):
                    full_z = 5 * g + 4
                    dve.wait_ge(*drained('z', l, full_z))
                    for m in range(5 * g, 5 * g + 4):
                        dve.wait_ge(*drained('z', l, m))
                    gs = slice(5 * g, 5 * g + 5)
                    zz, sh = z[:, gs, :], shifted[:, gs, :]
                    tt(sh[:, :, 1:T - 1], zz[:, :, 0:T - 2], zz[:, :, 2:T], A).then_inc(*E.step())
                    dve.wait_ge(*E.latest())
                    dve.tensor_copy(sh[:, :, TP - 1:TP + 1], zz[:, :, TP - 2:TP + 2:3]).then_inc(*E.step())
                    dve.tensor_copy(sh[:, :, 0:T:T - 1], zz[:, :, 1:T - 1:T - 3]).then_inc(*E.step())
                    dve.wait_ge(*E.latest())
                    for m in range(5 * g, 5 * g + 5):
                        ts(z[:, m, :], z[:, m, :], mix[:, 0, m:m + 1], None, M).then_inc(*E.step())
                    dve.wait_ge(*E.latest())
                    for m in range(5 * g, 5 * g + 5):
                        ins = stt(z[:, m, :], shifted[:, m, :], mix[:, 1, m:m + 1], z[:, m, :], M, A)
                        ins.then_inc(*E.up("mix_done", l)) if m == NZ - 1 else ins.then_inc(*E.step())
                dve.wait_ge(*E.latest())
                r_, k_, v_ = z[:, 0:4, :], z[:, 4:8, :], z[:, 8:12, :]
                for m in range(NM):
                    ins = ts(kk[:, m, :], z[:, 4 + m, :], v("k_k", l, m), None, M)
                    ins.then_inc(*E.up("kkp_ready", l)) if m == 3 else ins.then_inc(*E.step())
                dve.wait_ge(*E.latest())
                dve.wait_ge(*at("second_in"))
                for m in range(4):
                    dve.wait_ge(*drained("cf", l, m))
                dve.memset(glu, 0.0).then_inc(*E.step())
                dve.wait_ge(*E.latest())
                for m in range(2):
                    tt(glu[:, m, 15:15 + TP], cvT[:, m, 0:TP], conv_b[:, m, 0:TP], M).then_inc(*E.step())
                    tt(glu[:, m, TP + 30:].rearrange("p (r t) -> p r t", r=4)[:, :, 15:15 + GRID],
                             cvT[:, m, TP:T].rearrange("p (r t) -> p r t", r=4),
                             conv_b[:, m, TP:T].rearrange("p (r t) -> p r t", r=4), M).then_inc(*E.up("glu_ready", l))
                for m in range(NM):
                    dve.wait_ge(*drained('kks', l, m))
                nrm = tmp4[0]
                ts(nrm, nrm, 1e-12, None, ALU.max).then_inc(*E.step()); dve.wait_ge(*E.latest())
                dve.reciprocal(nrm, nrm).then_inc(*E.step()); dve.wait_ge(*E.latest())
                tt(kk, kk, nrm.rearrange("p (m t) -> p m t", m=NM), M).then_inc(*E.up("kk_ready", l))
                for j in range(NCP):
                    dve.wait_ge(*filled("fno1", l, j))
                    dve.tensor_copy(fno_z[:, j, :, :], bank("fno1", l, j)[:, :].rearrange("p (m w) -> p m w", m=2)).then_inc(*E.read("fno1", l, j))

                def prep(d):
                    sg, ag, F3 = tmp4[0], tmp4[1], tmp4[3]
                    for m in range(NM):
                        dve.wait_ge(*drained('low', l, d, 0, m))
                    for m in range(NM):
                        o_ = slice(m * T, (m + 1) * T)
                        dve.tensor_tensor_scan(tmp4[2][:, o_], tab("reset"), sg[:, o_], 0.0, M, A).then_inc(*E.step())
                    dve.wait_ge(*E.latest())
                    cs = tmp4[2]
                    if d == 1:
                        tt(F3, sg, cs, SUB).then_inc(*E.step()); dve.wait_ge(*E.latest())
                        tot = cs.rearrange("p (m c t) -> p m c t", m=NM, c=NC_)
                        for m in range(NM):
                            tt(F3.rearrange("p (m c t) -> p m c t", m=NM, c=NC_)[:, m],
                                      F3.rearrange("p (m c t) -> p m c t", m=NM, c=NC_)[:, m],
                                      tot[:, m, :, C - 1:C].broadcast_to([P, NC_, C]), A).then_inc(*E.step())
                        dve.wait_ge(*E.latest())
                    L = tmp4[L3(d)]
                    tt(sg, L, sg, SUB).then_inc(*E.up("L_ready", l, d))
                    ar = AR.rearrange("p m c k t -> p k m c t")
                    v4 = lambda x: x.rearrange("p (m c t) -> p m c t", m=NM, c=NC_)
                    v3 = lambda x: x.rearrange("p (m t) -> p m t", m=NM)
                    kk4 = kk.rearrange("p m (c t) -> p m c t", c=NC_)
                    for m in range(NM):
                        dve.wait_ge(*drained('low', l, d, 1, m))
                    tt(BK[:, 0], kk, v3(ag), M).then_inc(*E.step())
                    for m in range(NM):
                        ts(BK[:, 1, m, :], v3(ag)[:, m, :], v("k_a", l, m), oneka[:, m:m + 1], M, A).then_inc(*E.step())
                    dve.wait_ge(*E.latest())
                    tt(BK[:, 1], BK[:, 1], k_, M).then_inc(*E.step())
                    dve.wait_ge(*at("E1_ready", l, d))
                    for m in range(NM):
                        stt(ar[:, 0, m], kk4[:, m], -1.0, v4(sg)[:, m], M, M).then_inc(*E.step())
                    dve.wait_ge(*at("E2_ready", l, d))
                    for m in range(NM):
                        tt(ar[:, 1, m], r_[:, m, :].rearrange("p (c t) -> p c t", c=NC_), v4(tmp4[other(d)])[:, m], M).then_inc(*E.step())
                    dve.wait_ge(*at("E3_ready", l, d))
                    dve.wait_ge(*E.latest())
                    tt(BK[:, 0], BK[:, 0], v3(L), M).then_inc(*E.step())
                    tt(BK[:, 1], BK[:, 1], v3(L), M).then_inc(*E.up("ark_ready", l, d))

                dve.wait_ge(*filled("cf", l, 5))
                prep(0)
                dve.wait_ge(*filled("cln", l, 0))
                for m in range(2):
                    ins = stt(cvT[:, m, :], bank("cln", l, 0)[:, 0:T], -1.0 / CC, cvT[:, m, :], M, A)
                    if m == 0:
                        ins.then_inc(*E.step())
                    else:
                        ins.then_inc(*E.read("cln", l, 0))
                dve.wait_ge(*drained('cln', l, 1))
                dve.reciprocal(conv_b[:, 0, :], conv_b[:, 0, :]).then_inc(*E.step()); dve.wait_ge(*E.latest())
                for m in range(2):
                    tt(cvT[:, m, :], cvT[:, m, :], conv_b[:, 0, :], M).then_inc(*E.step())
                dve.wait_ge(*E.latest())
                for m in range(2):
                    ts(cvT[:, m, :], cvT[:, m, :], v("conv_ln_g", l, m), v("conv_ln_b", l, m), M, A).then_inc(*E.up("conv_affine", l))
                dve.wait_ge(*at("conv_sig", l))
                tt(cvT, cvT, conv_b, M).then_inc(*E.up("cv_ready", l))

                for d in range(2):
                    if d == 1:
                        dve.wait_ge(*filled("Y", l, 0, NCP - 1))
                        prep(1)
                    for cp in range(NCP):
                        for hp in range(NH // 2):
                            dve.wait_ge(*filled("pair", l, d, cp, hp))
                            src = bank("pair", l, d, cp, hp)[:, :].rearrange("p (h w) -> p h w", h=2)
                            msk = pair_mask[:, d:d + 1, :].broadcast_to([P, 2, 256])
                            h0 = 4 * (hp // 2) + hp % 2
                            tt(S1[:, cp, h0:h0 + 3:2, :], src, msk, M).then_inc(*E.read("pair", l, d, cp, hp))
                    for u in range(NCP):
                        dve.tensor_copy(TQ[:, u, :, :], tab("eye2").rearrange("p (a w) -> p a w", a=1).broadcast_to([P, NH, C]))\
                            .then_inc(*E.up("TQ_ready", l, d, u))
                    for lev in range(LEVELS):
                        msk = level_mask[:, lev:lev + 1, B * d:B * d + C].bitcast(I32).broadcast_to([P, NH, C])
                        for u in range(NCP):
                            dve.wait_ge(*filled("TAT", l, d, lev, u))
                            src = bank("TAT", l, d, lev, u)[:, :].rearrange("p (h w) -> p h w", h=NH)
                            dve.copy_predicated(TQ[:, u, :, :], msk, src).then_inc(*E.read("TAT", l, d, lev, u))
                    dve.wait_ge(*at("Q_zero", l, d))
                    for u in range(NCP):
                        dve.wait_ge(*filled("QO", l, d, u))
                        for par in range(2):
                            q = slice(64 * par + 32 * d, 64 * par + 32 * d + 32)
                            ins = dve.tensor_copy(Q[q, u, :, (1 - d) * B:(2 - d) * B],
                                                  bank("QO", l, d, u)[q, 0:256].rearrange("p (h w) -> p h w", h=NH))
                        ins.then_inc(*E.read("QO", l, d, u))
                    c0 = starts(d)[0]
                    dve.wait_ge(*at("St_zero", l))
                    dve.memset(St[:, c0, :, :], 0.0).then_inc(*E.up("S_ready", l, d, c0))
                    for c in order(d):
                        cp, par = divmod(c, 2)
                        q = slice(64 * par, 64 * par + 64)
                        dve.wait_ge(*filled("U", l, d, c))
                        dve.tensor_copy(U[q, cp, :, :], bank("U", l, d, c)[q, :].rearrange("p (h v) -> p h v", h=NH)).then_inc(*E.read("U", l, d, c))
                        n = nxt(d, c)
                        if n is None:
                            continue
                        dve.wait_ge(*filled("S", l, d, c))
                        dst = lambda r: Sfin[r, :, :] if n == "end" else St[r, n, :, r]
                        if n == "end" and (l, d) != (0, 0):
                            dve.wait_ge(*filled("sf", *((l, 0) if d else (l - 1, 1))))
                        for r in (slice(0, 64), slice(64, P)):
                            ins = tt(dst(r), bank("S", l, d, c)[r, 0:256].rearrange("p (m v) -> p m v", m=NM), St[r, c, :, r], A)
                        ins.then_inc(*E.read("S", l, d, c))
                        dve.wait_ge(*E.latest())
                        for r in (slice(0, 64), slice(64, P)):
                            ins = tt(dst(r), dst(r), pc[r, :, c:c + 1].broadcast_to([64, NM, HD]), M)
                        if n == "end":
                            ins.then_inc(*E.up("Sfin_ready", l, d))
                        else:
                            ins.then_inc(*E.up("S_ready", l, d, n))
                    if d == 0 and l + 1 < DEPTH:
                        modulation(l + 1)
                    if d == 1:
                        for cp in range(NCP):
                            dve.wait_ge(*filled("Y", l, d, cp))
                            if cp == 0:
                                for i in range(NCP):
                                    dve.wait_ge(*drained('Y', l, 0, i))
                            tt(Y[:, cp, :], Y[:, cp, :], bank("Y", l, d, cp)[:, :], A).then_inc(*E.read("Y", l, d, cp))
                        dve.wait_ge(*E.latest())
                for g in range(4):
                    rest("gate", l, g, hT[:, 2 * g:2 * g + 2, :])
                Yh = Y.rearrange("p c (h v) -> p (c h) v", v=HD)

                def gated(b_, m):
                    dve.wait_ge(*filled("br", l, b_, m))
                    dve.wait_ge(*drained('gate', l, b_, m))
                    g = gsig(b_ * KD + m)
                    dst = merged[m] if b_ == 0 else g
                    tt(dst, g, bank("br", l, b_, m)[:, 0:T], M).then_inc(*E.read("br", l, b_, m))
                    if b_ > 0:
                        dve.wait_ge(*E.latest())
                        tt(merged[m], merged[m], g, A).then_inc(*E.up("gated", l, b_, m))

                dve.tensor_reduce(stat[:, 0:24], Yh, AX.X, A).then_inc(*E.step())
                dve.wait_ge(*E.latest())
                ts(stat[:, 0:24], stat[:, 0:24], 1.0 / HD, None, M).then_inc(*E.step())
                dve.wait_ge(*E.latest())
                tt(Yh, Yh, stat[:, 0:24].rearrange("p (a b) -> p a b", b=1).broadcast_to([P, 24, HD]), SUB)\
                    .then_inc(*E.up("Y_centred", l))
                for m in range(3):
                    gated(0, m)
                dve.wait_ge(*at("Ysq_ready", l))
                dve.tensor_reduce(stat[:, 0:24], tmp4[2].rearrange("p (n v) -> p n v", v=HD), AX.X, A)\
                    .then_inc(*E.up("Yvar_ready", l))
                for m in range(3, 6):
                    gated(0, m)
                dve.wait_ge(*at("Ystd_ready", l))
                dve.reciprocal(stat[:, 24:48], stat[:, 24:48]).then_inc(*E.step())
                dve.wait_ge(*E.latest())
                tt(Yh, Yh, stat[:, 24:48].rearrange("p (a b) -> p a b", b=1).broadcast_to([P, 24, HD]), M)\
                    .then_inc(*E.up("yn_ready", l))
                for m in range(6, KD):
                    gated(0, m)
                for m in range(NM):
                    o_ = tmp4[1][:, m * T:(m + 1) * T]
                    ins = stt(o_, z[:, m, :], v("r_k", l, m), z[:, 4 + m, :], M, M)
                    ins.then_inc(*E.up("rk_ready", l)) if m == 3 else ins.then_inc(*E.step())
                for m in range(KD):
                    gated(1, m)
                for cp in range(NCP):
                    dve.wait_ge(*filled("yt", l, cp))
                    for m in range(NM):
                        ins = ts(yT[:, m, cp * P:(cp + 1) * P], bank("yt", l, cp)[:, m * P:(m + 1) * P],
                                 v("gn_g", l, m), v("gn_b", l, m), M, A)
                        if m < 3:
                            ins.then_inc(*E.step())
                    ins.then_inc(*E.read("yt", l, cp))
                for m in range(NM):
                    dve.wait_ge(*filled("bon", l, m))
                    tt(tmp4[2][:, m * T:(m + 1) * T], bank("bon", l, m)[:, 0:T], z[:, 8 + m, :], M).then_inc(*E.read("bon", l, m))
                dve.wait_ge(*E.latest())
                tt(yT, yT, tmp4[2].rearrange("p (m t) -> p m t", m=NM), A).then_inc(*E.step()); dve.wait_ge(*E.latest())
                for m in range(NM):
                    dve.wait_ge(*filled("gup", l, m))
                    tt(yT[:, m, :], yT[:, m, :], bank("gup", l, m)[:, 0:T], M).then_inc(*E.read("gup", l, m))
                for m in range(KD):
                    gated(2, m)
                    if m > 0:
                        rest_merged(l, m - 1)
                rest_merged(l, KD - 1)
                residual(lambda m: ("o", l, m), l, 16, 1)
                normed(l, 1)
                if l % 2 == 0:
                    for g in range(4):
                        rest("ffn", l, g, hT[:, 2 * g:2 * g + 2, :])
                    for m in range(KF):
                        dve.wait_ge(*at("fsig_ready", l, m))
                        dve.wait_ge(*filled("fg", l, m))
                        tt(fsig[m % 3], fsig[m % 3], bank("fg", l, m)[:, 0:T], M).then_inc(*E.read("fg", l, m))
                        dve.wait_ge(*E.latest())
                        dve.wait_ge(*filled("fu", l, m))
                        if m >= 3:
                            dve.wait_ge(*at("prod_rest", l, m - 3))
                        tt(fprod[m % 3], fsig[m % 3], bank("fu", l, m)[:, 0:T], M).then_inc(*E.read("fu", l, m))
                        if m > 0:
                            rest_prod(l, m - 1)
                    rest_prod(l, KF - 1)
                    residual(lambda m: ("fdown", l, m), l, 40, 2)
            dve.wait_ge(*filled("logit"))
            lg = rt[:, R_LG:R_LG + 24]
            dve.tensor_copy(lg, bank("logit")[:, 0:24]).then_inc(*E.read("logit")); dve.wait_ge(*E.latest())
            for j in range(3):
                dve.max(rt[:, R_MX + 8 * j:R_MX + 8 * j + 8], lg[:, 8 * j:8 * j + 8]).then_inc(*E.step())
            dve.wait_ge(*E.latest())
            for j in range(3):
                dve.max_index(rt[:, R_IX + 8 * j:R_IX + 8 * j + 8].bitcast(U32), rt[:, R_MX + 8 * j:R_MX + 8 * j + 8],
                                     lg[:, 8 * j:8 * j + 8]).then_inc(*E.step())
            mx = rt[:, R_MX:R_MX + 24].rearrange("p (j e) -> p j e", j=3)
            tt(rt[:, R_D:R_D + 3], mx[:, :, 0], mx[:, :, 1], SUB).then_inc(*E.step())
            dve.wait_ge(*E.latest())
            dve.tensor_copy(rt[:, R_IF:R_IF + 24], rt[:, R_IX:R_IX + 24].bitcast(U32)).then_inc(*E.step()); dve.wait_ge(*E.latest())
            code8 = tab("code")[:, 0:NE]
            for j in range(3):
                for i in range(2):
                    ts(rt[:, R_OH + 24 * i + 8 * j:R_OH + 24 * i + 8 * j + 8], code8,
                              rt[:, R_IF + 8 * j + i:R_IF + 8 * j + i + 1], None, ALU.is_equal).then_inc(*E.step())
            dve.wait_ge(*E.latest())
            tt(rt[:, 0:24], rt[:, R_OH:R_OH + 24], rt[:, R_OH + 24:R_OH + 48], A).then_inc(*E.up("chosen_ready"))
            for i in range(2):
                dve.wait_ge(*at("weights_ready", i))
            for j in range(3):
                o_ = rt[:, R_OH + 8 * j:R_OH + 8 * j + 8]
                ts(o_, o_, rt[:, R_P + j:R_P + j + 1], None, M).then_inc(*E.step())
            dve.wait_ge(*E.latest())
            for j in range(3):
                for t in range(3):
                    stt(rt[:, R_CW + 24 * j + 8 * t:R_CW + 24 * j + 8 * t + 8],
                               rt[:, R_OH + 24 + 8 * j:R_OH + 24 + 8 * j + 8], rt[:, R_P + 3 + j:R_P + 4 + j],
                               rt[:, R_OH + 8 * j:R_OH + 8 * j + 8], M, A).then_inc(*E.step())
            dve.wait_ge(*filled("rank"))
            rk = rt[:, R_RK:R_RK + 24]
            stt(rk, bank("rank")[:, 0:24], 1.0, rt[:, 0:24], A, M).then_inc(*E.step())
            cnt = rt[:, R_CNT:R_CNT + 8]
            dve.tensor_copy(cnt, bank("rank")[:, 24:32]).then_inc(*E.read("rank")); dve.wait_ge(*E.latest())
            for j in range(3):
                for t in range(3):
                    ts(rt[:, R_SL + 24 * j + 8 * t:R_SL + 24 * j + 8 * t + 8], rk[:, 8 * j:8 * j + 8],
                              -1.0 - P * t, None, A).then_inc(*E.step())
            fl = rt[:, R_FL:R_FL + 16]
            for t in range(2):
                ts(fl[:, 8 * t:8 * t + 8], cnt, float(P * (t + 1)), None, ALU.is_gt).then_inc(*E.step())
            dve.wait_ge(*E.latest())
            dve.tensor_tensor_scan(rt[:, R_PS:R_PS + 16], ones[:, 0:16], fl, 0.0, M, A).then_inc(*E.step()); dve.wait_ge(*E.latest())
            tt(rt[:, R_PS:R_PS + 16], rt[:, R_PS:R_PS + 16], fl, M).then_inc(*E.step())
            jl = rt[:, R_JL:R_JL + 17]
            dve.wait_ge(*E.latest())
            dve.tensor_reduce(jl[:, 0:1], rt[:, R_PS:R_PS + 16], AX.X, ALU.max).then_inc(*E.step()); dve.wait_ge(*E.latest())
            ts(jl[:, 0:1], jl[:, 0:1], float(NE), None, A).then_inc(*E.step())
            dve.tensor_copy(jl[:, 1:9], code8).then_inc(*E.step())
            for q in range(8):
                o_ = rt[:, R_TM + 16 * q:R_TM + 16 * q + 16]
                stt(o_, rt[:, R_PS:R_PS + 16], float(q + 1), tab("code")[:, 8:24], ALU.is_equal, M).then_inc(*E.step())
            dve.wait_ge(*E.latest())
            dve.tensor_reduce(jl[:, 9:17], rt[:, R_TM:R_TM + 128].rearrange("p (q i) -> p q i", q=8), AX.X, A).then_inc(*E.step()); dve.wait_ge(*E.latest())
            t1 = rt[:, R_TM:R_TM + 17]
            ts(t1, jl, float(NE), -float(NE), ALU.is_ge, M).then_inc(*E.step())
            ts(rt[:, R_TM + 32:R_TM + 49], jl, float(2 * NE), -float(NE), ALU.is_ge, M).then_inc(*E.step()); dve.wait_ge(*E.latest())
            tt(t1, t1, rt[:, R_TM + 32:R_TM + 49], A).then_inc(*E.step()); dve.wait_ge(*E.latest())
            tt(t1, t1, jl, A).then_inc(*E.step()); dve.wait_ge(*E.latest())
            dve.tensor_copy(rt_i[:, 1:17], t1[:, 1:17]).then_inc(*E.step())
            dve.tensor_copy(rt_i[:, 0:1], jl[:, 0:1]).then_inc(*E.step())
            dve.tensor_copy(rt_i[:, 17:34], jl).then_inc(*E.up("jobs_ready"))
            for k in range(6):
                dve.wait_ge(*drained('htok', k))
            s = lambda name: sem(name).h
            dve.memset(yacc, 0.0).then_inc(*E.step())
            dve.wait_ge(*E.latest())
            dve.sem_inc(s("e_prod"), 3)
            dve.sem_inc(s("e_sc_done"), 6)
            njobs = dve.value_load(rt_i[0:1, 0:1], min_val=NE, max_val=NJOB)
            with dve.Fori(0, njobs) as i:
                code = dve.value_load(rt_i[0:1, bass.ds(i + 18, 1)], min_val=0, max_val=NCODE - 1)
                dve.wait_ge(s("e_hG"), i * 2 + 2)
                for j in range(3):
                    slot = rt[:, bass.ds(code + (R_SL + 24 * j), 1)]
                    w = rt[:, bass.ds(code + (R_CW + 24 * j), 1)]
                    ts(sel[:, j, :], iota, slot, None, ALU.is_equal)
                    ins = ts(selc[:, j, :], iota, slot, w, ALU.is_equal, M)
                ins.then_inc(s("e_sel"), 1)
                for c, (c0, n) in enumerate(CHUNKS):
                    dve.wait_ge(s("e_sig"), i * 3 + c + 1)
                    if c == 0:
                        dve.wait_ge(s("e_sc"), i * 6 + 6)
                    tt(esig[:, 0:n], esig[:, 0:n], psum[2 * (c % 2)][:, 0:n], M).then_inc(s("e_silu"), 1)
                    dve.wait_ge(s("e_silu"), i * 3 + c + 1)
                    tt(eprod[:, c0:c0 + n], esig[:, 0:n], psum[2 * (c % 2) + 1][:, 0:n], M).then_inc(s("e_prod"), 1)
                for n_ in range(6):
                    j, half = divmod(n_, 2)
                    dve.wait_ge(s("e_sc"), i * 6 + 6 + n_ + 1)
                    if n_ == 0:
                        dve.wait_ge(s("e_sc_done"), i * 6 + 6)
                    dst = yacc[:, j, half * 512:(half + 1) * 512]
                    tt(dst, dst, psum[6 + half][:, :], A).then_inc(s("e_sc_done"), 1)
            dve.tensor_copy(stat[:, 84:85], ident[:, 0:1]).then_inc(*E.up("yacc_ready"))
            residual(lambda m: ("ey", m), 1, 40, 2)
            normed(DEPTH, 0, lambda k: v("final_norm", 0, k))

        @block.gpsimd
        def _(pool):
            E = Counts("pool_step")

            def rests(*kinds):
                for n in phase_pieces(*kinds):
                    key, _, raw, _ = pieces[n]
                    pool.wait_ge(*at("rounded_ready", *key))
                    wr, wl = w_parts[n % NSLOT]
                    pool.tensor_tensor(wl, raw, wr.bitcast(F32), ALU.subtract).then_inc(*E.up("rest_ready", *key))

            for l in range(DEPTH):
                rests(("z", l), ("cf", l))
                pool.wait_ge(*filled("cf", l, 5))
                pool.memset(St, 0.0).then_inc(*E.up("St_zero", l))
                if l == 0:
                    pool.wait_ge(*drained('vec'))
                pool.wait_ge(*at("mix_done", l))
                for i in range(2 * CONV_W):
                    m, j = divmod(i, CONV_W)
                    if i >= 8 and (i - 8) % CONV_W == CONV_W - 1:
                        pool.wait_ge(*filled("conv_s", l, (i - 8) // CONV_W))
                    elif i >= 8:
                        pool.wait_ge(*at("diag_used", l, i - 8))
                    pool.tensor_scalar(diag[i % 8], ident, v("dw_w", l, 2 * j + m), None, ALU.mult).then_inc(*E.up("diag_ready", l, i))
                for d in range(2):
                    pool.wait_ge(*filled("pair", l, d, NCP - 1, NH // 2 - 1))
                    pool.memset(Q, 0.0).then_inc(*E.up("Q_zero", l, d))
                    pool.wait_ge(*E.latest())
                    for u in range(NCP):
                        pool.wait_ge(*drained("TAT", l, d, LEVELS - 1, u))
                    for g in range(4):
                        q = slice(32 * g, 32 * g + 32)
                        c0 = (g % 2) * B
                        pool.tensor_copy(Q[q, :, :, c0:c0 + B], TQ[q, :, :, B:C]).then_inc(*E.up("Qdiag_ready", l, d))
                rests(("gate", l), ("o", l))
                if l % 2 == 0:
                    rests(("fg", l), ("fu", l), ("fd", l))


_INS = ["x_prompt", "x_sample", "state_rwkv", "c", "c_ctx", "norm1", "norm2", "w_ada", "b_ada", "w_in",
        "dw_w", "dw_b", "conv_ln_g", "conv_ln_b", "w_conv_out", "w_fno_out", "shift_mu", "g_up",
        "dec_w0", "dec_up", "iclr_a0", "iclr_up", "k_k", "k_a", "r_k", "gn_g", "gn_b", "w_rwkv_out", "w_o",
        "ffn_w_gate", "ffn_w_up", "ffn_w_down", "w_router", "b_router",
        "moe_w_gate", "moe_w_up", "moe_w_down", "final_norm"]
_OUTS = [(1, TP, DM), (1, TS, DM), (1, DEPTH, 2, NH, HD, HD)]


def kernel(**inputs):
    import concourse.bacc as bacc
    from concourse.bass_utils import run_bass_kernel_spmd as run

    arrays = {n: np.ascontiguousarray(inputs[n]) for n in _INS}
    arrays["tables"] = np.concatenate(list(tables().values()), 1)
    marks = {}
    for _ in range(2):
        nc = bacc.Bacc("TRN2", target_bir_lowering=False, num_devices=1)
        dram = {n: nc.dram_tensor(f"in_{n}", a.shape, F32, kind="ExternalInput").ap() for n, a in arrays.items()}
        outs = [nc.dram_tensor(f"out_{i}", s, F32, kind="ExternalOutput").ap() for i, s in enumerate(_OUTS)]
        build(nc, dram, outs, marks)
    r = run(nc, [{f"in_{n}": a for n, a in arrays.items()}], core_ids=[0])
    return tuple(r.results[0][f"out_{i}"] for i in range(len(_OUTS)))
```

```python
from contextlib import ExitStack

import numpy as np
import concourse.bass as bass
from concourse import mybir

P = 128
DM, DEPTH = 1024, 2
TP, TS = 128, 256
T = TP + TS
SEG = ((0, TP), (TP, T))
KD = DM // P
GRID, CONV_W = 64, 31
CC, CF, CR = 256, 256, 512
HD, NH = 64, 8
NM = CR // P
C = 64
NC_ = T // C
NCP = T // P
B = C // 2
LEVELS = 5
NZ = 15
OFF_Z, OFF_G = 768, 2688
DFF, KF = 2816, 22
NE, DE, KE = 8, 1408, 11
CHUNKS = ((0, 512), (512, 512), (1024, 384))
DOWN = ((0, 4), (4, 4), (8, 3))
E_PIECES = [(which, 2 * k, 2, c0, n) for c0, n in CHUNKS for which in ("moe_w_gate", "moe_w_up") for k in range(KD // 2)]
E_PIECES += [("moe_w_down", k, 1, 0, DM) for k in range(KE - 1)]
E_PIECES += [("moe_w_down", KE - 1, 1, h * DM // 2, DM // 2) for h in range(2)]
NPC = len(E_PIECES)
E_RAW, E_PARTS = NPC // 2, 4
assert NPC % E_RAW == 0 and NPC % E_PARTS == 0
CHUNK_PIECES = KD
NCODE = 3 * NE
NJOB = 16
DECAY = float(np.exp(-0.5))

F32 = mybir.dt.float32
FILL = 4
F32R = mybir.dt.float32r
I32 = mybir.dt.int32
U32 = mybir.dt.uint32
ALU = mybir.AluOpType
ACT = mybir.ActivationFunctionType
AX = mybir.AxisListType


def tables():
    i = np.arange(P)
    out = {}
    out["ident"] = np.eye(P)
    out["ones"] = np.ones((P, P))
    out["before"] = (i[:, None] < i[None, :]) * 1.0
    out["iota"] = np.tile(np.arange(P), (P, 1))
    out["code"] = np.tile(np.arange(24), (P, 1))
    out["eps"] = np.tile(np.array([1e-6, 1e-5, 64e-5, 0.0]), (P, 1))
    out["heads"] = (i[:, None] // HD == i[None, :] // HD) * 1.0
    c = np.arange(HD)
    ang = 2 * np.pi * (np.outer(c, c) % HD) / HD
    for name, m in (("dft_c", np.cos(ang)), ("dft_s", np.sin(ang))):
        out[name] = np.kron(np.eye(2), m)
    for name, n in (("p", TP), ("s", TS)):
        t = np.arange(n)
        ang = 2 * np.pi * (np.outer(t, t) % n) / n
        scale = 1.0 / np.sqrt(n * HD)
        both = np.stack([np.cos(ang), -np.sin(ang)]) * scale
        out["time_" + name] = both.reshape(2, n // P, P, n).transpose(2, 1, 0, 3).reshape(P, -1)
    s, t = np.arange(C)[:, None], np.arange(C)[None, :]
    both = []
    for strict in (s < t, s > t):
        incl = strict | (s == t)
        both.append(np.concatenate([strict, incl, strict, incl], 1))
    out["pair_mask"] = np.tile(np.concatenate(both, 1), (2, 1))
    lev = []
    s, t = s[:B], t[:, :B]
    for m in range(LEVELS):
        b = 1 << m
        low = (s // (2 * b) == t // (2 * b)) & (s // b > t // b)
        lev += [low, low.T, low]
    out["level_mask"] = np.tile(np.concatenate(lev, 1), (4, 1))
    out["eye2"] = np.tile(np.eye(B), (4, 2))
    out["reset"] = np.tile(np.arange(T) % C != 0, (P, 1))
    return {k: np.asarray(v, np.float32) for k, v in out.items()}


FIRST = ("ident", "ones", "before", "iota", "code", "eps")


def table_columns():
    at, n = {}, 0
    for k, v in tables().items():
        at[k] = (n, v.shape[1])
        n += v.shape[1]
    return at, n


VEC = {
    "A": (("dw_w", 62), ("dw_b", 2), ("conv_ln_g", 2), ("conv_ln_b", 2), ("norm1", 8), ("norm2", 8)),
    "B": (("b_ada", 48), ("shift_mu", 15), ("dec_w0", 8), ("iclr_a0", 8), ("k_k", 4), ("k_a", 4),
          ("r_k", 4), ("gn_g", 4), ("gn_b", 4)),
}
SHARED = (("final_norm", 8), ("c", 8), ("c_ctx", 8))


R_LG, R_MX, R_IX, R_IF, R_D, R_P, R_OH = 24, 48, 72, 96, 120, 124, 132
R_CW, R_RK, R_CNT, R_SL, R_FL, R_PS, R_JL, R_TM = 180, 252, 276, 284, 356, 372, 388, 408


def order(d):
    return (0, 2, 1, 3, 4, 5) if d == 0 else (1, 5, 0, 4, 3, 2)


def steps(d):
    c = order(d)
    return (((0, c[0]), (1, c[1])), ((2, c[2]), (3, c[3])), ((4, c[4]),), ((5, c[5]),))


def starts(d):
    return (0, 2) if d == 0 else (1, 5)


def nxt(d, c):
    n = c + 1 if d == 0 else c - 1
    if d == 0:
        return "end" if c == 1 else None if c == 5 else n
    return "end" if c == 0 else None if c == 2 else n


def L3(d):
    return 2 if d == 0 else 3


def other(d):
    return 5 - L3(d)


def flat(ap):
    return ap if len(ap.shape) == 1 else ap.rearrange("a b -> (a b)")


def e_rester(n):
    name = "pool" if n % 3 == 2 else "dve"
    return f"e_rest_{name}", sum((m % 3 == 2) == (name == "pool") for m in range(n))


E_EACH = {name: sum(e_rester(n)[0] == name for n in range(NPC)) for name in ("e_rest_pool", "e_rest_dve")}


def e_transposes(pe, s, transpose, psum, eprod, i, c):
    pe.wait_ge(s("e_prod"), i * 3 + 3 + c + 1)
    if c == 2:
        pe.wait_ge(s("e_pT_rest"), i * 3 + 1)
    k0, kn = DOWN[c]
    for k in range(kn):
        last = transpose(psum[6 + c % 2][:, k * P:(k + 1) * P], eprod[:, (k0 + k) * P:(k0 + k + 1) * P])
    last.then_inc(s("e_pT_full"), 1)


def e_turned(psum, parts_, c):
    k0, kn = DOWN[c]
    src = psum[6 + c % 2][:, 0:kn * P].rearrange("p (k s) -> p k s", k=kn)
    return (src,) + tuple(p[:, k0:k0 + kn, :] for p in parts_)


def e_rest(eng, s, e_raw, e_w, i, n):
    _, _, kn, _, w = E_PIECES[n]
    eng.wait_ge(s("e_rounded"), i * NPC + n + 1)
    wr, wl = (p[:, 0:kn * w] for p in e_w[n % E_PARTS])
    eng.tensor_tensor(wl, e_raw[n % E_RAW][:, 0:kn * w], wr.bitcast(F32), ALU.subtract).then_inc(s(e_rester(n)[0]), 1)


def build(nc, dram, outs, marks):
    yp, ys, new_state = outs
    tcol, ncols = table_columns()

    with ExitStack() as ctx:
        TOTAL = 52992 - 80
        base = (nc.sbuf_base + 31) // 32 * 32
        ctx.enter_context(nc.sbuf_tensor("arena", [P, TOTAL], F32))
        psum = [ctx.enter_context(nc.psum_tensor(f"bank{i}", [P, 512], F32)) for i in range(8)]
        used = {}

        def cut(name, start, n):
            used[name] = (start, start + n)
            assert start + n <= TOTAL, (name, start + n)
            return nc.alloc_sbuf_tensor_at(name, [P, n], F32, offset=base + 4 * start, align_bytes=4)[:, :]

        def parts(name, w, k, *starts):
            return [nc.alloc_sbuf_tensor_at(f"{name}_{part}", [P, k * w], F32R, offset=base + 4 * start, align_bytes=4)[:, :]
                    .rearrange("p (k t) -> p k t", k=k) for part, start in zip(("rounded", "rest"), starts)]

        n_first = sum(tcol[k][1] for k in FIRST)
        o = 0
        xT = cut("xT", o, KD * T).rearrange("p (k t) -> p k t", k=KD); o += KD * T
        first = cut("first", o, n_first); o += n_first
        vec = cut("vec", o, 4 * P).rearrange("p (g c) -> p g c", g=4); o += 4 * P
        mods = cut("mods", o, 96 * DEPTH).rearrange("p (l m s) -> p l m s", l=DEPTH, s=2); o += 96 * DEPTH
        modAs = cut("modAs", o, 32 * DEPTH).rearrange("p (l w k s) -> p l w k s", l=DEPTH, w=2, s=2); o += 32 * DEPTH
        condp = cut("condp", o, 32 * KD).rearrange("p (k s) -> p k s", s=32); o += 32 * KD
        cond = cut("cond", o, 16).rearrange("p (k s) -> p k s", s=2); o += 16
        condx = cut("condx", o, 16).rearrange("p (k s) -> p k s", s=2); o += 16
        mix = cut("mix", o, 32).rearrange("p (w z) -> p w z", w=2); o += 32
        oneka = cut("oneka", o, 4); o += 4
        pc = cut("pc", o, 24).rearrange("p (m c) -> p m c", m=NM); o += 24
        stat = cut("stat", o, 96); o += 96
        hT = cut("hT", o, KD * T).rearrange("p (k t) -> p k t", k=KD); o += KD * T
        low_end = o
        second = cut("second", o, ncols - n_first); o += ncols - n_first
        RING, SLOT = 6, 4 * 256
        ring = [cut(f"ring{i}", o + i * SLOT, SLOT) for i in range(RING)]; o += RING * SLOT
        low = cut("low", o, 3 * CR).rearrange("p (w c) -> p w c", w=3); o += 3 * CR
        z = cut("z", o, NZ * T).rearrange("p (m t) -> p m t", m=NZ)
        rows = cut("rows", o, 4 * P).rearrange("p (g c) -> p g c", g=4)
        o += NZ * T
        cvT = cut("cvT", o, 2 * T).rearrange("p (m t) -> p m t", m=2); o += 2 * T
        fnT = cut("fnT", o, 2 * T).rearrange("p (m t) -> p m t", m=2); o += 2 * T
        kk = cut("kk", o, NM * T).rearrange("p (m t) -> p m t", m=NM); o += NM * T
        ffn_at = o
        AR = cut("AR", o, 2 * NM * T).rearrange("p (m c k t) -> p m c k t", m=NM, c=NC_, k=2)
        ksq = cut("ksq", o, NM * T).rearrange("p (m t) -> p m t", m=NM)
        o += 2 * NM * T
        BK = cut("BK", o, 2 * NM * T).rearrange("p (k m t) -> p k m t", k=2, m=NM)
        TQ = cut("TQ", o, 24 * C).rearrange("p (c h w) -> p c h w", c=NCP, h=NH)
        U = cut("U", o, 24 * C).rearrange("p (c h w) -> p c h w", c=NCP, h=NH)
        Q = cut("Q", o + 24 * C, 24 * C).rearrange("p (c h w) -> p c h w", c=NCP, h=NH)
        yT = cut("yT", o, NM * T).rearrange("p (m t) -> p m t", m=NM)
        o += 2 * NM * T
        S1 = cut("S1", o, 24 * 256).rearrange("p (c h w) -> p c h w", c=NCP, h=NH)
        tmp4 = [cut(f"tmp{i}", o + i * NM * T, NM * T) for i in range(4)]
        adas = cut("adas", o + NM * T, NM * T)
        shifted = cut("shifted", o, NZ * T).rearrange("p (m t) -> p m t", m=NZ)
        o += 24 * 256
        tok = cut("tok", o, 2 * NCP * CR).rearrange("p (k c w) -> p k c w", k=2, c=NCP)
        fno_u = cut("fno_u", o, 2 * T).rearrange("p (m t) -> p m t", m=2)
        fno_z = cut("fno_z", o + 2 * T, NCP * 512).rearrange("p (j m w) -> p j m w", j=NCP, m=2)
        sq = cut("sq", o, KD * T).rearrange("p (k t) -> p k t", k=KD)
        xin = cut("xin", o, 3 * DM).rearrange("p (j d) -> p j d", j=3)
        o += 2 * NCP * CR
        PADC = TP + 30 + 4 * (GRID + 30)
        glu = cut("glu", o, 2 * PADC).rearrange("p (m t) -> p m t", m=2)
        diag = [cut(f"diag{i}", o + 2 * PADC + i * P, P) for i in range(3)]
        assert 2 * PADC + 3 * P <= NCP * CR
        vtok = cut("vtok", o, NCP * CR).rearrange("p (c w) -> p c w", c=NCP); o += NCP * CR
        conv_b = cut("conv_b", o, 2 * T).rearrange("p (m t) -> p m t", m=2)
        diag += [cut(f"diag{3 + i}", o + 2 * T + i * P, P) for i in range(5)]
        Y = cut("Y", o, NCP * CR).rearrange("p (c w) -> p c w", c=NCP); o += NCP * CR
        St = cut("St", o, NC_ * 512).rearrange("p (c m v) -> p c m v", c=NC_, m=NM); o += NC_ * 512
        Sfin = cut("Sfin", o, 256).rearrange("p (m v) -> p m v", m=NM); o += 256
        XW = o
        Wb = [cut(f"Wb{i}", o + 512 * i, 512) for i in range(2)]
        Xs = [cut(f"Xs{i}", o + 256 * i, 256) for i in range(3)]
        rs = cut("rs", o, T); o += 1024
        st_in = cut("st_in", o, 1024); o += 1024
        sout = cut("sout", o, 512); o += 512
        fsig = [cut(f"fsig{i}", ffn_at + KF * T + i * T, T) for i in range(3)]
        fprod = [cut(f"fprod{i}", ffn_at + KF * T + (3 + i) * T, T) for i in range(3)]
        assert ffn_at + (KF + 6) * T <= used["tok"][0] and used["kk"][1] - used["z"][0] >= KF * T
        assert o <= TOTAL, o
        at_ = lambda name: used[name][0]
        merged = [cut(f"merged{k}", at_("Q") + k * T if k < 4 else at_("kk") + (k - 4) * T, T) for k in range(KD)]
        h_parts = {
            "z": parts("h1", T, KD, at_("AR"), at_("BK")),
            "gate": parts("hg", T, KD, at_("AR"), at_("tok")),
            "ffn": parts("h2", T, KD, at_("tok"), at_("vtok")),
            "merged": parts("merged", T, KD, at_("z"), at_("z") + KD * T),
            "prod": parts("prod", T, KF, at_("z"), ffn_at),
        }
        assert at_("z") + 2 * KD * T <= used["cvT"][1]
        NSLOT = 3
        w_parts = [parts(f"weights{i}", P, 4, at_("St") + 1024 * i, at_("St") + 1024 * i + 512) for i in range(NSLOT)]
        o = low_end
        htok = cut("htok", o, 3 * DM).rearrange("p (j d) -> p j d", j=3); o += 3 * DM
        hG = parts("hG", P, KD, o, o + DM); o += 2 * DM
        eprod = cut("eprod", o, DE)
        ey = cut("ey", o, DM); o += DE
        eprodT = parts("eprodT", P, KE, o, o + DE); o += 2 * DE
        sel = cut("sel", o, 3 * P).rearrange("p (j s) -> p j s", j=3); o += 3 * P
        selc = cut("selc", o, 3 * P).rearrange("p (j s) -> p j s", j=3); o += 3 * P
        selT = cut("selT", o, 3 * P).rearrange("p (j s) -> p j s", j=3); o += 3 * P
        esig = cut("esig", o, 512); o += 512
        rt = cut("rt", o, 900); o += 900
        rt_i = rt[:, 560:600].bitcast(I32)
        wrt = cut("wrt", o, 64).rearrange("p (k e) -> p k e", k=KD); o += 64
        brt = cut("brt", o, 8); o += 8
        yacc = cut("yacc", used["hT"][0], 3 * DM).rearrange("p (j d) -> p j d", j=3)
        o = (o + 7) // 8 * 8
        e_raw = [cut(f"e_raw{i}", o + i * DM, DM) for i in range(E_RAW)]; o += E_RAW * DM
        e_w = [[p[:, 0, :] for p in parts(f"e_w{i}", DM, 1, o + 2 * i * DM, o + (2 * i + 1) * DM)] for i in range(E_PARTS)]
        assert o + 2 * E_PARTS * DM <= TOTAL

        def tab(name):
            a, n = tcol[name]
            return first[:, a:a + n] if name in FIRST else second[:, a - n_first:a - n_first + n]

        ident, ones, heads, before, iota = (tab(k) for k in ("ident", "ones", "heads", "before", "iota"))
        pair_mask = tab("pair_mask").rearrange("p (d w) -> p d w", d=2)
        level_mask = tab("level_mask").rearrange("p (l w) -> p l w", l=LEVELS)
        time_p = tab("time_p").rearrange("p (j k n) -> p j k n", j=1, k=2)
        time_s = tab("time_s").rearrange("p (j k n) -> p j k n", j=2, k=2)
        eps = {v: tab("eps")[:, i:i + 1] for i, v in enumerate((1e-6, 1e-5, 64e-5))}

        vat = {}
        for l in range(DEPTH):
            for gi, g in enumerate("AB"):
                r = 0
                for name, n in VEC[g]:
                    vat[name, l] = (2 * l + gi, r)
                    r += n
                if g == "A" and l == 0:
                    for name, n in SHARED:
                        vat[name, 0] = (0, r)
                        r += n

        def v(name, l, i=0, n=1):
            g, r = vat[name, l]
            return vec[:, g, r + i:r + i + n]

        def gsig(i):
            return tmp4[3 if i % 8 >= 4 else 0][:, (i % 4) * T:(i % 4 + 1) * T]

        sems = {}

        class Sem:
            def __init__(self, name):
                self.h, self.n = ctx.enter_context(nc.semaphore(name)), 0

        def sem(name):
            if name not in sems:
                sems[name] = Sem(name)
            return sems[name]

        def at(name, *key):
            return sem(name).h, marks.get((name,) + key, 1)

        class Counts:

            def __init__(self, steps):
                self.steps = steps

            def up(self, name, *key, by=1):
                s = sem(name)
                s.n += by
                marks[(name,) + key] = s.n
                if by == 1:
                    self.last = (s.h, s.n)
                return s.h, by

            def step(self):
                return self.up(self.steps)

            def read(self, *job):
                name = f"bank_free{marks.get(('bank',) + job, 0)}"
                self.last = at(name, *job)
                return sem(name).h, 1

            def fill(self, *job):
                return self.up(f"bank_full{marks[('bank',) + job]}", *job)

            def latest(self):
                return self.last

        def bank(*job):
            return psum[marks.get(("bank",) + job, 0)]

        def filled(*job):
            return at(f"bank_full{marks.get(('bank',) + job, 0)}", *job)

        def drained(*job):
            return at(f"bank_free{marks.get(('bank',) + job, 0)}", *job)

        blocks = []

        def cols(w, c0, n, k0=0, k=4):
            return w.rearrange("(k p) n -> p k n", p=P)[:, k0:k0 + k, c0:c0 + n], k, n

        def add(key, src, last):
            blocks.append((key, src, last))

        def halves(key, w, c0, n, last):
            for half in range(2):
                add(key + (half,), cols(w, c0, n, 4 * half), last)

        def add_ada(l):
            for i in range(12):
                for half in range(2):
                    for j in range(2):
                        add(("ada", l, i, half, j), cols(dram["w_ada"][l], 512 * i + 256 * j, 256, 4 * half), ("ada", l, i, half))

        add_ada(0)
        for l in range(DEPTH):
            for i in range(8):
                halves(("z", l, i), dram["w_in"][l], OFF_Z + 256 * i, 256 if i < 7 else 128, ("z", l, min(2 * i + 1, 14)))
            for i in range(3):
                halves(("cf", l, i), dram["w_in"][l], 256 * i, 256, ("cf", l, 2 * i + 1))
            if l + 1 < DEPTH:
                add_ada(l + 1)
            for b, (w, k) in enumerate((("w_conv_out", 2), ("w_fno_out", 2), ("w_rwkv_out", 4))):
                for i in range(4):
                    add(("bw", l, b, i, 0), cols(dram[w][l], 256 * i, 256, 0, k), ("br", l, b, 2 * i + 1))
                    halves(("gate", l, b, i), dram["w_in"][l], OFF_G + DM * b + 256 * i, 256, ("gate", l, b, 2 * i + 1))
            for i in range(4):
                halves(("wo", l, i), dram["w_o"][l], 256 * i, 256, ("o", l, 2 * i + 1))
            if l % 2 == 0:
                for i in range(KF // 2):
                    halves(("fg", l, i), dram["ffn_w_gate"][l // 2], 256 * i, 256, ("fg", l, 2 * i + 1))
                    halves(("fu", l, i), dram["ffn_w_up"][l // 2], 256 * i, 256, ("fu", l, 2 * i + 1))
                for i in range(KF):
                    add(("fd", l, i), cols(dram["ffn_w_down"][l // 2], 0, DM, i, 1), ("fd", l, i))
        slot_of = {key: n % RING for n, (key, _, _) in enumerate(blocks)}

        pieces = []

        def tile_pieces(job, block, h):
            for half in range(2):
                n = 128 if block == ("z", block[1], 7) else 256
                raw = ring[slot_of[block + (half,)]][:, 0:4 * n].rearrange("p (k n) -> p k n", k=4)
                pieces.append((job + (half,), block + (half,), raw[:, :, h * P:(h + 1) * P], job if half else None))

        for l in range(DEPTH):
            for kind, n in (("z", NZ), ("cf", 6)):
                for m in range(n):
                    tile_pieces((kind, l, m), (kind, l, m // 2), m % 2)
            for b in range(3):
                for m in range(KD):
                    tile_pieces(("gate", l, b, m), ("gate", l, b, m // 2), m % 2)
            for m in range(KD):
                tile_pieces(("o", l, m), ("wo", l, m // 2), m % 2)
            if l % 2 == 0:
                for m in range(KF):
                    for kind in ("fg", "fu"):
                        tile_pieces((kind, l, m), (kind, l, m // 2), m % 2)
                for i in range(KF):
                    for half in range(2):
                        raw = ring[slot_of[("fd", l, i)]][:, half * 512:(half + 1) * 512].rearrange("p (k n) -> p k n", k=4)
                        pieces.append((("fd", l, i, half), ("fd", l, i), raw, None))
        piece_at = {key: n for n, (key, _, _, _) in enumerate(pieces)}
        last_piece = {block: key for key, block, _, _ in pieces}

        def phase_pieces(*kinds_l):
            return [n for n, (key, _, _, _) in enumerate(pieces) if key[:2] in kinds_l]

        block = ctx.enter_context(nc.Block())

        @block.sync
        def _(sp):
            S = Counts("sync_step")
            for n, (key, (src, k, w), last) in enumerate(blocks):
                if key[0] == "z" and key[2:] == (0, 0):
                    l = key[1]
                    if l > 0:
                        sp.wait_ge(*filled("gup", l - 1, 3))
                    for i, src_ in enumerate((dram["dec_up"][l].rearrange("d r c -> (d r) c"),
                                              dram["iclr_up"][l].rearrange("d r c -> (d r) c"), dram["g_up"][l])):
                        sp.dma_start(low[:, i, :], src_).then_inc(*S.up("low_in", l, by=16))
                if n >= RING:
                    prev = blocks[n - RING][2]
                    if blocks[n - RING][0] in last_piece:
                        sp.wait_ge(*at("rest_ready", *last_piece[blocks[n - RING][0]]))
                    elif prev[0] == "ada":
                        sp.wait_ge(*at("block_used", *prev))
                    else:
                        sp.wait_ge(*filled(*prev))
                dst = ring[n % RING][:, 0:k * w].rearrange("p (k n) -> p k n", k=k)
                sp.dma_start(dst, src).then_inc(*S.up(f"block_in{n % RING}", *key, by=16))
            sp.wait_ge(*at("h2_ready", 1))
            sp.wait_ge(*filled("o", 1, 7))
            sp.wait_ge(*at("out_stored", "state", 1, 1))

            def expert_weights(e, job):
                for n, (name, k0, kn, c0, w) in enumerate(E_PIECES):
                    by, before_ = e_rester((n - E_RAW) % NPC)
                    if n >= E_RAW and job is None:
                        sp.wait_ge(sem(by).h, before_ + 1)
                    elif n >= E_RAW:
                        sp.wait_ge(sem(by).h, job * E_EACH[by] + before_ + 1)
                    elif job is not None:
                        sp.wait_ge(sem(by).h, (job - 1) * E_EACH[by] + before_ + 1)
                    src = dram[name][0, e].rearrange("(k p) n -> p k n", p=P)[:, k0:k0 + kn, c0:c0 + w]
                    dst = e_raw[n % E_RAW][:, 0:kn * w].rearrange("p (k n) -> p k n", k=kn)
                    sp.dma_start(dst, src).then_inc(sem(f"e_in{n % E_RAW}").h, 16)

            expert_weights(0, None)
            sp.wait_ge(*at("jobs_ready"))
            jobs = sp.value_load(rt_i[0:1, 0:1], min_val=NE, max_val=NJOB)
            with sp.Fori(1, jobs) as j:
                e = sp.value_load(rt_i[0:1, bass.ds(j + 1, 1)], min_val=0, max_val=NE - 1)
                expert_weights(e, j)
            sp.wait_ge(sem("out_stored").h, 16 * 7)

        @block.tensor
        def _(pe):
            E = Counts("pe_step")
            jobs = [0]
            uses = [0] * 4
            prev_job = {}

            def used_for(b, *job):
                uses[b] += 1
                marks[(f"bank_free{b}",) + job] = uses[b]
                prev_job[b] = job

            def begin(*job):
                b = jobs[0] % 4
                jobs[0] += 1
                marks[("bank",) + job] = b
                if b in prev_job:
                    pe.wait_ge(*at(f"bank_free{b}", *prev_job[b]))
                used_for(b, *job)
                return psum[b]

            def transpose(out, src, n=P):
                return pe.transpose(out, src, ident[0:n, 0:n])

            def mm(out, lhsT, rhs, start, stop):
                return pe.matmul(out, lhsT, rhs, start=start, stop=stop)

            def tile(out, w, rhs, kn=KD):
                for k in range(kn):
                    last = mm(out, w(k), rhs(k), k == 0, k == kn - 1)
                return last

            pe.wait_ge(*at("first_in"))
            pe.wait_ge(*at("rows_in0"))
            def vectors(l):
                b = begin("vec", l)
                for g in (2 * l, 2 * l + 1):
                    n = sum(r for _, r in VEC["AB"[g % 2]]) + (24 if g == 0 else 0)
                    last = transpose(b[:, g * P:g * P + n], rows[0:n, g, :], n)
                last.then_inc(*E.fill("vec", l))

            vectors(0)
            pe.wait_ge(*at("x_in"))
            for k in range(KD):
                b = begin("xt", k)
                for j in range(3):
                    last = transpose(b[:, j * P:(j + 1) * P], xin[:, j, k * P:(k + 1) * P])
                last.then_inc(*E.fill("xt", k))
            for l in range(1, DEPTH):
                pe.wait_ge(*at(f"rows_in{l}"))
                vectors(l)

            def norm_sum(l, which):
                b = begin("norm", l, which)
                for k in range(KD):
                    if k % 2 == 0:
                        pe.wait_ge(*at("sq_ready", l, which, k // 2))
                    last = mm(b[:, 0:T], ones, sq[:, k, :], k == 0, k == KD - 1)
                last.then_inc(*E.fill("norm", l, which))

            def weights(key, n, kn=KD):
                slots = []
                for half in range((kn + 3) // 4):
                    key_ = key + (half,)
                    pe.wait_ge(*at(f"block_in{slot_of[key_]}", *key_))
                    slots.append(ring[slot_of[key_]][:, 0:min(kn, 4) * n].rearrange("p (k n) -> p k n", n=n))
                return lambda k, h: slots[k // 4][:, k % 4, h * P:(h + 1) * P]

            def three(out, w, x, i, k, start, stop):
                wr, wl, xr, xl = w[0][:, i], w[1][:, i], x[0][:, k], x[1][:, k]
                mm(out, wr, xr, start, False)
                mm(out, wr, xl, False, False)
                return mm(out, wl, xr, False, stop)

            def dense(job, phase, l, first=False):
                b = begin(*job)
                for half in range(2):
                    key = job + (half,)
                    pe.wait_ge(*at("rest_ready", *key))
                    w = w_parts[piece_at[key] % NSLOT]
                    for i in range(4):
                        k = 4 * half + i
                        if first and k % 2 == 0:
                            pe.wait_ge(*at("x_parts", phase, l, k // 2))
                        last = three(b[:, 0:T], w, h_parts[phase], i, k, k == 0, k == KD - 1)
                    if half == 0:
                        last.then_inc(*E.up("piece_used", *key))
                last.then_inc(*E.fill(*job))


            def ada(l, i):
                for half in range(2):
                    w = []
                    for j in range(2):
                        key = ("ada", l, i, half, j)
                        pe.wait_ge(*at(f"block_in{slot_of[key]}", *key))
                        w.append(ring[slot_of[key]].rearrange("p (k n) -> p k n", n=256))
                    for k in range(4):
                        for j in range(4):
                            last = mm(psum[4 + i // 4][32 * j:32 * j + 32, (i % 4) * P:(i % 4 + 1) * P],
                                      condp[:, 4 * half + k, :], w[j // 2][:, k, (j % 2) * P:(j % 2 + 1) * P],
                                      k + half == 0, k == 3 and half == 1)
                    last.then_inc(*E.up("block_used", "ada", l, i, half))
                    yield

            def ada_turn(l):
                for g in range(3):
                    b = begin("adaT", l, g)
                    pe.wait_ge(*at("ada_copied", l, g))
                    for i in range(4):
                        last = transpose(b[:, i * P:(i + 1) * P], adas[:, (4 * g + i) * P:(4 * g + i + 1) * P])
                    last.then_inc(*E.fill("adaT", l, g))

            for l in range(DEPTH):
                if l == 0:
                    pe.wait_ge(*at("cond_ready"))
                    for i in range(12):
                        for _ in ada(0, i):
                            pass
                    ada_turn(0)
                next_ada = (1 for i in range(12 if l + 1 < DEPTH else 0) for _ in ada(l + 1, i))
                norm_sum(l, 0)
                for m in range(NZ):
                    dense(("z", l, m), "z", l, m == 0)
                for m in range(6):
                    dense(("cf", l, m), "z", l)
                if l == 0:
                    pe.wait_ge(*at("second_in"))
                for m in range(NM):
                    b = begin("kks", l, m)
                    if m == 0:
                        pe.wait_ge(*at("ksq_ready", l))
                    mm(b[:, 0:T], heads, ksq[:, m, :], True, True).then_inc(*E.fill("kks", l, m))
                def lowrank(d):
                    if d == 0:
                        pe.wait_ge(*at("low_in", l))
                        pe.wait_ge(*at("low_in_ready", l))
                    r = slice(64 * d, 64 * d + 64)
                    for which in range(2):
                        for m in range(NM):
                            b = begin("low", l, d, which, m)
                            mm(b[:, 0:T], low[r, which, m * P:(m + 1) * P], z[r, 13 + which, :], True, True)\
                                .then_inc(*E.fill("low", l, d, which, m))

                lowrank(0)
                pe.wait_ge(*at("glu_ready", l))
                for m in range(2):
                    b = begin("conv", l, m)
                    b2 = begin("conv_s", l, m)
                    sp_ = glu[:, m, TP + 30:].rearrange("p (r t) -> p r t", r=4)
                    for j in range(CONV_W):
                        i = m * CONV_W + j
                        pe.wait_ge(*at("diag_ready", l, i))
                        mm(b[:, 0:TP], diag[i % 8], glu[:, m, j:j + TP], j == 0, j == CONV_W - 1)
                        last = mm(b2[:, 0:TS].rearrange("p (r t) -> p r t", r=4), diag[i % 8], sp_[:, :, j:j + GRID], j == 0, j == CONV_W - 1)
                        if j < CONV_W - 1:
                            last.then_inc(*E.up("diag_used", l, i))
                    last.then_inc(*E.fill("conv_s", l, m))
                for m in range(4, 6):
                    pe.wait_ge(*drained("cf", l, m))
                for j in range(NCP):
                    b = begin("fno1", l, j)
                    for m in range(2):
                        last = mm(b[:, m * 256:(m + 1) * 256], fno_u[:, m, j * P:(j + 1) * P],
                                  second[:, tcol["dft_c"][0] - n_first:tcol["dft_c"][0] - n_first + 256], True, True)
                    last.then_inc(*E.fill("fno1", l, j))
                for j in range(NCP):
                    pe.wait_ge(*drained("fno1", l, j))
                for m in range(2):
                    b = begin("fno2", l, m)
                    for i in range(2):
                        mm(b[:, 0:TP], fno_z[:, 0, m, i * P:(i + 1) * P], time_p[:, 0, i, :], i == 0, i == 1)
                    for j in range(2):
                        for i in range(2):
                            last = mm(b[:, TP:T], fno_z[:, 1 + j, m, i * P:(i + 1) * P], time_s[:, j, i, :],
                                      j == 0 and i == 0, j == 1 and i == 1)
                    last.then_inc(*E.fill("fno2", l, m))
                for w in range(2):
                    b = begin("cln", l, w)
                    if w == 0:
                        for m in range(2):
                            pe.wait_ge(*drained("conv", l, m))
                            pe.wait_ge(*drained("conv_s", l, m))
                    else:
                        pe.wait_ge(*at("conv_sq", l))
                    src = cvT if w == 0 else conv_b
                    for m in range(2):
                        last = mm(b[:, 0:T], ones, src[:, m, :], m == 0, m == 1)
                    last.then_inc(*E.fill("cln", l, w))

                for d in range(2):
                    if d == 1:
                        lowrank(1)
                        for _ in range(5):
                            next(next_ada, None)
                    pe.wait_ge(*at("ark_ready", l, d))
                    for cp in range(NCP):
                        for i in range(3 if d == 0 else 2):
                            b = begin("tok", l, d, cp, i)
                            for m in range(NM):
                                src = (BK[:, i, m, :] if i < 2 else z[:, 8 + m, :])[:, cp * P:(cp + 1) * P]
                                last = transpose(b[:, m * P:(m + 1) * P], src)
                            last.then_inc(*E.fill("tok", l, d, cp, i))
                    for cp in range(NCP):
                        for hp in range(NH // 2):
                            b = begin("pair", l, d, cp, hp)
                            r = slice(64 * (hp % 2), 64 * (hp % 2) + 64)
                            for i in range(2):
                                for hh in range(2):
                                    m = 2 * (hp // 2) + hh
                                    for par in range(2):
                                        q = slice(64 * par, 64 * par + 64)
                                        c = 2 * cp + par
                                        o_ = hh * 256 + i * P
                                        last = mm(b[q, o_:o_ + P], BK[r, i, m, c * C:(c + 1) * C],
                                                  AR[r, m, c, :, :], True, True)
                            last.then_inc(*E.fill("pair", l, d, cp, hp))
                    quarters = [(slice(32 * g, 32 * g + 32), g % 2) for g in range(4)]
                    for lev in range(LEVELS):
                        for u in range(NCP + 1):
                            if lev == 0:
                                if u == NCP:
                                    continue
                                b = begin("TAT", l, d, lev, u)
                                pe.wait_ge(*at("TQ_ready", l, d, u))
                                for h in range(NH):
                                    for q, blk in quarters:
                                        mm(b[q, h * C:h * C + B], S1[q, u, h, blk * B:(blk + 1) * B], TQ[q, u, h, 0:B],
                                           True, True)
                                    for q, blk in quarters:
                                        last = mm(b[q, h * C + B:(h + 1) * C], TQ[q, u, h, 0:B],
                                                  S1[q, u, h, blk * B:(blk + 1) * B], True, True)
                                last.then_inc(*E.fill("TAT", l, d, lev, u))
                                continue
                            if u < NCP:
                                b = begin("X", l, d, lev, u)
                                pe.wait_ge(*drained("TAT", l, d, lev - 1, u))
                                for h in range(NH):
                                    for q, blk in quarters:
                                        last = mm(b[q, h * B:(h + 1) * B], S1[q, u, h, blk * B:(blk + 1) * B],
                                                  TQ[q, u, h, 0:B], True, True)
                                last.then_inc(*E.fill("X", l, d, lev, u))
                            if u > 0:
                                w = u - 1
                                b = begin("TAT", l, d, lev, w)
                                pe.wait_ge(*drained("X", l, d, lev, w))
                                for h in range(NH):
                                    for q, blk in quarters:
                                        mm(b[q, h * C:h * C + B], TQ[q, w, h, B:C], Xs[w][q, h * B:(h + 1) * B], True, True)
                                    for q, blk in quarters:
                                        last = mm(b[q, h * C + B:(h + 1) * C], Xs[w][q, h * B:(h + 1) * B], TQ[q, w, h, B:C],
                                                  True, True)
                                last.then_inc(*E.fill("TAT", l, d, lev, w))
                    for u in range(NCP + 1):
                        if u < NCP:
                            b = begin("XO", l, d, u)
                            pe.wait_ge(*drained("TAT", l, d, LEVELS - 1, u))
                            for h in range(NH):
                                for par in range(2):
                                    fr, to = quarters[2 * par + d][0], quarters[2 * par + 1 - d][0]
                                    last = mm(b[to, h * B:(h + 1) * B], S1[fr, u, h, (1 - d) * B:(2 - d) * B],
                                              TQ[fr, u, h, 0:B], True, True)
                            last.then_inc(*E.fill("XO", l, d, u))
                        if u > 0:
                            w = u - 1
                            b = begin("QO", l, d, w)
                            pe.wait_ge(*drained("XO", l, d, w))
                            for h in range(NH):
                                for par in range(2):
                                    fr, to = quarters[2 * par + d][0], quarters[2 * par + 1 - d][0]
                                    last = mm(b[fr, h * B:(h + 1) * B], Xs[w][to, h * B:(h + 1) * B], TQ[to, w, h, B:C],
                                              True, True)
                            last.then_inc(*E.fill("QO", l, d, w))
                    def meanwhile():
                        if next(next_ada, None) is None:
                            for _ in range(FILL):
                                mm(psum[7][:, 0:P], ident, ident, True, True)

                    if d == 0:
                        pe.wait_ge(*at("st_in", l))
                    b = begin("s0", l, d)
                    sti = st_in.rearrange("p (d h k) -> p d h k", d=2, h=NH)
                    for m in range(NM):
                        last = transpose(b[:, m * C:(m + 1) * C], sti[0:64, d, 2 * m:2 * m + 2, :], 64)
                    last.then_inc(*E.fill("s0", l, d))
                    for step in steps(d):
                        for n, c in step:
                            cp, par = divmod(c, 2)
                            q = slice(64 * par, 64 * par + 64)
                            b = begin("W", l, d, c)
                            for h in range(NH):
                                mm(b[q, h * C:(h + 1) * C], S1[q, cp, h, 2 * C:3 * C], vtok[q, cp, h * C:(h + 1) * C],
                                   h == 0, False)
                            if c == starts(d)[1]:
                                pe.wait_ge(*drained("s0", l, d))
                            else:
                                pe.wait_ge(*at("S_ready", l, d, c))
                            for m in range(NM):
                                last = mm(b[q, m * P:(m + 1) * P], AR[:, m, c, 0, :], St[:, c, m, :], False, m == NM - 1)
                            last.then_inc(*E.fill("W", l, d, c))
                        meanwhile()
                        for n, c in step:
                            cp, par = divmod(c, 2)
                            q = slice(64 * par, 64 * par + 64)
                            b = begin("U", l, d, c)
                            pe.wait_ge(*drained("W", l, d, c))
                            if n == 0:
                                pe.wait_ge(*at("Qdiag_ready", l, d))
                                for u in range(NCP):
                                    pe.wait_ge(*drained("QO", l, d, u))
                            for h in range(NH):
                                last = mm(b[q, h * C:(h + 1) * C], Q[q, cp, h, :], Wb[n % 2][q, h * C:(h + 1) * C], True, True)
                            last.then_inc(*E.fill("U", l, d, c))
                        meanwhile()
                        for n, c in step:
                            if nxt(d, c) is None:
                                continue
                            cp, par = divmod(c, 2)
                            q = slice(64 * par, 64 * par + 64)
                            b = begin("S", l, d, c)
                            pe.wait_ge(*drained("U", l, d, c))
                            for h in range(NH):
                                m, r = h // 2, slice(64 * (h % 2), 64 * (h % 2) + 64)
                                oc = b[r, m * C:(m + 1) * C]
                                hs = slice(h * C, (h + 1) * C)
                                mm(oc, tok[q, 1, cp, hs], vtok[q, cp, hs], True, False)
                                last = mm(oc, tok[q, 0, cp, hs], U[q, cp, h, :], False, True)
                            last.then_inc(*E.fill("S", l, d, c))
                        meanwhile()
                    if d == 1:
                        for _ in next_ada:
                            pass
                    pe.wait_ge(*drained("U", l, d, order(d)[-1]))
                    for cp in range(NCP):
                        b = begin("Y", l, d, cp)
                        halves_ = [(slice(64 * par, 64 * par + 64), 2 * cp + par) for par in range(2)]
                        for m in range(NM):
                            for q, c in halves_:
                                mm(b[q, m * P:(m + 1) * P], AR[:, m, c, 1, :], St[:, c, m, :], m == 0, False)
                        for h in range(NH):
                            hs = slice(h * C, (h + 1) * C)
                            for q, c in halves_:
                                mm(b[q, hs], S1[q, cp, h, C:2 * C], U[q, cp, h, :], False, False)
                            for q, c in halves_:
                                last = mm(b[q, hs], S1[q, cp, h, 3 * C:4 * C], vtok[q, cp, hs], False, h == NH - 1)
                        last.then_inc(*E.fill("Y", l, d, cp))
                    b = begin("sf", l, d)
                    pe.wait_ge(*at("Sfin_ready", l, d))
                    for m in range(NM):
                        last = transpose(b[0:64, m * P:(m + 1) * P], Sfin[:, m, :])
                    last.then_inc(*E.fill("sf", l, d))
                def gates(b_, src, kn):
                    for m in range(KD):
                        if m % 2 == 0:
                            wb = weights(("bw", l, b_, m // 2), 256, kn)
                        dense(("gate", l, b_, m), "gate", l, b_ == 0 and m == 0)
                        b = begin("br", l, b_, m)
                        tile(b[:, 0:T], lambda k: wb(k, m % 2), lambda k: src[:, k, :], kn).then_inc(*E.fill("br", l, b_, m))

                pe.wait_ge(*at("cv_ready", l))
                gates(0, cvT, 2)
                for m in range(2):
                    pe.wait_ge(*drained("fno2", l, m))
                gates(1, fnT, 2)
                for cp in range(NCP):
                    b = begin("yt", l, cp)
                    if cp == 0:
                        pe.wait_ge(*at("yn_ready", l))
                    for m in range(NM):
                        last = transpose(b[:, m * P:(m + 1) * P], Y[:, cp, m * P:(m + 1) * P])
                    last.then_inc(*E.fill("yt", l, cp))
                for m in range(NM):
                    b = begin("bon", l, m)
                    if m == 0:
                        pe.wait_ge(*at("rk_ready", l))
                    mm(b[:, 0:T], heads, tmp4[1][:, m * T:(m + 1) * T], True, True).then_inc(*E.fill("bon", l, m))
                for m in range(NM):
                    b = begin("gup", l, m)
                    mm(b[:, 0:T], low[:, 2, m * P:(m + 1) * P], z[:, 12, :], True, True).then_inc(*E.fill("gup", l, m))
                for m in range(NM):
                    pe.wait_ge(*drained("gup", l, m))
                gates(2, yT, 4)
                if l + 1 < DEPTH:
                    ada_turn(l + 1)
                for m in range(KD):
                    dense(("o", l, m), "merged", l, m == 0)
                norm_sum(l, 1)
                if l % 2 == 0:
                    for m in range(KF):
                        dense(("fg", l, m), "ffn", l, m == 0)
                        dense(("fu", l, m), "ffn", l)
                    for m in range(4):
                        pe.wait_ge(*at(f"bank_free{m}", *prev_job[m]))
                    for i in range(KF):
                        pe.wait_ge(*at("prod_rest", l, i))
                        for half in range(2):
                            key = ("fd", l, i, half)
                            pe.wait_ge(*at("rest_ready", *key))
                            for m in range(4):
                                last = three(psum[4 * half + m][:, 0:T], w_parts[piece_at[key] % NSLOT], h_parts["prod"], m, i, i == 0, i == KF - 1)
                            last.then_inc(*E.up("piece_used", *key))
                    for m in range(4):
                        used_for(m, "fdown", l, m)
            b = begin("logit")
            pe.wait_ge(*at("h2_ready", DEPTH - 1))
            pe.wait_ge(*at("h_odd", DEPTH - 1, 1, 3))
            pe.wait_ge(*at("router_in"))
            for j in range(3):
                for k in range(KD):
                    mm(b[:, j * NE:(j + 1) * NE], hT[:, k, j * P:(j + 1) * P], wrt[:, k, :], k == 0, False)
                last = mm(b[:, j * NE:(j + 1) * NE], ones[0:1, :], brt[0:1, :], False, True)
            last.then_inc(*E.fill("logit"))
            for k in range(6):
                b = begin("htok", k)
                for i in range(4):
                    j, kk_ = divmod(4 * k + i, KD)
                    last = transpose(b[:, i * P:(i + 1) * P], hT[:, kk_, j * P:(j + 1) * P])
                last.then_inc(*E.fill("htok", k))
            b = begin("rank")
            pe.wait_ge(*at("chosen_ready"))
            ch = rt[:, 0:24]
            for j in range(3):
                for i in range(j + 1):
                    mm(b[:, j * NE:(j + 1) * NE], before if i == j else ones, ch[:, i * NE:(i + 1) * NE], i == 0, i == j)
            for i in range(3):
                last = mm(b[:, 24:32], ones, ch[:, i * NE:(i + 1) * NE], i == 0, i == 2)
            last.then_inc(*E.fill("rank"))
            pe.wait_ge(*at("jobs_ready"))
            for m in range(4):
                pe.wait_ge(*at(f"bank_free{m}", *prev_job[m]))
            pe.wait_ge(*at("fdown_done", 0))
            s = lambda name: sem(name).h
            pe.sem_inc(s("e_sc"), 6)
            pe.sem_inc(s("e_used"), E_PARTS)

            def e_piece(i, n, x, k_out):
                _, k0, kn, _, w = E_PIECES[n]
                by, before_ = e_rester(n)
                pe.wait_ge(s(by), i * E_EACH[by] + before_ + 1)
                wr, wl = e_w[n % E_PARTS]
                for k in range(kn):
                    for c0 in range(0, w, 512):
                        cols_ = slice(k * w + c0, k * w + min(w, c0 + 512))
                        out, start, stop = k_out(k0 + k, c0)
                        out = out[:, 0:cols_.stop - cols_.start]
                        mm(out, x[0][:, k0 + k, :], wr[:, cols_], start, False)
                        mm(out, x[1][:, k0 + k, :], wr[:, cols_], False, False)
                        last = mm(out, x[0][:, k0 + k, :], wl[:, cols_], False, stop)
                last.then_inc(s("e_used"), 1)

            njobs = pe.value_load(rt_i[0:1, 0:1], min_val=NE, max_val=NJOB)
            with pe.Fori(0, njobs) as i:
                pe.wait_ge(s("e_sel"), i + 1)
                pe.wait_ge(s("e_ydrained"), i * 2 + 2)
                for j in range(3):
                    last = transpose(psum[4][:, j * P:(j + 1) * P], selc[:, j, :])
                last.then_inc(s("e_selT_full"), 1)
                pe.wait_ge(s("e_sc_done"), i * 6 + 6)
                for k in range(KD):
                    for j in range(3):
                        last = mm(psum[6 + k // 4][:, (k % 4) * P:(k % 4 + 1) * P], htok[:, j, k * P:(k + 1) * P],
                                  sel[:, j, :], j == 0, j == 2)
                    if k % 4 == 3:
                        last.then_inc(s("e_gather"), 1)
                pe.wait_ge(s("e_hG_rest"), i * 2 + 2 + 2)
                for c in range(3):
                    pe.wait_ge(s("e_prod"), i * 3 + 3 + (1 if c == 2 else 0))
                    for n in range(c * CHUNK_PIECES, (c + 1) * CHUNK_PIECES):
                        which = int(E_PIECES[n][0] == "moe_w_up")
                        e_piece(i, n, hG, lambda k, c0: (psum[2 * (c % 2) + which], k == 0, k == KD - 1))
                    if c > 0:
                        e_transposes(pe, s, transpose, psum, eprod, i, c - 1)
                for n in range(3 * CHUNK_PIECES, NPC):
                    k0 = E_PIECES[n][1]
                    if k0 == 0:
                        pe.wait_ge(s("e_selT"), i + 1)
                    if k0 == DOWN[1][0]:
                        e_transposes(pe, s, transpose, psum, eprod, i, 2)
                    for c in range(3):
                        if k0 == DOWN[c][0]:
                            pe.wait_ge(s("e_pT_rest"), i * 3 + c + 1)
                    e_piece(i, n, eprodT, lambda k, c0: (psum[4 + (E_PIECES[n][3] + c0) // 512], k == 0, k == KE - 1))
                pe.wait_ge(s("e_ydrained"), i * 2 + 2 + 2)
                for j in range(3):
                    for half in range(2):
                        n_ = 2 * j + half
                        if n_ >= 2:
                            pe.wait_ge(s("e_sc_done"), i * 6 + 6 + n_ - 1)
                        mm(psum[6 + half][:, :], selT[:, j, :], ey[:, half * 512:(half + 1) * 512], True, True)\
                            .then_inc(s("e_sc"), 1)
            for m in range(4):
                prev_job.pop(m, None)
            pe.wait_ge(*at("yacc_ready"))
            for k in range(KD):
                b = begin("ey", k)
                for j in range(3):
                    last = transpose(b[:, j * P:(j + 1) * P], yacc[:, j, k * P:(k + 1) * P])
                last.then_inc(*E.fill("ey", k))
            norm_sum(DEPTH, 0)
            pe.wait_ge(*at("h_ready", DEPTH))
            for j in range(3):
                for half in range(2):
                    b = begin("yo", j, half)
                    for k in range(4):
                        last = transpose(b[:, k * P:(k + 1) * P], sq[:, 4 * half + k, j * P:(j + 1) * P])
                    last.then_inc(*E.fill("yo", j, half))

        @block.scalar
        def _(act):
            E = Counts("act_step")
            a = act.activation

            act.dma_start(first, dram["tables"][:, 0:n_first]).then_inc(*E.up("first_in", by=16))
            def rows_in(l):
                for g in (2 * l, 2 * l + 1):
                    r = 0
                    for name, n in VEC["AB"[g % 2]] + (SHARED if g == 0 else ()):
                        src = dram[name] if r >= sum(n_ for _, n_ in VEC["AB"[g % 2]]) else dram[name][l]
                        act.dma_start(rows[r:r + n, g, :], flat(src).rearrange("(r c) -> r c", c=P))\
                            .then_inc(*E.up(f"rows_in{l}", by=16))
                        r += n

            rows_in(0)
            for j in range(3):
                src = dram["x_prompt"][0] if j == 0 else dram["x_sample"][0][(j - 1) * P:j * P, :]
                act.dma_start(xin[:, j, :], src).then_inc(*E.up("x_in", by=16))
            for l in range(1, DEPTH):
                rows_in(l)
            act.dma_start(second, dram["tables"][:, n_first:ncols]).then_inc(*E.up("second_in", by=16))

            def load_state(l):
                sti = st_in.rearrange("p (d h k) -> p d h k", d=2, h=NH)
                for d in range(2):
                    act.dma_start(sti[0:64, d, :, :], dram["state_rwkv"][0, l, d].rearrange("h v k -> v h k"))\
                        .then_inc(*E.up("st_in", l, by=16))

            load_state(0)
            def vectors(l):
                act.wait_ge(*filled("vec", l))
                for g in (2 * l, 2 * l + 1):
                    n = sum(r for _, r in VEC["AB"[g % 2]]) + (24 if g == 0 else 0)
                    ins = a(vec[:, g, 0:n], bank("vec", l)[:, g * P:g * P + n], ACT.Copy)
                ins.then_inc(*E.read("vec", l))

            vectors(0)
            act.wait_ge(*E.latest())
            for i, name in ((0, "c_ctx"), (1, "c")):
                a(condx[:, :, i], v(name, 0, 0, 8), ACT.Copy).then_inc(*E.step())
                a(cond[:, :, i], v(name, 0, 0, 8), ACT.Sigmoid).then_inc(*E.up("cond_sig", i))
            for k in range(KD):
                act.wait_ge(*filled("xt", k))
                a(xT[:, k, :], bank("xt", k)[:, 0:T], ACT.Copy).then_inc(*E.read("xt", k))
            for l in range(1, DEPTH):
                vectors(l)

            def ada_copies(l):
                for g in range(3):
                    act.wait_ge(*at("block_used", "ada", l, 4 * g + 3, 1))
                    a(adas[:, g * 512:(g + 1) * 512], psum[4 + g][:, :], ACT.Copy).then_inc(*E.up("ada_copied", l, g))

            def squares(l, which):
                for i in range(4):
                    m = 2 * i + 1
                    if which == 1:
                        act.wait_ge(*drained("o", l, m))
                    elif l == DEPTH:
                        act.wait_ge(*drained("ey", m))
                    elif l > 0 and m < 4:
                        act.wait_ge(*at(f"bank_free{m}", "fdown", l - 1, m))
                    elif l > 0:
                        act.wait_ge(*at("fdown_done", l - 1))
                    elif i == 0:
                        act.wait_ge(*E.latest())
                    a(sq[:, 2 * i:2 * i + 2, :], xT[:, 2 * i:2 * i + 2, :], ACT.Square).then_inc(*E.up("sq_ready", l, which, i))

            def root(l, which):
                act.wait_ge(*filled("norm", l, which))
                a(rs, bank("norm", l, which)[:, 0:T], ACT.Sqrt, bias=eps[1e-6], scale=1.0 / DM)\
                    .then_inc(*E.read("norm", l, which))

            def convert(n):
                key, block, raw, _ = pieces[n]
                if n in posted:
                    return
                posted.add(n)
                act.wait_ge(*at(f"block_in{slot_of[block]}", *block))
                if n >= NSLOT:
                    prev, _, _, job = pieces[n - NSLOT]
                    act.wait_ge(*(filled(*job) if job else at("piece_used", *prev)))
                a(w_parts[n % NSLOT][0], raw, ACT.Copy).then_inc(*E.up("rounded_ready", *key))

            posted = set()

            def ahead(*job):
                n = piece_at[job + (1,)]
                for i in range(n + 1, n + NSLOT):
                    if i < len(pieces) and pieces[i][0][:2] in allowed:
                        convert(i)

            allowed = []

            def start_phase(*kinds):
                allowed[:] = kinds
                n = min(i for i, p in enumerate(pieces) if p[0][:2] == kinds[0])
                for i in range(n, n + NSLOT):
                    convert(i)

            def rounded(phase, l, g, src):
                a(h_parts[phase][0][:, 2 * g:2 * g + 2, :], src, ACT.Copy).then_inc(*E.up("x_rounded", phase, l, g))

            def modulate(l, which):
                for i in range(2):
                    act.wait_ge(*at("xn_ready", l, which, i))
                    for k in (4 * i, 4 * i + 2):
                        for s_, (t0, t1) in enumerate(SEG):
                            ins = a(hT[:, k, t0:t1], hT[:, k, t0:t1], ACT.Identity,
                                    bias=mods[:, l, 24 * which + k, s_:s_ + 1], scale=modAs[:, l, which, k, s_:s_ + 1])
                        ins.then_inc(*E.up("h2_ready" if which else "h_ready", l))
                    if which == 0 or l % 2 == 0:
                        act.wait_ge(*E.latest())
                        for g in (2 * i, 2 * i + 1):
                            act.wait_ge(*at("h_odd", l, which, g))
                            rounded("ffn" if which else "z", l, g, hT[:, 2 * g:2 * g + 2, :])

            for l in range(DEPTH):
                squares(l, 0)
                if l == 0:
                    ada_copies(0)
                start_phase(("z", l), ("cf", l))
                root(l, 0)
                act.wait_ge(*at("modA_ready", l))
                modulate(l, 0)
                for m in range(NZ):
                    ahead("z", l, m)
                    act.wait_ge(*filled("z", l, m))
                    a(z[:, m, :], bank("z", l, m)[:, 0:T], ACT.Copy).then_inc(*E.read("z", l, m))
                for m in range(6):
                    ahead("cf", l, m)
                    act.wait_ge(*filled("cf", l, m))
                    src = bank("cf", l, m)[:, 0:T]
                    if m < 2:
                        ins = a(cvT[:, m, :], src, ACT.Copy)
                    elif m < 4:
                        ins = a(conv_b[:, m - 2, :], src, ACT.Sigmoid)
                    else:
                        ins = a(fno_u[:, m - 4, :], src, ACT.Copy)
                    ins.then_inc(*E.read("cf", l, m))
                act.wait_ge(*at("mix_done", l))
                a(z[:, 12, :], z[:, 12, :], ACT.Sigmoid).then_inc(*E.up("act_step"))
                a(z[:, 13, :], z[:, 13, :], ACT.Tanh).then_inc(*E.up("low_in_ready", l))
                act.wait_ge(*at("kkp_ready", l))
                a(ksq, kk, ACT.Square).then_inc(*E.up("ksq_ready", l))
                for m in range(NM):
                    act.wait_ge(*filled("kks", l, m))
                    a(ksq[:, m, :], bank("kks", l, m)[:, 0:T], ACT.Sqrt).then_inc(*E.read("kks", l, m))

                def lowrank(d):
                    if d == 1:
                        act.wait_ge(*filled("Y", l, 0, NCP - 1))
                    for which, name in enumerate(("dec_w0", "iclr_a0")):
                        for m in range(NM):
                            act.wait_ge(*filled("low", l, d, which, m))
                            ins = a(tmp4[which][:, m * T:(m + 1) * T], bank("low", l, d, which, m)[:, 0:T], ACT.Sigmoid,
                                    bias=v(name, l, NM * d + m))
                            ins.then_inc(*E.read("low", l, d, which, m))

                def exps(d):
                    act.wait_ge(*at("L_ready", l, d))
                    L = L3(d)
                    tot = tmp4[2].rearrange("p (m c t) -> p m c t", m=NM, c=NC_)[:, :, :, C - 1]
                    a(pc, tot, ACT.Exp, scale=-DECAY).then_inc(*E.step())
                    a(tmp4[0], tmp4[0], ACT.Exp, scale=-DECAY).then_inc(*E.up("E1_ready", l, d))
                    act.wait_ge(*E.latest())
                    a(tmp4[other(d)], tmp4[L], ACT.Exp, scale=-DECAY).then_inc(*E.up("E2_ready", l, d))
                    act.wait_ge(*E.latest())
                    a(tmp4[L], tmp4[L], ACT.Exp, scale=DECAY).then_inc(*E.up("E3_ready", l, d))

                lowrank(0)
                exps(0)
                for m in range(2):
                    act.wait_ge(*filled("conv_s", l, m))
                    if m == 0:
                        act.wait_ge(*at("glu_ready", l))
                    a(cvT[:, m, 0:TP], bank("conv", l, m)[:, 0:TP], ACT.Identity, bias=v("dw_b", l, m))\
                        .then_inc(*E.read("conv", l, m))
                    a(cvT[:, m, TP:T], bank("conv_s", l, m)[:, 0:TS], ACT.Identity, bias=v("dw_b", l, m))\
                        .then_inc(*E.read("conv_s", l, m))
                for m in range(2):
                    act.wait_ge(*filled("fno2", l, m))
                    a(fnT[:, m, :], bank("fno2", l, m)[:, 0:T], ACT.Copy).then_inc(*E.read("fno2", l, m))
                act.wait_ge(*drained("cln", l, 0))
                a(conv_b, cvT, ACT.Square).then_inc(*E.up("conv_sq", l))
                act.wait_ge(*filled("cln", l, 1))
                a(conv_b[:, 0, :], bank("cln", l, 1)[:, 0:T], ACT.Sqrt, bias=eps[1e-5], scale=1.0 / CC)\
                    .then_inc(*E.read("cln", l, 1))
                act.wait_ge(*at("conv_affine", l))
                a(conv_b, cvT, ACT.Sigmoid).then_inc(*E.up("conv_sig", l))

                for d in range(2):
                    if d == 1:
                        lowrank(1)
                        exps(1)
                    for cp in range(NCP):
                        for i in range(3 if d == 0 else 2):
                            act.wait_ge(*filled("tok", l, d, cp, i))
                            dst = tok[:, i, cp, :] if i < 2 else vtok[:, cp, :]
                            a(dst, bank("tok", l, d, cp, i)[:, :], ACT.Copy).then_inc(*E.read("tok", l, d, cp, i))
                    for lev in range(1, LEVELS):
                        for u in range(NCP):
                            act.wait_ge(*filled("X", l, d, lev, u))
                            if lev > 1:
                                act.wait_ge(*filled("TAT", l, d, lev - 1, u))
                            a(Xs[u], bank("X", l, d, lev, u)[:, 0:256], ACT.Copy).then_inc(*E.read("X", l, d, lev, u))
                    for u in range(NCP):
                        act.wait_ge(*filled("XO", l, d, u))
                        act.wait_ge(*filled("TAT", l, d, LEVELS - 1, u))
                        for par in range(2):
                            q = slice(64 * par + 32 * (1 - d), 64 * par + 32 * (2 - d))
                            ins = a(Xs[u][q, :], bank("XO", l, d, u)[q, 0:256], ACT.Copy)
                        ins.then_inc(*E.read("XO", l, d, u))
                    act.wait_ge(*filled("s0", l, d))
                    act.wait_ge(*filled("QO", l, d, NCP - 1))
                    act.wait_ge(*at("St_zero", l))
                    c0 = starts(d)[1]
                    for hh in range(2):
                        r = slice(64 * hh, 64 * hh + 64)
                        ins = a(St[r, c0, :, r], bank("s0", l, d)[r, 0:256].rearrange("p (m v) -> p m v", m=NM), ACT.Copy)
                    ins.then_inc(*E.read("s0", l, d))
                    if d == 1 and l + 1 < DEPTH:
                        load_state(l + 1)
                    for n, c in enumerate(order(d)):
                        q = slice(64 * (c % 2), 64 * (c % 2) + 64)
                        act.wait_ge(*filled("W", l, d, c))
                        if n >= 2:
                            act.wait_ge(*filled("U", l, d, order(d)[n - 2]))
                        a(Wb[n % 2][q, :], bank("W", l, d, c)[q, :], ACT.Copy).then_inc(*E.read("W", l, d, c))
                    if d == 0:
                        for cp in range(NCP):
                            act.wait_ge(*filled("Y", l, d, cp))
                            a(Y[:, cp, :], bank("Y", l, d, cp)[:, :], ACT.Copy).then_inc(*E.read("Y", l, d, cp))
                    act.wait_ge(*filled("sf", l, d))
                    if (l, d) != (0, 0):
                        act.wait_ge(*at("out_stored", "state", *((l, 0) if d else (l - 1, 1))))
                    so = sout[0:64, :]
                    a(so, bank("sf", l, d)[0:64, :], ACT.Copy).then_inc(*E.read("sf", l, d))
                    act.wait_ge(*E.latest())
                    act.dma_start(new_state[0, l, d].rearrange("h v k -> v h k"), so.rearrange("p (h k) -> p h k", h=NH))\
                        .then_inc(*E.up("out_stored", "state", l, d, by=16))
                act.wait_ge(*filled("sf", l, 1))
                act.wait_ge(*filled("Y", l, 1, NCP - 1))
                start_phase(("gate", l), ("o", l))
                for g in range(4):
                    rounded("gate", l, g, hT[:, 2 * g:2 * g + 2, :])
                for b_ in range(3):
                    for m in range(KD):
                        ahead("gate", l, b_, m)
                        act.wait_ge(*filled("gate", l, b_, m))
                        i = b_ * KD + m
                        if i >= 16:
                            act.wait_ge(*at("gated", l, *divmod(i - 8, KD)))
                        elif i >= 8:
                            act.wait_ge(*drained("br", l, 0, m))
                        a(gsig(i), bank("gate", l, b_, m)[:, 0:T], ACT.Sigmoid).then_inc(*E.read("gate", l, b_, m))
                        if i == 1:
                            act.wait_ge(*at("Y_centred", l))
                            a(tmp4[2].rearrange("p (c w) -> p c w", c=NCP), Y, ACT.Square).then_inc(*E.up("Ysq_ready", l))
                        if i == 3:
                            act.wait_ge(*at("Yvar_ready", l))
                            a(stat[:, 24:48], stat[:, 0:24], ACT.Sqrt, bias=eps[64e-5], scale=1.0 / HD)\
                                .then_inc(*E.up("Ystd_ready", l))
                        if b_ == 2 and m == 1 and l + 1 < DEPTH:
                            for i in range(NM):
                                act.wait_ge(*drained("gup", l, i))
                            ada_copies(l + 1)
                        if b_ == 2 and m > 0:
                            act.wait_ge(*at("gated", l, 2, m - 1))
                            a(h_parts["merged"][0][:, m - 1, :], merged[m - 1], ACT.Copy).then_inc(*E.up("m_rounded", l, m - 1))
                act.wait_ge(*at("gated", l, 2, KD - 1))
                a(h_parts["merged"][0][:, KD - 1, :], merged[KD - 1], ACT.Copy).then_inc(*E.up("m_rounded", l, KD - 1))
                for m in range(KD):
                    ahead("o", l, m)
                squares(l, 1)
                if l % 2 == 0:
                    start_phase(("fg", l), ("fu", l), ("fd", l))
                root(l, 1)
                modulate(l, 1)
                if l % 2 == 0:
                    for m in range(KF + 1):
                        if m < KF:
                            ahead("fg", l, m)
                            act.wait_ge(*filled("fg", l, m))
                            if m >= 3:
                                act.wait_ge(*drained("fu", l, m - 3))
                            a(fsig[m % 3], bank("fg", l, m)[:, 0:T], ACT.Sigmoid).then_inc(*E.up("fsig_ready", l, m))
                            ahead("fu", l, m)
                        if m > 0:
                            act.wait_ge(*drained("fu", l, m - 1))
                            a(h_parts["prod"][0][:, m - 1, :], fprod[(m - 1) % 3], ACT.Copy)\
                                .then_inc(*E.up("prod_rounded", l, m - 1))
                    for n in phase_pieces(("fd", l)):
                        convert(n)
            act.dma_start(wrt, dram["w_router"][0].rearrange("(k p) e -> p k e", p=P)).then_inc(*E.up("router_in", by=16))
            act.dma_start(brt[0:1, :], dram["b_router"]).then_inc(*E.up("router_in", by=16))
            act.wait_ge(*at("chosen_ready"))
            for i in range(2):
                a(rt[:, R_P + 3 * i:R_P + 3 * i + 3], rt[:, R_D:R_D + 3], ACT.Sigmoid, scale=1.0 if i == 0 else -1.0)\
                    .then_inc(*E.up("weights_ready", i))
            for k in range(6):
                act.wait_ge(*filled("htok", k))
                flatk = htok.rearrange("p j d -> p (j d)")[:, k * 512:(k + 1) * 512]
                a(flatk, bank("htok", k)[:, :], ACT.Copy).then_inc(*E.read("htok", k))
            s = lambda name: sem(name).h
            act.wait_ge(*at("jobs_ready"))
            act.sem_inc(s("e_ydrained"), 2)
            njobs = act.value_load(rt_i[0:1, 0:1], min_val=NE, max_val=NJOB)
            with act.Fori(0, njobs) as i:
                def e_round(n0, n1):
                    for n in range(n0, n1):
                        _, _, kn, _, w = E_PIECES[n]
                        act.wait_ge(s("e_used"), i * NPC + n + 1)
                        act.wait_ge(s(f"e_in{n % E_RAW}"), i * (16 * NPC // E_RAW) + 16 * (n // E_RAW + 1))
                        a(e_w[n % E_PARTS][0][:, 0:kn * w], e_raw[n % E_RAW][:, 0:kn * w], ACT.Copy).then_inc(s("e_rounded"), 1)

                def e_turn(c):
                    act.wait_ge(s("e_pT_full"), i * 3 + c + 1)
                    src, dst, _ = e_turned(psum, eprodT, c)
                    a(dst, src, ACT.Copy).then_inc(s("e_pT"), 1)

                e_round(0, E_PARTS)
                act.wait_ge(s("e_selT_full"), i + 1)
                act.wait_ge(s("e_sc"), i * 6 + 6)
                a(selT, psum[4][:, 0:3 * P].rearrange("p (j s) -> p j s", j=3), ACT.Copy).then_inc(s("e_selT"), 1)
                for h in range(2):
                    act.wait_ge(s("e_gather"), i * 2 + h + 1)
                    a(hG[0][:, 4 * h:4 * h + 4, :], psum[6 + h][:, :].rearrange("p (k s) -> p k s", k=4), ACT.Copy)\
                        .then_inc(s("e_hG"), 1)
                done = E_PARTS
                for c, (c0, n) in enumerate(CHUNKS):
                    e_round(done, CHUNK_PIECES * (c + 1) + E_PARTS - 1)
                    done = CHUNK_PIECES * (c + 1) + E_PARTS - 1
                    act.wait_ge(s("e_used"), i * NPC + E_PARTS + CHUNK_PIECES * (c + 1))
                    act.wait_ge(s("e_prod"), i * 3 + 3 + c)
                    a(esig[:, 0:n], psum[2 * (c % 2)][:, 0:n], ACT.Sigmoid).then_inc(s("e_sig"), 1)
                    if c > 0:
                        e_turn(c - 1)
                e_round(done, done + 4)
                e_turn(2)
                e_round(done + 4, NPC)
                act.wait_ge(s("e_used"), i * NPC + E_PARTS + NPC)
                for half in range(2):
                    a(ey[:, half * 512:(half + 1) * 512], psum[4 + half][:, :], ACT.Copy).then_inc(s("e_ydrained"), 1)
            squares(DEPTH, 0)
            root(DEPTH, 0)
            for j in range(3):
                for half in range(2):
                    act.wait_ge(*filled("yo", j, half))
                    a(htok[:, j, half * 512:(half + 1) * 512], bank("yo", j, half)[:, :], ACT.Copy)\
                        .then_inc(*E.read("yo", j, half))
                act.wait_ge(*E.latest())
                dst = yp[0] if j == 0 else ys[0][(j - 1) * P:j * P, :]
                act.dma_start(dst, htok[:, j, :]).then_inc(*E.up("out_stored", "y", j, by=16))

        @block.vector
        def _(dve):
            E = Counts("dve_step")
            tt, ts, stt = dve.tensor_tensor, dve.tensor_scalar, dve.scalar_tensor_tensor
            M, A, SUB = ALU.mult, ALU.add, ALU.subtract

            dve.memset(condp, 0.0).then_inc(*E.step())
            dve.wait_ge(*E.latest())
            for i in range(2):
                dve.wait_ge(*at("cond_sig", i))
            tt(condp[:, :, 0:2], cond, condx, M).then_inc(*E.up("cond_ready"))

            def normed(l, which, scale=None):
                dve.wait_ge(*drained("norm", l, which))
                dve.reciprocal(rs, rs).then_inc(*E.step())
                dve.wait_ge(*E.latest())
                dst = hT if scale is None else sq
                if scale is None:
                    for i in range(2):
                        tt(hT[:, 4 * i:4 * i + 4, :], xT[:, 4 * i:4 * i + 4, :],
                                 rs.rearrange("p (a t) -> p a t", a=1).broadcast_to([P, 4, T]), M)\
                                     .then_inc(*E.up("xn_ready", l, which, i))
                        dve.wait_ge(*E.latest())
                        for g in (2 * i, 2 * i + 1):
                            k = 2 * g + 1
                            for s_, (t0, t1) in enumerate(SEG):
                                ins = ts(hT[:, k, t0:t1], hT[:, k, t0:t1], modAs[:, l, which, k, s_:s_ + 1],
                                         mods[:, l, 24 * which + k, s_:s_ + 1], M, A)
                            ins.then_inc(*E.up("h_odd", l, which, g))
                else:
                    for k in range(KD):
                        ins = stt(sq[:, k, :], xT[:, k, :], scale(k), rs, M, M)
                        if k < KD - 1:
                            ins.then_inc(*E.step())
                        else:
                            ins.then_inc(*E.up("h_ready", l))

            def residual(job, l, gate, which):
                for m in range(KD):
                    src = bank(*job(m)) if job(m)[0] != "fdown" else psum[m]
                    if job(m)[0] == "fdown":
                        dve.wait_ge(*at("piece_used", "fd", l, KF - 1, m // 4))
                    else:
                        dve.wait_ge(*filled(*job(m)))
                    for s_, (t0, t1) in enumerate(SEG):
                        ins = stt(xT[:, m, t0:t1], src[:, t0:t1], mods[:, l, gate + m, s_:s_ + 1], xT[:, m, t0:t1], M, A)
                        if s_ == 0:
                            ins.then_inc(*E.step())
                    if job(m)[0] == "fdown":
                        if m < 4:
                            ins.then_inc(sem(f"bank_free{m}").h, 1)
                        else:
                            ins.then_inc(*E.up("fdown_done", l))
                    else:
                        ins.then_inc(*E.read(*job(m)))

            def rest(phase, l, g, src):
                dve.wait_ge(*at("x_rounded", phase, l, g))
                xr, xl = (p[:, 2 * g:2 * g + 2, :] for p in h_parts[phase])
                tt(xl, src, xr.bitcast(F32), SUB).then_inc(*E.up("x_parts", phase, l, g))

            def rest_merged(l, m):
                dve.wait_ge(*at("m_rounded", l, m))
                xr, xl = (p[:, m, :] for p in h_parts["merged"])
                ins = tt(xl, merged[m], xr.bitcast(F32), SUB)
                ins.then_inc(*(E.up("x_parts", "merged", l, m // 2) if m % 2 else E.step()))

            def rest_prod(l, m):
                dve.wait_ge(*at("prod_rounded", l, m))
                xr, xl = (p[:, m, :] for p in h_parts["prod"])
                tt(xl, fprod[m % 3], xr.bitcast(F32), SUB).then_inc(*E.up("prod_rest", l, m))

            def modulation(l):
                ba = v("b_ada", l, 0, 48)
                for g in range(3):
                    dve.wait_ge(*filled("adaT", l, g))
                    tb = bank("adaT", l, g)[:, :].rearrange("p (m r) -> p m r", r=32)
                    for s_ in range(2):
                        ins = tt(mods[:, l, 16 * g:16 * g + 16, s_], tb[:, :, s_], ba[:, 16 * g:16 * g + 16], A)
                        if s_ == 0:
                            ins.then_inc(*E.step())
                    ins.then_inc(*E.read("adaT", l, g))
                dve.wait_ge(*E.latest())
                for which, name in ((0, "norm1"), (1, "norm2")):
                    for s_ in range(2):
                        stt(modAs[:, l, which, :, s_], mods[:, l, 24 * which + 8:24 * which + 16, s_], 1.0,
                            v(name, l, 0, 8), A, M).then_inc(*E.up("modA_ready", l))

            for l in range(DEPTH):
                if l == 0:
                    modulation(0)
                dve.wait_ge(*E.latest())
                mu = v("shift_mu", l, 0, NZ)
                ts(mix[:, 0, 0:NZ], mu, -1.0, 1.0, M, A).then_inc(*E.step())
                ts(mix[:, 1, 0:NZ], mu, 0.5, None, M).then_inc(*E.step())
                ts(oneka, v("k_a", l, 0, 4), -1.0, 1.0, M, A).then_inc(*E.step())
                normed(l, 0)
                for g in range(4):
                    rest("z", l, g, hT[:, 2 * g:2 * g + 2, :])
                for g in range(3):
                    full_z = 5 * g + 4
                    dve.wait_ge(*drained('z', l, full_z))
                    for m in range(5 * g, 5 * g + 4):
                        dve.wait_ge(*drained('z', l, m))
                    gs = slice(5 * g, 5 * g + 5)
                    zz, sh = z[:, gs, :], shifted[:, gs, :]
                    tt(sh[:, :, 1:T - 1], zz[:, :, 0:T - 2], zz[:, :, 2:T], A).then_inc(*E.step())
                    dve.wait_ge(*E.latest())
                    dve.tensor_copy(sh[:, :, TP - 1:TP + 1], zz[:, :, TP - 2:TP + 2:3]).then_inc(*E.step())
                    dve.tensor_copy(sh[:, :, 0:T:T - 1], zz[:, :, 1:T - 1:T - 3]).then_inc(*E.step())
                    dve.wait_ge(*E.latest())
                    for m in range(5 * g, 5 * g + 5):
                        ts(z[:, m, :], z[:, m, :], mix[:, 0, m:m + 1], None, M).then_inc(*E.step())
                    dve.wait_ge(*E.latest())
                    for m in range(5 * g, 5 * g + 5):
                        ins = stt(z[:, m, :], shifted[:, m, :], mix[:, 1, m:m + 1], z[:, m, :], M, A)
                        ins.then_inc(*E.up("mix_done", l)) if m == NZ - 1 else ins.then_inc(*E.step())
                dve.wait_ge(*E.latest())
                r_, k_, v_ = z[:, 0:4, :], z[:, 4:8, :], z[:, 8:12, :]
                for m in range(NM):
                    ins = ts(kk[:, m, :], z[:, 4 + m, :], v("k_k", l, m), None, M)
                    ins.then_inc(*E.up("kkp_ready", l)) if m == 3 else ins.then_inc(*E.step())
                dve.wait_ge(*E.latest())
                dve.wait_ge(*at("second_in"))
                for m in range(4):
                    dve.wait_ge(*drained("cf", l, m))
                dve.memset(glu, 0.0).then_inc(*E.step())
                dve.wait_ge(*E.latest())
                for m in range(2):
                    tt(glu[:, m, 15:15 + TP], cvT[:, m, 0:TP], conv_b[:, m, 0:TP], M).then_inc(*E.step())
                    tt(glu[:, m, TP + 30:].rearrange("p (r t) -> p r t", r=4)[:, :, 15:15 + GRID],
                             cvT[:, m, TP:T].rearrange("p (r t) -> p r t", r=4),
                             conv_b[:, m, TP:T].rearrange("p (r t) -> p r t", r=4), M).then_inc(*E.up("glu_ready", l))
                for m in range(NM):
                    dve.wait_ge(*drained('kks', l, m))
                nrm = ksq
                ts(nrm, nrm, 1e-12, None, ALU.max).then_inc(*E.step())
                dve.wait_ge(*E.latest())
                dve.reciprocal(nrm, nrm).then_inc(*E.step())
                dve.wait_ge(*E.latest())
                tt(kk, kk, nrm, M).then_inc(*E.up("kk_ready", l))
                def prep(d):
                    sg, ag, F3 = tmp4[0], tmp4[1], tmp4[3]
                    for m in range(NM):
                        dve.wait_ge(*drained('low', l, d, 0, m))
                    for m in range(NM):
                        o_ = slice(m * T, (m + 1) * T)
                        dve.tensor_tensor_scan(tmp4[2][:, o_], tab("reset"), sg[:, o_], 0.0, M, A).then_inc(*E.step())
                    dve.wait_ge(*E.latest())
                    cs = tmp4[2]
                    if d == 1:
                        tt(F3, sg, cs, SUB).then_inc(*E.step())
                        dve.wait_ge(*E.latest())
                        tot = cs.rearrange("p (m c t) -> p m c t", m=NM, c=NC_)
                        for m in range(NM):
                            tt(F3.rearrange("p (m c t) -> p m c t", m=NM, c=NC_)[:, m],
                                      F3.rearrange("p (m c t) -> p m c t", m=NM, c=NC_)[:, m],
                                      tot[:, m, :, C - 1:C].broadcast_to([P, NC_, C]), A).then_inc(*E.step())
                        dve.wait_ge(*E.latest())
                    L = tmp4[L3(d)]
                    tt(sg, L, sg, SUB).then_inc(*E.up("L_ready", l, d))
                    ar = AR.rearrange("p m c k t -> p k m c t")
                    v4 = lambda x: x.rearrange("p (m c t) -> p m c t", m=NM, c=NC_)
                    v3 = lambda x: x.rearrange("p (m t) -> p m t", m=NM)
                    kk4 = kk.rearrange("p m (c t) -> p m c t", c=NC_)
                    for m in range(NM):
                        dve.wait_ge(*drained('low', l, d, 1, m))
                    tt(BK[:, 0], kk, v3(ag), M).then_inc(*E.step())
                    for m in range(NM):
                        ts(BK[:, 1, m, :], v3(ag)[:, m, :], v("k_a", l, m), oneka[:, m:m + 1], M, A).then_inc(*E.step())
                    dve.wait_ge(*E.latest())
                    tt(BK[:, 1], BK[:, 1], k_, M).then_inc(*E.step())
                    dve.wait_ge(*at("E1_ready", l, d))
                    for m in range(NM):
                        stt(ar[:, 0, m], kk4[:, m], -1.0, v4(sg)[:, m], M, M).then_inc(*E.step())
                    dve.wait_ge(*at("E2_ready", l, d))
                    for m in range(NM):
                        tt(ar[:, 1, m], r_[:, m, :].rearrange("p (c t) -> p c t", c=NC_), v4(tmp4[other(d)])[:, m], M)\
                            .then_inc(*E.step())
                    dve.wait_ge(*at("E3_ready", l, d))
                    dve.wait_ge(*E.latest())
                    tt(BK[:, 0], BK[:, 0], v3(L), M).then_inc(*E.step())
                    tt(BK[:, 1], BK[:, 1], v3(L), M).then_inc(*E.up("ark_ready", l, d))

                dve.wait_ge(*filled("cf", l, 5))
                prep(0)
                for j in range(NCP):
                    dve.wait_ge(*filled("fno1", l, j))
                    dve.tensor_copy(fno_z[:, j, :, :], bank("fno1", l, j)[:, :].rearrange("p (m w) -> p m w", m=2))\
                        .then_inc(*E.read("fno1", l, j))

                dve.wait_ge(*filled("cln", l, 0))
                for m in range(2):
                    ins = stt(cvT[:, m, :], bank("cln", l, 0)[:, 0:T], -1.0 / CC, cvT[:, m, :], M, A)
                    if m == 0:
                        ins.then_inc(*E.step())
                    else:
                        ins.then_inc(*E.read("cln", l, 0))
                dve.wait_ge(*drained('cln', l, 1))
                dve.reciprocal(conv_b[:, 0, :], conv_b[:, 0, :]).then_inc(*E.step())
                dve.wait_ge(*E.latest())
                for m in range(2):
                    tt(cvT[:, m, :], cvT[:, m, :], conv_b[:, 0, :], M).then_inc(*E.step())
                dve.wait_ge(*E.latest())
                for m in range(2):
                    ts(cvT[:, m, :], cvT[:, m, :], v("conv_ln_g", l, m), v("conv_ln_b", l, m), M, A)\
                        .then_inc(*E.up("conv_affine", l))
                dve.wait_ge(*at("conv_sig", l))
                tt(cvT, cvT, conv_b, M).then_inc(*E.up("cv_ready", l))

                for d in range(2):
                    if d == 1:
                        dve.wait_ge(*filled("Y", l, 0, NCP - 1))
                        prep(1)
                    for cp in range(NCP):
                        for hp in range(NH // 2):
                            dve.wait_ge(*filled("pair", l, d, cp, hp))
                            src = bank("pair", l, d, cp, hp)[:, :].rearrange("p (h w) -> p h w", h=2)
                            msk = pair_mask[:, d:d + 1, :].broadcast_to([P, 2, 256])
                            h0 = 4 * (hp // 2) + hp % 2
                            tt(S1[:, cp, h0:h0 + 3:2, :], src, msk, M).then_inc(*E.read("pair", l, d, cp, hp))
                    for u in range(NCP):
                        dve.tensor_copy(TQ[:, u, :, :], tab("eye2").rearrange("p (a w) -> p a w", a=1).broadcast_to([P, NH, C]))\
                            .then_inc(*E.up("TQ_ready", l, d, u))
                    for lev in range(LEVELS):
                        msk = level_mask[:, lev:lev + 1, B * d:B * d + C].bitcast(I32).broadcast_to([P, NH, C])
                        for u in range(NCP):
                            dve.wait_ge(*filled("TAT", l, d, lev, u))
                            src = bank("TAT", l, d, lev, u)[:, :].rearrange("p (h w) -> p h w", h=NH)
                            dve.copy_predicated(TQ[:, u, :, :], msk, src).then_inc(*E.read("TAT", l, d, lev, u))
                    dve.wait_ge(*at("Q_zero", l, d))
                    for u in range(NCP):
                        dve.wait_ge(*filled("QO", l, d, u))
                        for par in range(2):
                            q = slice(64 * par + 32 * d, 64 * par + 32 * d + 32)
                            ins = dve.tensor_copy(Q[q, u, :, (1 - d) * B:(2 - d) * B],
                                                  bank("QO", l, d, u)[q, 0:256].rearrange("p (h w) -> p h w", h=NH))
                        ins.then_inc(*E.read("QO", l, d, u))
                    c0 = starts(d)[0]
                    dve.wait_ge(*at("St_zero", l))
                    dve.memset(St[:, c0, :, :], 0.0).then_inc(*E.up("S_ready", l, d, c0))
                    for step in steps(d):
                        for _, c in step:
                            cp, par = divmod(c, 2)
                            q = slice(64 * par, 64 * par + 64)
                            dve.wait_ge(*filled("U", l, d, c))
                            dve.tensor_copy(U[q, cp, :, :], bank("U", l, d, c)[q, :].rearrange("p (h v) -> p h v", h=NH))\
                                .then_inc(*E.read("U", l, d, c))
                        for _, c in step:
                            n = nxt(d, c)
                            if n is None:
                                continue
                            dve.wait_ge(*filled("S", l, d, c))
                            dst = lambda r: Sfin[r, :, :] if n == "end" else St[r, n, :, r]
                            if n == "end" and (l, d) != (0, 0):
                                dve.wait_ge(*filled("sf", *((l, 0) if d else (l - 1, 1))))
                            for r in (slice(0, 64), slice(64, P)):
                                ins = tt(dst(r), bank("S", l, d, c)[r, 0:256].rearrange("p (m v) -> p m v", m=NM),
                                         St[r, c, :, r], A)
                            ins.then_inc(*E.read("S", l, d, c))
                            dve.wait_ge(*E.latest())
                            for r in (slice(0, 64), slice(64, P)):
                                ins = tt(dst(r), dst(r), pc[r, :, c:c + 1].broadcast_to([64, NM, HD]), M)
                            if n == "end":
                                ins.then_inc(*E.up("Sfin_ready", l, d))
                            else:
                                ins.then_inc(*E.up("S_ready", l, d, n))
                    if d == 1:
                        for cp in range(NCP):
                            dve.wait_ge(*filled("Y", l, d, cp))
                            if cp == 0:
                                for i in range(NCP):
                                    dve.wait_ge(*drained('Y', l, 0, i))
                            tt(Y[:, cp, :], Y[:, cp, :], bank("Y", l, d, cp)[:, :], A).then_inc(*E.read("Y", l, d, cp))
                        dve.wait_ge(*E.latest())
                for g in range(4):
                    rest("gate", l, g, hT[:, 2 * g:2 * g + 2, :])
                Yh = Y.rearrange("p c (h v) -> p (c h) v", v=HD)

                def gated(b_, m):
                    dve.wait_ge(*filled("br", l, b_, m))
                    dve.wait_ge(*drained('gate', l, b_, m))
                    g = gsig(b_ * KD + m)
                    dst = merged[m] if b_ == 0 else g
                    tt(dst, g, bank("br", l, b_, m)[:, 0:T], M).then_inc(*E.read("br", l, b_, m))
                    if b_ > 0:
                        dve.wait_ge(*E.latest())
                        tt(merged[m], merged[m], g, A).then_inc(*E.up("gated", l, b_, m))

                dve.tensor_reduce(stat[:, 0:24], Yh, AX.X, A).then_inc(*E.step())
                dve.wait_ge(*E.latest())
                ts(stat[:, 0:24], stat[:, 0:24], 1.0 / HD, None, M).then_inc(*E.step())
                dve.wait_ge(*E.latest())
                tt(Yh, Yh, stat[:, 0:24].rearrange("p (a b) -> p a b", b=1).broadcast_to([P, 24, HD]), SUB)\
                    .then_inc(*E.up("Y_centred", l))
                for m in range(3):
                    gated(0, m)
                dve.wait_ge(*at("Ysq_ready", l))
                dve.tensor_reduce(stat[:, 0:24], tmp4[2].rearrange("p (n v) -> p n v", v=HD), AX.X, A)\
                    .then_inc(*E.up("Yvar_ready", l))
                for m in range(3, 6):
                    gated(0, m)
                dve.wait_ge(*at("Ystd_ready", l))
                dve.reciprocal(stat[:, 24:48], stat[:, 24:48]).then_inc(*E.step())
                dve.wait_ge(*E.latest())
                tt(Yh, Yh, stat[:, 24:48].rearrange("p (a b) -> p a b", b=1).broadcast_to([P, 24, HD]), M)\
                    .then_inc(*E.up("yn_ready", l))
                for m in range(6, KD):
                    gated(0, m)
                for m in range(NM):
                    o_ = tmp4[1][:, m * T:(m + 1) * T]
                    ins = stt(o_, z[:, m, :], v("r_k", l, m), z[:, 4 + m, :], M, M)
                    ins.then_inc(*E.up("rk_ready", l)) if m == 3 else ins.then_inc(*E.step())
                for m in range(KD):
                    gated(1, m)
                for cp in range(NCP):
                    dve.wait_ge(*filled("yt", l, cp))
                    for m in range(NM):
                        ins = ts(yT[:, m, cp * P:(cp + 1) * P], bank("yt", l, cp)[:, m * P:(m + 1) * P],
                                 v("gn_g", l, m), v("gn_b", l, m), M, A)
                        if m < 3:
                            ins.then_inc(*E.step())
                    ins.then_inc(*E.read("yt", l, cp))
                for m in range(NM):
                    dve.wait_ge(*filled("bon", l, m))
                    tt(tmp4[2][:, m * T:(m + 1) * T], bank("bon", l, m)[:, 0:T], z[:, 8 + m, :], M).then_inc(*E.read("bon", l, m))
                dve.wait_ge(*E.latest())
                tt(yT, yT, tmp4[2].rearrange("p (m t) -> p m t", m=NM), A).then_inc(*E.step())
                dve.wait_ge(*E.latest())
                for m in range(NM):
                    dve.wait_ge(*filled("gup", l, m))
                    tt(yT[:, m, :], yT[:, m, :], bank("gup", l, m)[:, 0:T], M).then_inc(*E.read("gup", l, m))
                for m in range(KD):
                    gated(2, m)
                    if m > 0:
                        rest_merged(l, m - 1)
                rest_merged(l, KD - 1)
                if l + 1 < DEPTH:
                    modulation(l + 1)
                residual(lambda m: ("o", l, m), l, 16, 1)
                normed(l, 1)
                if l % 2 == 0:
                    for g in range(4):
                        rest("ffn", l, g, hT[:, 2 * g:2 * g + 2, :])
                    for m in range(KF):
                        dve.wait_ge(*at("fsig_ready", l, m))
                        dve.wait_ge(*filled("fg", l, m))
                        tt(fsig[m % 3], fsig[m % 3], bank("fg", l, m)[:, 0:T], M).then_inc(*E.read("fg", l, m))
                        dve.wait_ge(*E.latest())
                        dve.wait_ge(*filled("fu", l, m))
                        if m >= 3:
                            dve.wait_ge(*at("prod_rest", l, m - 3))
                        tt(fprod[m % 3], fsig[m % 3], bank("fu", l, m)[:, 0:T], M).then_inc(*E.read("fu", l, m))
                        if m > 0:
                            rest_prod(l, m - 1)
                    rest_prod(l, KF - 1)
                    residual(lambda m: ("fdown", l, m), l, 40, 2)
            dve.wait_ge(*filled("logit"))
            lg = rt[:, R_LG:R_LG + 24]
            dve.tensor_copy(lg, bank("logit")[:, 0:24]).then_inc(*E.read("logit"))
            dve.wait_ge(*E.latest())
            for j in range(3):
                dve.max(rt[:, R_MX + 8 * j:R_MX + 8 * j + 8], lg[:, 8 * j:8 * j + 8]).then_inc(*E.step())
            dve.wait_ge(*E.latest())
            for j in range(3):
                dve.max_index(rt[:, R_IX + 8 * j:R_IX + 8 * j + 8].bitcast(U32), rt[:, R_MX + 8 * j:R_MX + 8 * j + 8],
                                     lg[:, 8 * j:8 * j + 8]).then_inc(*E.step())
            mx = rt[:, R_MX:R_MX + 24].rearrange("p (j e) -> p j e", j=3)
            tt(rt[:, R_D:R_D + 3], mx[:, :, 0], mx[:, :, 1], SUB).then_inc(*E.step())
            dve.wait_ge(*E.latest())
            dve.tensor_copy(rt[:, R_IF:R_IF + 24], rt[:, R_IX:R_IX + 24].bitcast(U32)).then_inc(*E.step())
            dve.wait_ge(*E.latest())
            code8 = tab("code")[:, 0:NE]
            for j in range(3):
                for i in range(2):
                    ts(rt[:, R_OH + 24 * i + 8 * j:R_OH + 24 * i + 8 * j + 8], code8,
                              rt[:, R_IF + 8 * j + i:R_IF + 8 * j + i + 1], None, ALU.is_equal).then_inc(*E.step())
            dve.wait_ge(*E.latest())
            tt(rt[:, 0:24], rt[:, R_OH:R_OH + 24], rt[:, R_OH + 24:R_OH + 48], A).then_inc(*E.up("chosen_ready"))
            for i in range(2):
                dve.wait_ge(*at("weights_ready", i))
            for j in range(3):
                o_ = rt[:, R_OH + 8 * j:R_OH + 8 * j + 8]
                ts(o_, o_, rt[:, R_P + j:R_P + j + 1], None, M).then_inc(*E.step())
            dve.wait_ge(*E.latest())
            for j in range(3):
                for t in range(3):
                    stt(rt[:, R_CW + 24 * j + 8 * t:R_CW + 24 * j + 8 * t + 8],
                               rt[:, R_OH + 24 + 8 * j:R_OH + 24 + 8 * j + 8], rt[:, R_P + 3 + j:R_P + 4 + j],
                               rt[:, R_OH + 8 * j:R_OH + 8 * j + 8], M, A).then_inc(*E.step())
            dve.wait_ge(*filled("rank"))
            rk = rt[:, R_RK:R_RK + 24]
            stt(rk, bank("rank")[:, 0:24], 1.0, rt[:, 0:24], A, M).then_inc(*E.step())
            cnt = rt[:, R_CNT:R_CNT + 8]
            dve.tensor_copy(cnt, bank("rank")[:, 24:32]).then_inc(*E.read("rank"))
            dve.wait_ge(*E.latest())
            for j in range(3):
                for t in range(3):
                    ts(rt[:, R_SL + 24 * j + 8 * t:R_SL + 24 * j + 8 * t + 8], rk[:, 8 * j:8 * j + 8],
                              -1.0 - P * t, None, A).then_inc(*E.step())
            fl = rt[:, R_FL:R_FL + 16]
            for t in range(2):
                ts(fl[:, 8 * t:8 * t + 8], cnt, float(P * (t + 1)), None, ALU.is_gt).then_inc(*E.step())
            dve.wait_ge(*E.latest())
            dve.tensor_tensor_scan(rt[:, R_PS:R_PS + 16], ones[:, 0:16], fl, 0.0, M, A).then_inc(*E.step())
            dve.wait_ge(*E.latest())
            tt(rt[:, R_PS:R_PS + 16], rt[:, R_PS:R_PS + 16], fl, M).then_inc(*E.step())
            jl = rt[:, R_JL:R_JL + 17]
            dve.wait_ge(*E.latest())
            dve.tensor_reduce(jl[:, 0:1], rt[:, R_PS:R_PS + 16], AX.X, ALU.max).then_inc(*E.step())
            dve.wait_ge(*E.latest())
            ts(jl[:, 0:1], jl[:, 0:1], float(NE), None, A).then_inc(*E.step())
            dve.tensor_copy(jl[:, 1:9], code8).then_inc(*E.step())
            for q in range(8):
                o_ = rt[:, R_TM + 16 * q:R_TM + 16 * q + 16]
                stt(o_, rt[:, R_PS:R_PS + 16], float(q + 1), tab("code")[:, 8:24], ALU.is_equal, M).then_inc(*E.step())
            dve.wait_ge(*E.latest())
            dve.tensor_reduce(jl[:, 9:17], rt[:, R_TM:R_TM + 128].rearrange("p (q i) -> p q i", q=8), AX.X, A).then_inc(*E.step())
            dve.wait_ge(*E.latest())
            t1 = rt[:, R_TM:R_TM + 17]
            ts(t1, jl, float(NE), -float(NE), ALU.is_ge, M).then_inc(*E.step())
            ts(rt[:, R_TM + 32:R_TM + 49], jl, float(2 * NE), -float(NE), ALU.is_ge, M).then_inc(*E.step())
            dve.wait_ge(*E.latest())
            tt(t1, t1, rt[:, R_TM + 32:R_TM + 49], A).then_inc(*E.step())
            dve.wait_ge(*E.latest())
            tt(t1, t1, jl, A).then_inc(*E.step())
            dve.wait_ge(*E.latest())
            dve.tensor_copy(rt_i[:, 1:17], t1[:, 1:17]).then_inc(*E.step())
            dve.tensor_copy(rt_i[:, 0:1], jl[:, 0:1]).then_inc(*E.step())
            dve.tensor_copy(rt_i[:, 17:34], jl).then_inc(*E.up("jobs_ready"))
            for k in range(6):
                dve.wait_ge(*drained('htok', k))
            s = lambda name: sem(name).h
            dve.memset(yacc, 0.0).then_inc(*E.step())
            dve.wait_ge(*E.latest())
            dve.sem_inc(s("e_prod"), 3)
            dve.sem_inc(s("e_sc_done"), 6)
            dve.sem_inc(s("e_hG_rest"), 2)
            njobs = dve.value_load(rt_i[0:1, 0:1], min_val=NE, max_val=NJOB)

            def select(code):
                for j in range(3):
                    slot = rt[:, bass.ds(code + (R_SL + 24 * j), 1)]
                    w = rt[:, bass.ds(code + (R_CW + 24 * j), 1)]
                    ts(sel[:, j, :], iota, slot, None, ALU.is_equal)
                    ins = ts(selc[:, j, :], iota, slot, w, ALU.is_equal, M)
                return ins

            select(dve.value_load(rt_i[0:1, 18:19], min_val=0, max_val=NCODE - 1)).then_inc(s("e_sel"), 1)
            with dve.Fori(0, njobs) as i:
                def e_rests(n0, n1):
                    for n in range(n0, n1):
                        if e_rester(n)[0] == "e_rest_dve":
                            e_rest(dve, s, e_raw, e_w, i, n)

                def e_turn_rest(c):
                    dve.wait_ge(s("e_pT"), i * 3 + c + 1)
                    src, rounded_, dst = e_turned(psum, eprodT, c)
                    tt(dst, src, rounded_.bitcast(F32), SUB).then_inc(s("e_pT_rest"), 1)

                e_rests(0, E_PARTS)
                for h in range(2):
                    dve.wait_ge(s("e_hG"), i * 2 + h + 1)
                    xr, xl = (p[:, 4 * h:4 * h + 4, :] for p in hG)
                    tt(xl, psum[6 + h][:, :].rearrange("p (k s) -> p k s", k=4), xr.bitcast(F32), SUB).then_inc(s("e_hG_rest"), 1)
                done = E_PARTS
                for c, (c0, n) in enumerate(CHUNKS):
                    e_rests(done, CHUNK_PIECES * (c + 1) + E_PARTS - 1)
                    done = CHUNK_PIECES * (c + 1) + E_PARTS - 1
                    dve.wait_ge(s("e_sig"), i * 3 + c + 1)
                    if c == 0:
                        dve.wait_ge(s("e_sc"), i * 6 + 6)
                    tt(esig[:, 0:n], esig[:, 0:n], psum[2 * (c % 2)][:, 0:n], M).then_inc(s("e_silu"), 1)
                    dve.wait_ge(s("e_silu"), i * 3 + c + 1)
                    tt(eprod[:, c0:c0 + n], esig[:, 0:n], psum[2 * (c % 2) + 1][:, 0:n], M).then_inc(s("e_prod"), 1)
                    if c > 0:
                        e_turn_rest(c - 1)
                e_rests(done, done + 4)
                e_turn_rest(2)
                e_rests(done + 4, NPC)
                select(dve.value_load(rt_i[0:1, bass.ds(i + 19, 1)], min_val=0, max_val=NCODE - 1)).then_inc(s("e_sel"), 1)
                for n_ in range(6):
                    j, half = divmod(n_, 2)
                    dve.wait_ge(s("e_sc"), i * 6 + 6 + n_ + 1)
                    if n_ == 0:
                        dve.wait_ge(s("e_sc_done"), i * 6 + 6)
                    dst = yacc[:, j, half * 512:(half + 1) * 512]
                    tt(dst, dst, psum[6 + half][:, :], A).then_inc(s("e_sc_done"), 1)
            dve.tensor_copy(stat[:, 84:85], ident[:, 0:1]).then_inc(*E.up("yacc_ready"))
            residual(lambda m: ("ey", m), 1, 40, 2)
            normed(DEPTH, 0, lambda k: v("final_norm", 0, k))

        @block.gpsimd
        def _(pool):
            E = Counts("pool_step")

            def rests(*kinds):
                for n in phase_pieces(*kinds):
                    key, _, raw, _ = pieces[n]
                    pool.wait_ge(*at("rounded_ready", *key))
                    wr, wl = w_parts[n % NSLOT]
                    pool.tensor_tensor(wl, raw, wr.bitcast(F32), ALU.subtract).then_inc(*E.up("rest_ready", *key))

            for l in range(DEPTH):
                rests(("z", l), ("cf", l))
                pool.wait_ge(*filled("cf", l, 5))
                pool.memset(St, 0.0).then_inc(*E.up("St_zero", l))
                if l == 0:
                    pool.wait_ge(*drained("vec", DEPTH - 1))
                pool.wait_ge(*at("mix_done", l))
                for i in range(2 * CONV_W):
                    m, j = divmod(i, CONV_W)
                    if i >= 8 and (i - 8) % CONV_W == CONV_W - 1:
                        pool.wait_ge(*filled("conv_s", l, (i - 8) // CONV_W))
                    elif i >= 8:
                        pool.wait_ge(*at("diag_used", l, i - 8))
                    pool.tensor_scalar(diag[i % 8], ident, v("dw_w", l, 2 * j + m), None, ALU.mult)\
                        .then_inc(*E.up("diag_ready", l, i))
                for d in range(2):
                    pool.wait_ge(*filled("pair", l, d, NCP - 1, NH // 2 - 1))
                    pool.memset(Q, 0.0).then_inc(*E.up("Q_zero", l, d))
                    pool.wait_ge(*E.latest())
                    for u in range(NCP):
                        pool.wait_ge(*drained("TAT", l, d, LEVELS - 1, u))
                    for g in range(4):
                        q = slice(32 * g, 32 * g + 32)
                        c0 = (g % 2) * B
                        pool.tensor_copy(Q[q, :, :, c0:c0 + B], TQ[q, :, :, B:C]).then_inc(*E.up("Qdiag_ready", l, d))
                rests(("gate", l), ("o", l))
                if l % 2 == 0:
                    rests(("fg", l), ("fu", l), ("fd", l))
            s = lambda name: sem(name).h
            pool.wait_ge(*at("jobs_ready"))
            njobs = pool.value_load(rt_i[0:1, 0:1], min_val=NE, max_val=NJOB)
            with pool.Fori(0, njobs) as i:
                for n in range(NPC):
                    if e_rester(n)[0] == "e_rest_pool":
                        e_rest(pool, s, e_raw, e_w, i, n)


_INS = ["x_prompt", "x_sample", "state_rwkv", "c", "c_ctx", "norm1", "norm2", "w_ada", "b_ada", "w_in",
        "dw_w", "dw_b", "conv_ln_g", "conv_ln_b", "w_conv_out", "w_fno_out", "shift_mu", "g_up",
        "dec_w0", "dec_up", "iclr_a0", "iclr_up", "k_k", "k_a", "r_k", "gn_g", "gn_b", "w_rwkv_out", "w_o",
        "ffn_w_gate", "ffn_w_up", "ffn_w_down", "w_router", "b_router",
        "moe_w_gate", "moe_w_up", "moe_w_down", "final_norm"]
_OUTS = [(1, TP, DM), (1, TS, DM), (1, DEPTH, 2, NH, HD, HD)]


def kernel(**inputs):
    import concourse.bacc as bacc
    from concourse.bass_utils import run_bass_kernel_spmd as run

    arrays = {n: np.ascontiguousarray(inputs[n]) for n in _INS}
    arrays["tables"] = np.concatenate(list(tables().values()), 1)
    marks = {}
    for _ in range(2):
        nc = bacc.Bacc("TRN2", target_bir_lowering=False, num_devices=1)
        dram = {n: nc.dram_tensor(f"in_{n}", a.shape, F32, kind="ExternalInput").ap() for n, a in arrays.items()}
        outs = [nc.dram_tensor(f"out_{i}", s, F32, kind="ExternalOutput").ap() for i, s in enumerate(_OUTS)]
        build(nc, dram, outs, marks)
    r = run(nc, [{f"in_{n}": a for n, a in arrays.items()}], core_ids=[0])
    return tuple(r.results[0][f"out_{i}"] for i in range(len(_OUTS)))
```
